# Optimizing a Trainium2 kernel written in Bass

```python
import math
import jax, jax.numpy as jnp
from jax import lax
import numpy as np

D_MODEL = 1024
BATCH = 1
SEQ = 256
DEPTH = 4

N_MIXERS = 3
BLOCK = 128
N_BUCKETS = 32
MAX_DISTANCE = 128
N_BIAS_CH = 16
DA_HEADS = 8
DA_QK_DIM = 64
DA_V_DIM = 2 * DA_QK_DIM
SB_HEADS = 16
SB_DIM = D_MODEL // SB_HEADS
SW_Q_HEADS = 16
SW_KV_HEADS = 4
SW_DIM = 64
SW_WINDOW = 128
D_FF = 2752
CONV_W = 3
EPS = 1e-6
NEG = -1e30
N_A = (DEPTH + 2) // 3
N_B = (DEPTH + 1) // 3
N_C = DEPTH // 3


def rmsnorm(x, g):
    xf = x.astype(jnp.float32)
    y = xf * lax.rsqrt(jnp.mean(xf * xf, axis=-1, keepdims=True) + EPS)
    return (y * g.astype(jnp.float32)).astype(x.dtype)

def t5_bucket(dist):
    max_exact = N_BUCKETS // 2
    d = jnp.maximum(dist, 0)
    large = max_exact + (jnp.log(jnp.maximum(d, 1).astype(jnp.float32) / max_exact)
                         / math.log(MAX_DISTANCE / max_exact) * (N_BUCKETS - max_exact)).astype(jnp.int32)
    large = jnp.minimum(large, N_BUCKETS - 1)
    return jnp.where(d < max_exact, d, large)

def lambda_init_fn(layer):
    return 0.8 - 0.6 * math.exp(-0.3 * layer)

def diff_attention(h, w_qkv, lam, subln, rel_bias, lambda_init):
    B, S, _ = h.shape
    nb = S // BLOCK
    qk_w = DA_HEADS * 2 * DA_QK_DIM
    qkv = h @ w_qkv
    q, k, v = jnp.split(qkv, [qk_w, 2 * qk_w], axis=-1)
    q = q.reshape(B, S, DA_HEADS, 2, DA_QK_DIM)
    k = k.reshape(B, S, DA_HEADS, 2, DA_QK_DIM)
    v = v.reshape(B, S, DA_HEADS, DA_V_DIM)
    lf = lam.astype(jnp.float32)
    lam_full = jnp.exp(jnp.sum(lf[0] * lf[1])) - jnp.exp(jnp.sum(lf[2] * lf[3])) + lambda_init
    bias_tab = rel_bias.astype(jnp.float32).reshape(N_BUCKETS, DA_HEADS, 2)
    k_pos = jnp.arange(S)
    scale = DA_QK_DIM ** -0.5
    q_blocks = jnp.moveaxis(q.reshape(B, nb, BLOCK, DA_HEADS, 2, DA_QK_DIM), 1, 0)

    def block(args):
        qb, start = args
        q_pos = start + jnp.arange(BLOCK)
        dist = q_pos[:, None] - k_pos[None, :]
        bias = jnp.transpose(bias_tab[t5_bucket(dist)], (2, 3, 0, 1))
        s = jnp.einsum('bqhjd,bkhjd->bhjqk', qb, k).astype(jnp.float32) * scale + bias
        s = jnp.where(dist >= 0, s, NEG)
        p = jax.nn.softmax(s, axis=-1)
        a = p[:, :, 0] - lam_full * p[:, :, 1]
        return jnp.einsum('bhqk,bkhe->bqhe', a.astype(v.dtype), v)

    o = lax.map(block, (q_blocks, jnp.arange(nb) * BLOCK))
    o = jnp.moveaxis(o, 0, 1).reshape(B, S, DA_HEADS, DA_V_DIM)
    o = rmsnorm(o, subln) * (1.0 - lambda_init)
    return o.reshape(B, S, DA_HEADS * DA_V_DIM)

def stick_breaking_attention(h, w_qkv):
    B, S, _ = h.shape
    nb = S // BLOCK
    qkv = h @ w_qkv
    q, k, v = jnp.split(qkv, 3, axis=-1)
    q = q.reshape(B, S, SB_HEADS, SB_DIM)
    k = k.reshape(B, S, SB_HEADS, SB_DIM)
    v = v.reshape(B, S, SB_HEADS, SB_DIM)
    k_pos = jnp.arange(S)
    scale = SB_DIM ** -0.5
    q_blocks = jnp.moveaxis(q.reshape(B, nb, BLOCK, SB_HEADS, SB_DIM), 1, 0)

    def block(args):
        qb, start = args
        q_pos = start + jnp.arange(BLOCK)
        strict = k_pos[None, :] < q_pos[:, None]
        z = jnp.einsum('bqhd,bkhd->bhqk', qb, k).astype(jnp.float32) * scale
        log_1m_beta = jnp.where(strict, jax.nn.log_sigmoid(-z), 0.0)
        between = lax.cumsum(log_1m_beta, axis=3, reverse=True) - log_1m_beta
        a = jnp.where(strict, jnp.exp(jax.nn.log_sigmoid(z) + between), 0.0)
        return jnp.einsum('bhqk,bkhd->bqhd', a.astype(v.dtype), v)

    o = lax.map(block, (q_blocks, jnp.arange(nb) * BLOCK))
    return jnp.moveaxis(o, 0, 1).reshape(B, S, SB_HEADS * SB_DIM)

def sliding_window_attention(h, w_qkv, sinks, rel_bias):
    B, S, _ = h.shape
    nb = S // BLOCK
    G = SW_Q_HEADS // SW_KV_HEADS
    q_w = SW_Q_HEADS * SW_DIM
    kv_w = SW_KV_HEADS * SW_DIM
    qkv = h @ w_qkv
    q, k, v = jnp.split(qkv, [q_w, q_w + kv_w], axis=-1)
    q = q.reshape(B, nb, BLOCK, SW_KV_HEADS, G, SW_DIM)
    k = k.reshape(B, nb, BLOCK, SW_KV_HEADS, SW_DIM)
    v = v.reshape(B, nb, BLOCK, SW_KV_HEADS, SW_DIM)

    def band(t):
        prev = jnp.pad(t[:, :-1], ((0, 0), (1, 0), (0, 0), (0, 0), (0, 0)))
        return jnp.concatenate([prev, t], axis=2)

    kb, vb = band(k), band(v)
    i = jnp.arange(BLOCK)[:, None]
    j = jnp.arange(2 * BLOCK)[None, :]
    dist = i + BLOCK - j
    in_window = (dist >= 0) & (dist < SW_WINDOW)
    blk = jnp.arange(nb)[:, None, None]
    valid = in_window[None] & ((blk * BLOCK - BLOCK + j[None]) >= 0)
    bias = rel_bias.astype(jnp.float32)[t5_bucket(dist)]
    bias = bias.reshape(BLOCK, 2 * BLOCK, SW_KV_HEADS, G).transpose(2, 3, 0, 1)
    s = jnp.einsum('bnqgrd,bnkgd->bngrqk', q, kb).astype(jnp.float32) * (SW_DIM ** -0.5) + bias
    s = jnp.where(valid[None, :, None, None], s, NEG)
    sink = jnp.broadcast_to(sinks.astype(jnp.float32).reshape(SW_KV_HEADS, G, 1, 1), s.shape[:-1] + (1,))
    p = jax.nn.softmax(jnp.concatenate([s, sink], axis=-1), axis=-1)[..., :-1]
    o = jnp.einsum('bngrqk,bnkgd->bnqgrd', p.astype(vb.dtype), vb)
    return o.reshape(B, S, q_w)

def conv_gated_ffn(h, w_up, conv_w, conv_b, w_down):
    u = h @ w_up
    C = u.shape[-1]
    u = lax.conv_general_dilated(u, conv_w[:, None, :].astype(u.dtype), window_strides=(1,),
                                 padding=[(CONV_W - 1, 0)], dimension_numbers=('NWC', 'WIO', 'NWC'),
                                 feature_group_count=C) + conv_b
    gate, val = jnp.split(u, 2, axis=-1)
    return (jax.nn.silu(gate) * val) @ w_down

def first_inputs(seed: int = 0) -> dict:
    key = jax.random.key(seed)
    ks = jax.random.split(key, 20)
    D, F = D_MODEL, D_FF
    nrm = lambda k, shape, fan_in: jax.random.normal(k, shape, jnp.float32) * fan_in ** -0.5
    gain = lambda k, shape: 1.0 + 0.05 * jax.random.normal(k, shape, jnp.float32)
    return {
        'x': jax.random.normal(ks[0], (BATCH, SEQ, D), jnp.float32),
        'rel_bias': 0.5 * jax.random.normal(ks[1], (N_BUCKETS, N_BIAS_CH), jnp.float32),
        'attn_norm': gain(ks[2], (DEPTH, D)),
        'ffn_norm': gain(ks[3], (DEPTH, D)),
        'w_o': nrm(ks[4], (DEPTH, D, D), D),
        'da_w_qkv': nrm(ks[5], (N_A, D, 2 * DA_HEADS * 2 * DA_QK_DIM + DA_HEADS * DA_V_DIM), D),
        'da_lambda': 0.1 * jax.random.normal(ks[6], (N_A, 4, DA_QK_DIM), jnp.float32),
        'da_subln': gain(ks[7], (N_A, DA_V_DIM)),
        'sb_w_qkv': nrm(ks[8], (N_B, D, 3 * SB_HEADS * SB_DIM), D),
        'sw_w_qkv': nrm(ks[9], (N_C, D, (SW_Q_HEADS + 2 * SW_KV_HEADS) * SW_DIM), D),
        'sw_sinks': 0.5 * jax.random.normal(ks[10], (N_C, SW_Q_HEADS), jnp.float32),
        'ffn_w_up': nrm(ks[11], (DEPTH, D, 2 * F), D),
        'ffn_conv_w': nrm(ks[12], (DEPTH, CONV_W, 2 * F), CONV_W),
        'ffn_conv_b': 0.02 * jax.random.normal(ks[13], (DEPTH, 2 * F), jnp.float32),
        'ffn_w_down': nrm(ks[14], (DEPTH, F, D), F),
        'final_norm': gain(ks[15], (D,)),
    }

def first_block(x, rel_bias, attn_norm, ffn_norm, w_o, da_w_qkv, da_lambda, da_subln, sb_w_qkv,
              sw_w_qkv, sw_sinks, ffn_w_up, ffn_conv_w, ffn_conv_b, ffn_w_down, final_norm):
    for layer in range(DEPTH):
        mixer = layer % N_MIXERS
        slot = layer // N_MIXERS
        h = rmsnorm(x, attn_norm[layer])
        if mixer == 0:
            m = diff_attention(h, da_w_qkv[slot], da_lambda[slot], da_subln[slot], rel_bias,
                               lambda_init_fn(layer))
        elif mixer == 1:
            m = stick_breaking_attention(h, sb_w_qkv[slot])
        else:
            m = sliding_window_attention(h, sw_w_qkv[slot], sw_sinks[slot], rel_bias)
        x = x + m @ w_o[layer]
        h = rmsnorm(x, ffn_norm[layer])
        x = x + conv_gated_ffn(h, ffn_w_up[layer], ffn_conv_w[layer], ffn_conv_b[layer], ffn_w_down[layer])
    return rmsnorm(x, final_norm)


DEPTH_2 = 1

D_MIX = D_MODEL
N_ATTN_HEADS = 8
ATTN_HEAD_DIM = 64
D_ATTN = N_ATTN_HEADS * ATTN_HEAD_DIM
D_POOL = D_MIX - D_ATTN
POOL_WINDOWS = (2, 4, 8, 16)
N_POOL_GROUPS = len(POOL_WINDOWS)
POOL_GROUP_DIM = D_POOL // N_POOL_GROUPS
D_IN = 3 * D_ATTN + D_POOL
MOBA_BLOCK = 256
MOBA_TOPK = 3
Q_CHUNK = 32
N_MEM = 256
XA_HEADS = 4
XA_HEAD_DIM = D_MODEL // XA_HEADS
D_FF_2 = 2816
MACARON_WEIGHT = 0.5
RMS_EPS = 1e-6


def rmsnorm_2(x, g):
    xf = x.astype(jnp.float32)
    r = lax.rsqrt(jnp.mean(xf * xf, axis=-1, keepdims=True) + RMS_EPS)
    return (xf * r).astype(x.dtype) * g

def swiglu(h, w_gate, w_up, w_down):
    return (jax.nn.silu(h @ w_gate) * (h @ w_up)) @ w_down

def alibi_slopes(n_heads):
    s = 2.0 ** (-8.0 * np.arange(1, n_heads + 1) / n_heads)
    return jnp.asarray(s, dtype=jnp.float32)

def moba_attention(q, k, v, slopes):
    B, H, S, dh = q.shape
    L = MOBA_BLOCK
    s_pad = ((S + L - 1) // L) * L
    pad = s_pad - S
    kp = jnp.pad(k, ((0, 0), (0, 0), (0, pad), (0, 0)))
    vp = jnp.pad(v, ((0, 0), (0, 0), (0, pad), (0, 0)))
    nb = s_pad // L
    n_sel = min(MOBA_TOPK, nb)
    kb = kp.reshape(B, H, nb, L, dh)
    vb = vp.reshape(B, H, nb, L, dh)
    k_mean = jnp.mean(kb, axis=3)
    qs = q * (dh ** -0.5)
    bi = jnp.arange(B)[:, None, None, None]
    hi = jnp.arange(H)[None, :, None, None]
    lpos = jnp.arange(L)
    slot = jnp.arange(n_sel)
    blk_ids = jnp.arange(nb)
    n_chunks = S // Q_CHUNK

    def chunk(c):
        start = c * Q_CHUNK
        qc = lax.dynamic_slice_in_dim(qs, start, Q_CHUNK, axis=2)
        qpos = start + jnp.arange(Q_CHUNK)
        qpos_f = qpos.astype(jnp.float32)
        own = start // L
        gate = jnp.einsum('bhqd,bhnd->bhqn', qc, k_mean).astype(jnp.float32)
        gate = jnp.where(blk_ids < own, gate, -jnp.inf)
        _, idx = lax.top_k(gate, n_sel)
        slot_ok = slot < own
        k_sel = kb[bi, hi, idx]
        v_sel = vb[bi, hi, idx]
        kpos_sel = (idx[..., None] * L + lpos).astype(jnp.float32)
        s_sel = (jnp.einsum('bhqd,bhqrld->bhqrl', qc, k_sel).astype(jnp.float32)
                 - slopes[:, None, None, None] * (qpos_f[:, None, None] - kpos_sel))
        s_sel = jnp.where(slot_ok[:, None], s_sel, -jnp.inf)
        k_own = lax.dynamic_index_in_dim(kb, own, axis=2, keepdims=False)
        v_own = lax.dynamic_index_in_dim(vb, own, axis=2, keepdims=False)
        kpos_own = own * L + lpos
        s_own = (jnp.einsum('bhqd,bhld->bhql', qc, k_own).astype(jnp.float32)
                 - slopes[:, None, None] * (qpos_f[:, None] - kpos_own.astype(jnp.float32)[None, :]))
        s_own = jnp.where(kpos_own[None, :] <= qpos[:, None], s_own, -jnp.inf)
        scores = jnp.concatenate([s_sel.reshape(B, H, Q_CHUNK, n_sel * L), s_own], axis=-1)
        p = jax.nn.softmax(scores, axis=-1)
        p_sel = p[..., :n_sel * L].reshape(B, H, Q_CHUNK, n_sel, L).astype(v.dtype)
        p_own = p[..., n_sel * L:].astype(v.dtype)
        return (jnp.einsum('bhqrl,bhqrld->bhqd', p_sel, v_sel)
                + jnp.einsum('bhql,bhld->bhqd', p_own, v_own))

    outs = lax.map(chunk, jnp.arange(n_chunks))
    return outs.transpose(1, 2, 0, 3, 4).reshape(B, H, S, dh)

def multiscale_pool(p, pool_w, pool_scale):
    B, S, C = p.shape
    pf = p.reshape(B, S, N_POOL_GROUPS, POOL_GROUP_DIM).astype(jnp.float32)
    cs = jnp.concatenate([jnp.zeros((B, 1, N_POOL_GROUPS, POOL_GROUP_DIM), jnp.float32),
                          lax.cumsum(pf, axis=1)], axis=1)
    t = jnp.arange(S)
    outs = []
    for g, w in enumerate(POOL_WINDOWS):
        lo = jnp.maximum(t + 1 - w, 0)
        cnt = (t + 1 - lo).astype(jnp.float32)
        mean = (cs[:, 1:, g] - cs[:, lo, g]) / cnt[None, :, None]
        outs.append(mean - pf[:, :, g])
    d = jnp.stack(outs, axis=2).astype(p.dtype)
    y = jnp.einsum('bsgc,gcd->bsgd', d, pool_w)
    return y.reshape(B, S, C) * pool_scale

def memory_cross_attention(h, mem_n, wq, wkv, wo):
    B, S, _ = h.shape
    M = mem_n.shape[1]
    q = (h @ wq).reshape(B, S, XA_HEADS, XA_HEAD_DIM)
    kv = mem_n @ wkv
    k = kv[..., :D_MODEL].reshape(B, M, XA_HEADS, XA_HEAD_DIM)
    v = kv[..., D_MODEL:].reshape(B, M, XA_HEADS, XA_HEAD_DIM)
    s = jnp.einsum('bshd,bmhd->bhsm', q, k).astype(jnp.float32) * (XA_HEAD_DIM ** -0.5)
    p = jax.nn.softmax(s, axis=-1).astype(v.dtype)
    o = jnp.einsum('bhsm,bmhd->bshd', p, v).reshape(B, S, XA_HEADS * XA_HEAD_DIM)
    return o @ wo

def second_inputs(seed: int = 0) -> dict:
    key = jax.random.key(seed)
    ks = jax.random.split(key, 24)

    def nrm(k, shape, fan_in):
        return jax.random.normal(k, shape, jnp.float32) * fan_in ** -0.5

    def gain(k, shape):
        return 1.0 + 0.1 * jax.random.normal(k, shape, jnp.float32)

    L = DEPTH_2
    return {
        "x": jax.random.normal(ks[0], (BATCH, SEQ, D_MODEL), jnp.float32),
        "mem": jax.random.normal(ks[1], (BATCH, N_MEM, D_MODEL), jnp.float32),
        "ffn1_pre_g": gain(ks[2], (L, D_MODEL)),
        "ffn1_w_gate": nrm(ks[3], (L, D_MODEL, D_FF_2), D_MODEL),
        "ffn1_w_up": nrm(ks[4], (L, D_MODEL, D_FF_2), D_MODEL),
        "ffn1_w_down": nrm(ks[5], (L, D_FF_2, D_MODEL), D_FF_2),
        "ffn1_post_g": gain(ks[6], (L, D_MODEL)),
        "mix_pre_g": gain(ks[7], (L, D_MODEL)),
        "w_in": nrm(ks[8], (L, D_MODEL, D_IN), D_MODEL),
        "pool_w": nrm(ks[9], (L, N_POOL_GROUPS, POOL_GROUP_DIM, POOL_GROUP_DIM), POOL_GROUP_DIM),
        "pool_scale": gain(ks[10], (L, D_POOL)),
        "w_out": nrm(ks[11], (L, D_MIX, D_MODEL), D_MIX),
        "mix_post_g": gain(ks[12], (L, D_MODEL)),
        "xa_pre_g": gain(ks[13], (L, D_MODEL)),
        "mem_g": gain(ks[14], (L, D_MODEL)),
        "xa_wq": nrm(ks[15], (L, D_MODEL, XA_HEADS * XA_HEAD_DIM), D_MODEL),
        "xa_wkv": nrm(ks[16], (L, D_MODEL, 2 * XA_HEADS * XA_HEAD_DIM), D_MODEL),
        "xa_wo": nrm(ks[17], (L, XA_HEADS * XA_HEAD_DIM, D_MODEL), XA_HEADS * XA_HEAD_DIM),
        "xa_post_g": gain(ks[18], (L, D_MODEL)),
        "ffn2_pre_g": gain(ks[19], (L, D_MODEL)),
        "ffn2_w_gate": nrm(ks[20], (L, D_MODEL, D_FF_2), D_MODEL),
        "ffn2_w_up": nrm(ks[21], (L, D_MODEL, D_FF_2), D_MODEL),
        "ffn2_w_down": nrm(ks[22], (L, D_FF_2, D_MODEL), D_FF_2),
        "ffn2_post_g": gain(ks[23], (L, D_MODEL)),
    }

def second_block(x, mem, ffn1_pre_g, ffn1_w_gate, ffn1_w_up, ffn1_w_down, ffn1_post_g,
              mix_pre_g, w_in, pool_w, pool_scale, w_out, mix_post_g,
              xa_pre_g, mem_g, xa_wq, xa_wkv, xa_wo, xa_post_g,
              ffn2_pre_g, ffn2_w_gate, ffn2_w_up, ffn2_w_down, ffn2_post_g):
    B, S, _ = x.shape
    slopes = alibi_slopes(N_ATTN_HEADS)
    for l in range(DEPTH_2):
        h = rmsnorm_2(x, ffn1_pre_g[l])
        f = swiglu(h, ffn1_w_gate[l], ffn1_w_up[l], ffn1_w_down[l])
        x = x + MACARON_WEIGHT * rmsnorm_2(f, ffn1_post_g[l])

        h = rmsnorm_2(x, mix_pre_g[l])
        proj = h @ w_in[l]
        q = proj[..., :D_ATTN]
        k = proj[..., D_ATTN:2 * D_ATTN]
        v = proj[..., 2 * D_ATTN:3 * D_ATTN]
        p_in = proj[..., 3 * D_ATTN:]
        to_heads = lambda t: t.reshape(B, S, N_ATTN_HEADS, ATTN_HEAD_DIM).transpose(0, 2, 1, 3)
        attn = moba_attention(to_heads(q), to_heads(k), to_heads(v), slopes)
        attn = attn.transpose(0, 2, 1, 3).reshape(B, S, D_ATTN)
        pool = multiscale_pool(p_in, pool_w[l], pool_scale[l])
        y = jnp.concatenate([attn, pool], axis=-1) @ w_out[l]
        x = x + rmsnorm_2(y, mix_post_g[l])

        h = rmsnorm_2(x, xa_pre_g[l])
        mem_n = rmsnorm_2(mem, mem_g[l])
        c = memory_cross_attention(h, mem_n, xa_wq[l], xa_wkv[l], xa_wo[l])
        x = x + rmsnorm_2(c, xa_post_g[l])

        h = rmsnorm_2(x, ffn2_pre_g[l])
        f = swiglu(h, ffn2_w_gate[l], ffn2_w_up[l], ffn2_w_down[l])
        x = x + MACARON_WEIGHT * rmsnorm_2(f, ffn2_post_g[l])
    return x


def setup_inputs(seed=0):
    out = dict(first_inputs(seed))
    for name, value in second_inputs(seed + 1).items():
        if name != "x":
            out[name + "_2"] = value
    return out


def reference(
    x, rel_bias, attn_norm, ffn_norm, w_o, da_w_qkv, da_lambda, da_subln, sb_w_qkv, sw_w_qkv,
    sw_sinks, ffn_w_up, ffn_conv_w, ffn_conv_b, ffn_w_down, final_norm, mem_2, ffn1_pre_g_2,
    ffn1_w_gate_2, ffn1_w_up_2, ffn1_w_down_2, ffn1_post_g_2, mix_pre_g_2, w_in_2, pool_w_2,
    pool_scale_2, w_out_2, mix_post_g_2, xa_pre_g_2, mem_g_2, xa_wq_2, xa_wkv_2, xa_wo_2,
    xa_post_g_2, ffn2_pre_g_2, ffn2_w_gate_2, ffn2_w_up_2, ffn2_w_down_2, ffn2_post_g_2,
):
    x = first_block(
        x, rel_bias, attn_norm, ffn_norm, w_o, da_w_qkv, da_lambda, da_subln, sb_w_qkv,
        sw_w_qkv, sw_sinks, ffn_w_up, ffn_conv_w, ffn_conv_b, ffn_w_down, final_norm,
    )
    return second_block(
        x, mem_2, ffn1_pre_g_2, ffn1_w_gate_2, ffn1_w_up_2, ffn1_w_down_2, ffn1_post_g_2,
        mix_pre_g_2, w_in_2, pool_w_2, pool_scale_2, w_out_2, mix_post_g_2, xa_pre_g_2, mem_g_2,
        xa_wq_2, xa_wkv_2, xa_wo_2, xa_post_g_2, ffn2_pre_g_2, ffn2_w_gate_2, ffn2_w_up_2,
        ffn2_w_down_2, ffn2_post_g_2,
    )


_drawn_inputs = setup_inputs


def setup_inputs(seed=0):
    import zlib

    import numpy as np

    out = dict(_drawn_inputs(seed))
    spreads = {}
    factors = {'sw_sinks': 4.658}
    for name, (base, spread) in spreads.items():
        noise = np.random.default_rng([zlib.crc32(name.encode()), seed]).standard_normal(out[name].shape)
        drawn = base * np.exp(spread * noise) if base else spread * noise
        out[name] = __import__('jax').numpy.asarray(drawn.astype(out[name].dtype))
    for name, factor in factors.items():
        out[name] = (out[name] * factor).astype(out[name].dtype)
    return out
```

```python
import math
from contextlib import ExitStack

import numpy as np

import concourse.bass as bass
from concourse import mybir

P = 128
T = 256
D = 1024
KC = D // P
QB = T // P
BW = 256
BE = KC * BW
RING = 3
DEPTH = 4
F1, F2 = 2752, 2816
NSTEP = 11
NLOOP = 4
NCH = 2 * NSTEP
HD = 64
N_BUCKETS, MAX_DIST = 32, 128
NEG = -1e30
EPS = 1e-6
TW = 384
MACARON = 0.5

F32, F32R = mybir.dt.float32, mybir.dt.float32r
ALU, ACT = mybir.AluOpType, mybir.ActivationFunctionType
AX_X = mybir.AxisListType.X

G_ATTN, G_FFN, G_FINAL = 0, 4, 8
(G_FFN1_PRE, G_FFN1_POST, G_MIX_PRE, G_MIX_POST, G_XA_PRE, G_MEM, G_XA_POST, G_FFN2_PRE,
 G_FFN2_POST) = range(9, 18)
G_POOL, G_SUBLN, NG = 18, 19, 21


def lambda_init(layer):
    return 0.8 - 0.6 * math.exp(-0.3 * layer)


def dve_splits(n):
    return 2 * (n // RING) + min(n % RING, 1) + 1


def plan():
    c = dict(n=0, u=0, f=0, stat=0, x=4, y=0, hd=0, sg=0, fill=[0, 0], kg=0)
    out = []

    def prep(src, gain, a, r):
        out.append(dict(kind="prep", src=src, gain=gain, act=a, fill=c["fill"][a], stat=c["stat"], x=c["x"], r=r))
        c["fill"][a] += 1
        c["stat"] += 1
        return c["stat"] - 1

    def lin(a, blocks, stat=None, r=0):
        out.append(dict(kind="lin", act=a, fill=c["fill"][a] - 1, n=c["n"], u=c["u"], blocks=blocks, stat=stat, r=r,
                        x=c["x"], y=c["y"]))
        c["n"] += len(blocks)
        if blocks[0][0] == "proj":
            c["x"] += 4
        elif blocks[0][0] == "y":
            c["y"] += 4
        else:
            c["u"] += len(blocks)

    def attend(kind, a, heads, **kw):
        out.append(dict(kind=kind, act=a, fill=c["fill"][a], sg=c["sg"], kg=c["kg"], u=c["u"], heads=heads, y=c["y"],
                        stat=c["stat"], **kw))
        c["fill"][a] += 1
        if kind == "soft":
            c["sg"] += heads // 2
        if kw.get("diff") is not None:
            c["y"] += 8
        if kind == "stick":
            c["kg"] += heads // 2

    def ffn(F, a, wup, wdown, conv, dst, stat):
        out.append(dict(kind="ffn", F=F, act=a, fill=c["fill"][a] - 1, n=c["n"], u=c["u"], f=c["f"], hd=c["hd"],
                        up=wup, down=wdown, conv=conv, dst=dst, stat=stat, x=c["x"], y=c["y"]))
        c["n"] += 3 * NSTEP
        c["u"] += NCH
        c["f"] += NCH
        c["hd"] += NSTEP
        c[dst] += 4

    def scale_x(src, gain, weight):
        out.append(dict(kind="post", src=src, gain=gain, weight=weight, stat=c["stat"], x=c["x"], y=c["y"]))
        c["stat"] += 1
        c["x"] += 4

    def qkv(w, nq, nk, nv, k="k"):
        return ([("q", w, i * BW, i) for i in range(nq)] + [(k, w, (nq + i) * BW, i) for i in range(nk)]
                + [("v", w, (nq + nk + i) * BW, i) for i in range(nv)])

    for l in range(DEPTH):
        s = prep("x", G_ATTN + l, 0, 0)
        if l % 3 == 0:
            lin(0, qkv(("da_w_qkv", l // 3), 4, 4, 4), s)
            attend("soft", 1, 16, diff=l // 3, layer=l, scale=HD ** -0.5)
        elif l % 3 == 1:
            lin(0, qkv(("sb_w_qkv", 0), 4, 4, 4), s)
            attend("stick", 1, 16, scale=HD ** -0.5)
        else:
            lin(0, qkv(("sw_w_qkv", 0), 4, 1, 1, "kdup"), s)
            attend("soft", 1, 16, sink=True, scale=HD ** -0.5)
        lin(1, [("proj", ("w_o", l), i * BW, i) for i in range(4)])
        s = prep("x", G_FFN + l, 0, 0)
        ffn(F1, 0, [("ffn_w_up", l, 0), ("ffn_w_up", l, F1)], ("ffn_w_down", l), l, "x", s)
    scale_x("x", G_FINAL, None)

    s = prep("x", G_FFN1_PRE, 0, 0)
    ffn(F2, 0, [("ffn1_w_gate_2", 0, 0), ("ffn1_w_up_2", 0, 0)], ("ffn1_w_down_2", 0), None, "y", s)
    scale_x("y", G_FFN1_POST, MACARON)
    s = prep("x", G_MIX_PRE, 0, 0)
    lin(0, qkv(("w_in_2", 0), 2, 2, 2) + [("pool", ("w_in_2", 0), (6 + i) * BW, i) for i in range(2)], s)
    attend("soft", 1, 8, moba=True, scale=HD ** -0.5)
    lin(1, [("y", ("w_out_2", 0), i * BW, i) for i in range(4)])
    scale_x("y", G_MIX_POST, 1.0)
    s = prep("mem", G_MEM, 0, 1)
    lin(0, [("k", ("xa_wkv_2", 0), i * BW, i) for i in range(4)]
        + [("v", ("xa_wkv_2", 0), (4 + i) * BW, i) for i in range(4)], s, 1)
    s = prep("x", G_XA_PRE, 1, 0)
    lin(1, [("q", ("xa_wq_2", 0), i * BW, i) for i in range(4)], s)
    attend("soft", 0, 4, cross=True, scale=256 ** -0.5)
    lin(0, [("y", ("xa_wo_2", 0), i * BW, i) for i in range(4)])
    scale_x("y", G_XA_POST, 1.0)
    s = prep("x", G_FFN2_PRE, 0, 0)
    ffn(F2, 0, [("ffn2_w_gate_2", 0, 0), ("ffn2_w_up_2", 0, 0)], ("ffn2_w_down_2", 0), None, "y", s)
    scale_x("y", G_FFN2_POST, MACARON)
    return out, c


def model_kernel(nc, io, out):
    phases, total = plan()
    NBLOCKS = total["n"]
    rT_count = {n: i + 1 for i, n in enumerate(ph["n"] for ph in phases
                                               if ph["kind"] == "lin" and any(b[0] == "v" for b in ph["blocks"]))}
    ok_count = {sg: i + 1 for i, sg in enumerate(ph["sg"] for ph in phases if ph["kind"] == "soft" and not ph.get("cross"))}
    ok_count["cnt"] = 5
    with ExitStack() as ctx:
        def sb(name, shape, dt=F32):
            return ctx.enter_context(nc.sbuf_tensor("sb_" + name, shape, dt))

        def sem(name):
            return ctx.enter_context(nc.semaphore(name))

        raw = sb("raw", [P, RING, BE])
        w_hi = sb("w_hi", [P, RING, BE], F32R)
        w_lo = sb("w_lo", [P, RING, BE], F32R)
        x = sb("x", [P, KC, T])
        a_hi = [sb(f"a_hi{i}", [P, KC, T], F32R) for i in range(2)]
        a_lo = [sb(f"a_lo{i}", [P, KC, T], F32R) for i in range(2)]
        qT = sb("qT", [P, KC, T])
        kT = sb("kT", [P, KC, T])
        v = sb("v", [P, QB, D])
        y = sb("y", [P, KC, T])
        work = sb("work", [P, 6144])
        bias = sb("bias", [P, 16, T])
        cw = sb("cw", [P, NCH * 32])
        gains = sb("gains", [P, KC, NG])
        ident = sb("ident", [P, P])
        ones = sb("ones", [P, P])
        upper = sb("upper", [P, P])
        r_all = sb("r_all", [P, 2, T])
        sd = sb("sd", [P, T])
        rT = sb("rT", [P, QB])
        poolw = sb("poolw", [P, 4, P])
        lam = sb("lam", [P, 2, 4, HD])
        lam_s = sb("lam_s", [P, 4])
        lam_fac = sb("lam_fac", [P, 2, 4])
        sink = sb("sink", [P, 16])
        sm_small = sb("sm_small", [P, 2, 5, 4])
        hh = sb("hh", [P, 4, T], F32R)
        hl = sb("hl", [P, 4, T], F32R)
        eps_t = sb("eps_t", [P, 2])

        us = work[:, 0:1024].rearrange("p (c h t) -> p c h t", c=2, h=2)
        acc = work[:, 1024:2048].rearrange("p (c h t) -> p c h t", c=2, h=2)
        sil = work[:, 2048:2560].rearrange("p (c t) -> p c t", c=2)
        hid = work[:, 2560:3072].rearrange("p (c t) -> p c t", c=2)
        prob = work[:, 0:2048].rearrange("p (b s k) -> p b s k", b=2, s=2)
        probT = work[:, 2048:4096].rearrange("p (b s k) -> p b s k", b=2, s=2)
        diag = work[:, 4096:5120].rearrange("p (b i q) -> p b i q", b=2, i=4)
        win_b = work[:, 5120:6144].rearrange("p (g t) -> p g t", g=4)
        zbuf = work[:, 0:3072].rearrange("p (h k) -> p h k", h=8)
        tbuf = work[:, 3072:6144].rearrange("p (h k) -> p h k", h=8)
        conv_rows = work[0:32, 0:2816]
        gain_rows = work[0:NG, 2816:3840]
        x_rows = work[:, 4096:6144].rearrange("p (b d) -> p b d", b=QB)
        sq = qT
        pin = y[:, 0:4, :]
        win_a = y[:, 4:8, :]
        inv_cnt = bias[:, 8:12, :]
        table_sb = v[0:16, 0, 0:TW]

        PS = ctx.enter_context(nc.psum_tensor("ps", [P, 8, 512], F32))
        DB = [PS[:, i, :] for i in range(4)]
        UB = [PS[:, 4 + i, :] for i in range(4)]

        bias_dram = nc.dram_tensor("bias_dram", [16, P * TW], F32)

        s_const = sem("s_const")
        s_xin = sem("s_xin")
        s_gin = sem("s_gin")
        s_cin = sem("s_cin")
        s_misc = sem("s_misc")
        s_tab_in = sem("s_tab_in")
        s_mem_in = sem("s_mem_in")
        s_setup_pe = sem("s_setup_pe")
        s_gain = sem("s_gain")
        s_conv = sem("s_conv")
        s_tab = sem("s_tab")
        s_tab_out = sem("s_tab_out")
        s_bias_in = sem("s_bias_in")
        s_bias_ok = sem("s_bias_ok")
        s_lam = sem("s_lam")
        s_memT = sem("s_memT")
        s_mem_ok = sem("s_mem_ok")
        raw_ready = [sem(f"raw_ready{i}") for i in range(RING)]
        hi_ready = sem("hi_ready")
        lo_dve = sem("lo_dve")
        lo_pool = sem("lo_pool")
        blocks_done = sem("blocks_done")
        half_done = sem("half_done")
        u_free = sem("u_free")
        x_ready = sem("x_ready")
        y_ready = sem("y_ready")
        act_hi = [sem(f"act_hi{i}") for i in range(2)]
        act_lo = [sem(f"act_lo{i}") for i in range(2)]
        sq_ready = sem("sq_ready")
        sq_tree = sem("sq_tree")
        sq_sum = sem("sq_sum")
        ss_done = sem("ss_done")
        sd_ready = sem("sd_ready")
        r_ready = sem("r_ready")
        rT_done = sem("rT_done")
        rT_ready = sem("rT_ready")
        post_t = sem("post_t")
        conv_acc = sem("conv_acc")
        conv_t1 = sem("conv_t1")
        conv_t0 = sem("conv_t0")
        sil_ready = sem("sil_ready")
        hid_ready = sem("hid_ready")
        hh_ready = sem("hh_ready")
        hl_ready = sem("hl_ready")
        scores_ready = sem("scores_ready")
        biased = sem("biased")
        negmax = sem("negmax")
        exp_ready = sem("exp_ready")
        sink_exp = sem("sink_exp")
        rs_ready = sem("rs_ready")
        diag_ready = sem("diag_ready")
        pt_done = sem("pt_done")
        pt_ready = sem("pt_ready")
        pv_done = sem("pv_done")
        sub_sq = sem("sub_sq")
        sub_ss = sem("sub_ss")
        sub_sd = sem("sub_sd")
        sub_t = sem("sub_t")
        win_ok = sem("win_ok")
        poolmix_done = sem("poolmix_done")
        z_done = sem("z_done")
        z_copied = sem("z_copied")
        t_exp = sem("t_exp")
        t_ln = sem("t_ln")
        sp_sum = sem("sp_sum")
        sp_ready = sem("sp_ready")
        cs_done = sem("cs_done")
        z_less = sem("z_less")
        a_exp = sem("a_exp")
        a_ready = sem("a_ready")
        spv_done = sem("spv_done")
        dve_link = sem("dve_link")
        act_link = sem("act_link")
        pool_link = sem("pool_link")
        s_outT = sem("s_outT")
        s_outc = sem("s_outc")
        s_out = sem("s_out")

        block = ctx.enter_context(nc.Block())

        def both(ap, n=2):
            return ap.unsqueeze(1).to_broadcast([ap.shape[0], n, ap.shape[1]])

        def wait_block(eng, a, s=0):
            if a % RING == 2:
                eng.wait_ge(lo_pool, a // RING + 1 + s)
            else:
                eng.wait_ge(lo_dve, dve_splits(a) + 2 * s)

        def up_block(ph, s0, part):
            return ph["n"] + part if s0 == 0 else ph["n"] + 3 * s0 - 1 + part

        def down_block(ph, s0):
            return ph["n"] + (3 * NSTEP - 1 if s0 == NSTEP - 1 else 3 * s0 + 4)

        def cols(ph, s0):
            return (ph["F"] - (NSTEP - 1) * 2 * P) // 2 if s0 == NSTEP - 1 else P

        def ffn_steps(eng, up, down):
            up(0, 0)
            with eng.Fori(0, NLOOP) as i:
                for d in range(2):
                    up(d + 1, 2 * i)
                    down(d, 2 * i)
            for s in range(2 * NLOOP, NSTEP - 1):
                up(s + 1, 0)
                down(s, 0)
            down(NSTEP - 1, 0)

        @block.sync
        def _(sp):
            def load(a, s, dst, src):
                if a >= RING:
                    wait_block(sp, a - RING, s)
                sp.dma_start(dst, src).then_inc(raw_ready[a % RING], 16)

            def slot(a, k):
                return raw[:, a % RING, :].rearrange("p (k n) -> p k n", k=k)

            sp.dma_start(x_rows, io["x"][0].rearrange("(b p) d -> p b d", p=P)).then_inc(s_xin, 16)
            sp.wait_ge(s_const, 1)
            for i, (name, n) in enumerate((("attn_norm", 4), ("ffn_norm", 4))):
                sp.dma_start(gain_rows[4 * i:4 * i + n, :], io[name]).then_inc(s_gin, 16)
            sp.dma_start(gain_rows[8:9, :], io["final_norm"].unsqueeze(0)).then_inc(s_gin, 16)
            for i, name in enumerate(("ffn1_pre_g_2", "ffn1_post_g_2", "mix_pre_g_2", "mix_post_g_2", "xa_pre_g_2",
                                      "mem_g_2", "xa_post_g_2", "ffn2_pre_g_2", "ffn2_post_g_2")):
                sp.dma_start(gain_rows[9 + i:10 + i, :], io[name]).then_inc(s_gin, 16)
            sp.dma_start(gain_rows[18:19, 0:512], io["pool_scale_2"]).then_inc(s_gin, 16)
            sp.dma_start(gain_rows[19:21, 0:P], io["da_subln"]).then_inc(s_gin, 16)
            for ph in phases:
                if ph["kind"] == "lin":
                    for i, (_, (w, l), c0, _) in enumerate(ph["blocks"]):
                        src = io[w][l][:, c0:c0 + BW].rearrange("(k p) n -> p k n", p=P)
                        load(ph["n"] + i, 0, slot(ph["n"] + i, KC), src)
                elif ph["kind"] == "ffn":
                    def up(s0, s, ph=ph):
                        n = cols(ph, s0)
                        for part in range(2):
                            w, l, c0 = ph["up"][part]
                            b = up_block(ph, s0, part)
                            src = io[w][l][:, bass.ds(c0 + 2 * P * s0 + 2 * P * s, 2 * n)]
                            load(b, s, slot(b, KC)[:, :, 0:2 * n], src.rearrange("(k p) n -> p k n", p=P))

                    def down(s0, s, ph=ph):
                        n = cols(ph, s0)
                        w, l = ph["down"]
                        b = down_block(ph, s0)
                        src = io[w][l][bass.ds(2 * P * s0 + 2 * P * s, 2 * n), :]
                        load(b, s, slot(b, 2)[0:n, :, :], src.rearrange("(k p) n -> p k n", p=n))

                    ffn_steps(sp, up, down)
                elif ph.get("moba"):
                    moba_lo = 8 * (ph["fill"] + 1)
                elif ph.get("gain") == G_MIX_POST:
                    sp.wait_ge(act_lo[1], moba_lo)
                    sp.dma_start(x_rows, io["mem_2"][0].rearrange("(b p) d -> p b d", p=P)).then_inc(s_mem_in, 16)
            sp.wait_ge(s_outc, 4)
            sp.dma_start(out[0].rearrange("(b p) d -> p b d", p=P), x_rows).then_inc(s_out, 16)
            sp.wait_ge(s_out, 16)

        def make_alibi(pool, link):
            dist = y[:, 0, :]
            idx = y[:, 1, :].bitcast(mybir.dt.int32)
            link(pool.iota(idx, pattern=[[-1, T]], base=P, channel_multiplier=1))
            link(pool.tensor_copy(dist, idx))
            for h in range(8):
                ins = pool.tensor_scalar(bias[:, h, :], dist, -2.0 ** -(h + 1), None, ALU.mult)
            link(ins)
            pool.affine_select(out=bias[:, 0:8, P:T], in_=bias[:, 0:8, P:T], compare_op=ALU.is_ge, fill=NEG, base=0,
                               pattern=[[0, 8], [-1, P]], channel_multiplier=1).then_inc(s_bias_ok, 1)
            link(pool.iota(idx, pattern=[[1, T]], base=1, channel_multiplier=0))
            link(pool.tensor_copy(dist, idx))
            for g in range(4):
                ins = pool.tensor_scalar(inv_cnt[:, g, :], dist, float(2 << g), None, ALU.min)
            ins.then_inc(s_bias_ok, 1)

        @block.gpsimd
        def _(pool):
            links = [0]

            def link(ins):
                links[0] += 1
                ins.then_inc(pool_link, 1)
                pool.wait_ge(pool_link, links[0])

            def split(a, s=0):
                if a % RING == 2 and a < NBLOCKS:
                    pool.wait_ge(hi_ready, a + 1 + RING * s)
                    pool.tensor_tensor(w_lo[:, 2, :], raw[:, 2, :], w_hi[:, 2, :].bitcast(F32), ALU.subtract)\
                        .then_inc(lo_pool, 1)

            def causal(ap, heads, op, fill):
                return pool.affine_select(out=ap, in_=ap, compare_op=op, fill=fill, base=0,
                                          pattern=[[0, heads], [-1, P]], channel_multiplier=1)

            def anticausal(ap, heads):
                return pool.affine_select(out=ap, in_=ap, compare_op=ALU.is_gt, fill=0.0, base=0,
                                          pattern=[[0, heads], [1, P]], channel_multiplier=-1)

            pool.memset(work[0:32, 0:3840], 0.0).then_inc(s_const, 1)
            link(pool.memset(ident[:, :], 0.0))
            pool.affine_select(out=ident[:, :], in_=ident[:, :], compare_op=ALU.not_equal, fill=1.0, base=0,
                               pattern=[[-1, P]], channel_multiplier=1).then_inc(s_const, 1)
            pool.memset(ones[:, :], 1.0).then_inc(s_const, 1)
            link(pool.memset(upper[:, :], 1.0))
            pool.affine_select(out=upper[:, :], in_=upper[:, :], compare_op=ALU.is_ge, fill=0.0, base=0,
                               pattern=[[-1, P]], channel_multiplier=1).then_inc(s_const, 1)
            pool.memset(lam_fac[:, :, :], 1.0).then_inc(s_const, 1)

            def mask_bias():
                causal(bias[:, :, P:T], 16, ALU.is_ge, NEG).then_inc(s_bias_ok, 1)

            def square_sum(ph):
                pool.wait_ge(sq_ready, ph["stat"] + 1)
                for i, n in enumerate((4, 2, 1)):
                    ins = pool.tensor_tensor(sq[:, 0:n, :], sq[:, 0:n, :], sq[:, n:2 * n, :], ALU.add)
                    if n > 1:
                        ins.then_inc(sq_tree, 1)
                        pool.wait_ge(sq_tree, 2 * ph["stat"] + i + 1)
                    else:
                        ins.then_inc(sq_sum, 1)

            def load_bias():
                src = bass.AP(bias_dram, 127, [[TW - 1, P], [P * TW, 16], [1, T]])
                pool.dma_start(bias[:, :, :], src).then_inc(s_bias_in, 16)

            pool.wait_ge(s_tab, 1)
            pool.dma_start(bias_dram[:, :].rearrange("h (q z) -> h q z", q=P),
                           table_sb.unsqueeze(1).to_broadcast([16, P, TW])).then_inc(s_tab_out, 16)
            split(0), split(1)
            for ph in phases:
                kind = ph["kind"]
                if kind in ("prep", "post"):
                    square_sum(ph)
                elif kind == "lin":
                    for i in range(len(ph["blocks"])):
                        b = ph["n"] + i
                        if i == 0:
                            split(b + 2)
                        if b == 0:
                            pool.wait_ge(s_tab_out, 16)
                            load_bias()
                        if i < len(ph["blocks"]) - 1:
                            split(b + 3)
                    if ph["n"] == 0:
                        pool.wait_ge(s_bias_in, 16)
                        mask_bias()
                elif kind == "soft":
                    for g in range(ph["heads"] // 2):
                        pool.wait_ge(rs_ready, ph["sg"] + g + 1)
                        if g >= 2:
                            pool.wait_ge(pt_done, ph["sg"] + g - 1)
                        for i in range(4):
                            ins = pool.tensor_scalar(diag[:, g % 2, i, :], ident[:, :], sm_small[:, g % 2, 3, i:i + 1],
                                                     None, ALU.mult)
                        ins.then_inc(diag_ready, 1)
                elif kind == "stick":
                    for half in range(2):
                        for g in range(4):
                            pool.wait_ge(sp_sum, ph["kg"] + 4 * half + g + 1)
                            anticausal(tbuf[:, 2 * g:2 * g + 2, 0:P], 2)
                            anticausal(tbuf[:, 2 * g:2 * g + 2, 2 * P:3 * P], 2).then_inc(sp_ready, 1)
                        for g in range(4):
                            pool.wait_ge(a_exp, ph["kg"] + 4 * half + g + 1)
                            anticausal(zbuf[:, 2 * g:2 * g + 2, 0:P], 2)
                            anticausal(zbuf[:, 2 * g:2 * g + 2, 2 * P:3 * P], 2).then_inc(a_ready, 1)
                elif kind == "ffn":
                    def hidden(s0, s, ph=ph):
                        n = cols(ph, s0)
                        for c in range(2):
                            f = ph["f"] + 2 * s0 + c
                            at = 2 * (s0 % 2) + c
                            pool.wait_ge(hh_ready, f + 1 + 2 * s)
                            pool.tensor_tensor(hl[0:n, at, :], hid[0:n, c, :], hh[0:n, at, :].bitcast(F32),
                                               ALU.subtract).then_inc(hl_ready, 1)

                    def up(s0, s, ph=ph):
                        b = up_block(ph, s0, 0)
                        if s0 == 0:
                            split(b + 2)
                        split(b + 3, s)
                        split(b + 4, s)
                        hidden(s0, s)

                    def down(s0, s, ph=ph):
                        if s0 < NSTEP - 1:
                            split(down_block(ph, s0) + 3, s)

                    ffn_steps(pool, up, down)
                    if ph["conv"] == 1:
                        pool.affine_select(out=bias[:, :, 0:P], in_=bias[:, :, 0:P], compare_op=ALU.is_gt, fill=NEG,
                                           base=0, pattern=[[0, 16], [1, P]], channel_multiplier=-1)\
                            .then_inc(s_bias_ok, 1)
                    if ph["conv"] == 2:
                        load_bias()
                        pool.wait_ge(s_bias_in, 32)
                        mask_bias()
                    if ph["conv"] == 3:
                        make_alibi(pool, link)

        def softmax_act(act, ph):
            G = ph["heads"] // 2
            a = ph["act"]
            W = T * 2 if ph.get("cross") else 3 * P
            A = T if ph.get("cross") else P

            def exps(g):
                sg = ph["sg"] + g
                act.wait_ge(negmax, sg + 1)
                small = sm_small[:, g % 2]
                for i in range(4):
                    s, lo, hi = i % 2, (0, A)[i // 2], (A, W)[i // 2]
                    p = prob[:, g % 2, s, lo:hi]
                    ins = act.activation(p, p, ACT.Exp, bias=small[:, 1, i:i + 1], accum_out=small[:, 2, i:i + 1])
                if ph.get("sink"):
                    ins = act.activation(small[:, 4, :], small[:, 4, :], ACT.Exp)
                ins.then_inc(exp_ready, 1)

            def copy_pt(g):
                sg = ph["sg"] + g
                act.wait_ge(pt_done, sg + 1)
                if g >= 2:
                    act.wait_ge(pv_done, sg - 1)
                if ph.get("diff") is not None:
                    act.activation(probT[:, g % 2, 0, 0:W], UB[0][:, 0:W], ACT.Copy).then_inc(pt_ready, 1)
                else:
                    act.activation(probT[:, g % 2, :, 0:W], PS[:, 4:6, 0:W], ACT.Copy).then_inc(pt_ready, 1)

            def out_hi(g):
                sg = ph["sg"] + g
                act.wait_ge(pv_done, sg + 1)
                if ph.get("diff") is not None:
                    act.activation(y[:, g, :], UB[2 + g % 2][:, 0:T], ACT.Copy).then_inc(y_ready, 1)
                elif ph.get("cross"):
                    for i in range(4):
                        act.activation(a_hi[a][:, 4 * g + i, :], UB[2 + i // 2][:, (i % 2) * T:(i % 2 + 1) * T],
                                       ACT.Copy).then_inc(act_hi[a], 1)
                else:
                    act.activation(a_hi[a][:, g, :], UB[2 + g % 2][:, 0:T], ACT.Copy).then_inc(act_hi[a], 1)

            for g in range(G + 2):
                if g < G:
                    exps(g)
                if 1 <= g <= G:
                    copy_pt(g - 1)
                if g >= 2:
                    out_hi(g - 2)
            if ph.get("diff") is not None:
                j = ph["diff"]
                act.wait_ge(y_ready, ph["y"] + 8)
                for i in range(4):
                    act.activation(sq[:, 2 * i:2 * i + 2, :], y[:, 2 * i:2 * i + 2, :], ACT.Square).then_inc(sub_sq, 1)
                for i in range(4):
                    act.wait_ge(sub_ss, 4 * j + i + 1)
                    act.activation(kT[:, 2 * i:2 * i + 2, :], DB[i].rearrange("p (a b) -> p a b", a=2), ACT.Sqrt,
                                   scale=1.0 / P, bias=eps_t[:, 0:1]).then_inc(sub_sd, 1)
                for i in range(4):
                    act.wait_ge(sub_t, 4 * j + i + 1)
                    act.activation(a_hi[a][:, 2 * i:2 * i + 2, :], y[:, 2 * i:2 * i + 2, :], ACT.Copy,
                                   scale=1.0 - lambda_init(ph["layer"])).then_inc(act_hi[a], 2)
            if ph.get("moba"):
                act.wait_ge(poolmix_done, 1)
                for g in range(4):
                    act.activation(a_hi[a][:, 4 + g, :], DB[g // 2][:, (g % 2) * T:(g % 2 + 1) * T], ACT.Copy,
                                   scale=gains[:, g, G_POOL:G_POOL + 1]).then_inc(act_hi[a], 1)

        def stick_act(act, ph):
            a = ph["act"]
            for half in range(2):
                k0 = ph["kg"] + 4 * half
                for g in range(4):
                    act.wait_ge(z_done, k0 + g + 1)
                    act.wait_ge(z_copied, k0 + g + 1)
                    S = PS[:, 2 * (g % 2):2 * (g % 2) + 2, 0:3 * P]
                    t = tbuf[:, 2 * g:2 * g + 2, :]
                    if half == 1:
                        act.wait_ge(cs_done, k0)
                    act.activation(t, S, ACT.Abs, scale=ph["scale"]).then_inc(act_link, 1)
                    act.wait_ge(act_link, k0 - ph["kg"] + g + 1)
                    act.activation(t, t, ACT.Exp, scale=-1.0).then_inc(t_exp, 1)
                for g in range(4):
                    t = tbuf[:, 2 * g:2 * g + 2, :]
                    act.wait_ge(t_exp, k0 + g + 1)
                    act.activation(t, t, ACT.Ln, bias=1.0).then_inc(t_ln, 1)
                for g in range(4):
                    z = zbuf[:, 2 * g:2 * g + 2, :]
                    act.wait_ge(z_less, k0 + g + 1)
                    act.activation(z, z, ACT.Exp).then_inc(a_exp, 1)
                for g in range(4):
                    act.wait_ge(spv_done, k0 + g + 1)
                    act.activation(a_hi[a][:, 4 * half + g, :], UB[g][:, 0:T], ACT.Copy).then_inc(act_hi[a], 1)

        @block.scalar
        def _(act):
            act.wait_ge(s_const, 1)
            act.dma_start(conv_rows[0:24, 0:F1], io["ffn_conv_w"].rearrange("l w (h f) -> (l w h) f", h=2))\
                .then_inc(s_cin, 16)
            act.dma_start(conv_rows[24:32, 0:F1], io["ffn_conv_b"].rearrange("l (h f) -> (l h) f", h=2))\
                .then_inc(s_cin, 16)
            act.dma_start(kT[0:N_BUCKETS, 0, 0:16], io["rel_bias"]).then_inc(s_tab_in, 16)
            act.dma_start(kT[0:N_BUCKETS, 2:4, :].rearrange("p a b -> p (a b)")[:, 0:TW], io["bucket_of_distance"])\
                .then_inc(s_tab_in, 16)
            act.dma_start(lam[:, :, :, :].rearrange("p a b c -> p (a b c)"),
                          io["da_lambda"].rearrange("a b c -> (a b c)").unsqueeze(0).to_broadcast([P, 2 * 4 * HD]))\
                .then_inc(s_misc, 16)
            act.dma_start(sink[:, :], io["sw_sinks"].to_broadcast([P, 16])).then_inc(s_misc, 16)
            act.dma_start(poolw[:, :, :], io["pool_w_2"][0].rearrange("g c d -> c g d")).then_inc(s_misc, 16)

            def split(a, s=0):
                if a >= NBLOCKS:
                    return
                act.wait_ge(raw_ready[a % RING], 16 * (a // RING + 1) + 16 * s)
                if a >= RING:
                    act.wait_ge(blocks_done, a - RING + 1 + RING * s)
                act.activation(w_hi[:, a % RING, :], raw[:, a % RING, :], ACT.Copy).then_inc(hi_ready, 1)

            def root(ph, si, n=D, mul=1.0):
                act.wait_ge(ss_done, si + 1)
                if si >= 1:
                    act.wait_ge(r_ready, si)
                act.activation(sd[:, :], DB[3][:, 0:T], ACT.Sqrt, scale=mul / n, bias=eps_ap(mul))\
                    .then_inc(sd_ready, 1)

            def eps_ap(mul):
                return eps_t[:, (0 if mul == 1.0 else 1):(1 if mul == 1.0 else 2)]

            split(0), split(1)
            act.wait_ge(s_lam, 1)
            act.activation(lam_s[:, :], lam_s[:, :], ACT.Exp).then_inc(s_lam, 1)
            for ph in phases:
                kind = ph["kind"]
                if kind == "prep":
                    src = x if ph["src"] == "x" else y
                    if ph["src"] == "mem":
                        act.wait_ge(s_mem_ok, 4)
                    for c in range(KC):
                        if ph["src"] == "x":
                            act.wait_ge(x_ready, ph["x"] - 4 + c // 2 + 1)
                        if c == 0 and ph["stat"] == 0:
                            act.wait_ge(s_gain, 1)
                        act.activation(a_hi[ph["act"]][:, c, :], src[:, c, :], ACT.Copy,
                                       scale=gains[:, c, ph["gain"]:ph["gain"] + 1]).then_inc(act_hi[ph["act"]], 1)
                    act.activation(sq[:, :, :], src[:, :, :], ACT.Square).then_inc(sq_ready, 1)
                elif kind == "post":
                    if ph["src"] == "y":
                        act.wait_ge(y_ready, ph["y"])
                        act.activation(sq[:, :, :], y[:, :, :], ACT.Square).then_inc(sq_ready, 1)
                    else:
                        act.wait_ge(x_ready, ph["x"])
                        act.activation(sq[:, :, :], x[:, :, :], ACT.Square).then_inc(sq_ready, 1)
                    w = ph["weight"] or 1.0
                    root(ph, ph["stat"], mul=w ** -2)
                elif kind == "lin":
                    for i in range(len(ph["blocks"])):
                        b = ph["n"] + i
                        if i == 0:
                            split(b + 2)
                        if i < len(ph["blocks"]) - 1:
                            split(b + 3)
                        if i == 0 and ph["stat"] is not None:
                            root(ph, ph["stat"])
                elif kind == "soft":
                    softmax_act(act, ph)
                elif kind == "stick":
                    stick_act(act, ph)
                elif kind == "ffn":
                    def up(s0, s, ph=ph):
                        b = up_block(ph, s0, 0)
                        if s0 == 0:
                            split(b + 2)
                        split(b + 3, s)
                        if s0 == 0:
                            root(ph, ph["stat"])
                        split(b + 4, s)
                        n = cols(ph, s0)
                        if ph["conv"] is not None:
                            for c in range(2):
                                u = ph["u"] + 2 * s0 + c
                                f = ph["f"] + 2 * s0 + c
                                act.wait_ge(u_free, u + 1 + 2 * s)
                                if f >= 2:
                                    act.wait_ge(hid_ready, f - 1 + 2 * s)
                                for h in range(2):
                                    at = (2 * s0 + c) * 32
                                    rw, rb = (ph["conv"] * 3 + 2) * 2 + h, 24 + ph["conv"] * 2 + h
                                    act.activation(acc[0:n, c, h, :], us[0:n, c, h, :], ACT.Identity,
                                                   scale=cw[0:n, bass.ds(at + rw + 64 * s, 1)],
                                                   bias=cw[0:n, bass.ds(at + rb + 64 * s, 1)]).then_inc(conv_acc, 1)
                        for c in range(2):
                            f = ph["f"] + 2 * s0 + c
                            if ph["conv"] is not None:
                                act.wait_ge(conv_t0, 2 * f + 1 + 4 * s)
                                src = acc[0:n, c, 0, :]
                            else:
                                act.wait_ge(u_free, ph["u"] + 2 * s0 + c + 1 + 2 * s)
                                act.wait_ge(hid_ready, f - 1 + 2 * s)
                                src = us[0:n, c, 0, :]
                            act.activation(sil[0:n, c, :], src, ACT.Silu).then_inc(sil_ready, 1)
                        for c in range(2):
                            if c == 0 and s0 >= 1:
                                act.wait_ge(blocks_done, ph["n"] + 3 * s0 - 1 + 3 * s)
                            act.wait_ge(hid_ready, ph["f"] + 2 * s0 + c + 1 + 2 * s)
                            act.activation(hh[0:n, 2 * (s0 % 2) + c, :], hid[0:n, c, :], ACT.Copy).then_inc(hh_ready, 1)

                    def down(s0, s, ph=ph):
                        if s0 < NSTEP - 1:
                            split(down_block(ph, s0) + 3, s)

                    ffn_steps(act, up, down)

        @block.tensor
        def _(pe):
            def product(o, hi1, lo1, hi2, lo2, start, stop):
                pe.matmul(o, hi1, hi2, start=start, stop=False, skip_group_check=True)
                pe.matmul(o, hi1, lo2, start=False, stop=False, skip_group_check=True)
                return pe.matmul(o, lo1, hi2, start=False, stop=stop, skip_group_check=True)

            def weights(a, k):
                s = a % RING
                return (w_hi[:, s, :].rearrange("p (k n) -> p k n", k=k), w_lo[:, s, :].rearrange("p (k n) -> p k n", k=k))

            def square_total(si):
                pe.wait_ge(sq_sum, si + 1)
                pe.matmul(DB[3][:, 0:T], ones[:, :], sq[:, 0, :], start=True, stop=True, skip_group_check=True)\
                    .then_inc(ss_done, 1)

            def linear(ph):
                a = ph["act"]
                ah, al = a_hi[a], a_lo[a]
                turned = False
                for i, (typ, _, _, _) in enumerate(ph["blocks"]):
                    counted = typ not in ("proj", "y")
                    b, u = ph["n"] + i, ph["u"] + i if counted else i
                    wait_block(pe, b)
                    if counted and u >= 4:
                        pe.wait_ge(u_free, u - 3)
                    elif i == 0:
                        pe.wait_ge(act_lo[a], 8 * (ph["fill"] + 1))
                    if typ == "v" and not turned:
                        turned = True
                        pe.wait_ge(r_ready, ph["stat"] + 1)
                        for q in range(QB):
                            ins = pe.matmul(DB[3][:, T + q:T + q + 1], r_all[0:1, ph["r"], q * P:(q + 1) * P],
                                            ones[0:1, 0:1], start=True, stop=True, skip_group_check=True)
                        ins.then_inc(rT_done, 1)
                    wh, wl = weights(b, KC)
                    o = UB[u % 4]
                    for j in range(2):
                        for k in range(KC):
                            if i == 0 and j == 0:
                                pe.wait_ge(act_hi[a], 8 * ph["fill"] + k + 1)
                                pe.wait_ge(act_lo[a], 8 * ph["fill"] + k + 1)
                            oj = o[:, j * T:(j + 1) * T]
                            if typ == "v":
                                ts = slice(j * P, (j + 1) * P)
                                ins = product(oj, ah[:, k, ts], al[:, k, ts], wh[:, k, :], wl[:, k, :], k == 0, k == KC - 1)
                            else:
                                cs = slice(j * P, (j + 1) * P)
                                ins = product(oj, wh[:, k, cs], wl[:, k, cs], ah[:, k, :], al[:, k, :], k == 0, k == KC - 1)
                    ins.then_inc(blocks_done, 1)
                    if i == 0 and ph["stat"] is not None:
                        square_total(ph["stat"])

            def ffn(ph):
                a = ph["act"]

                def up(s0, s):
                    n = cols(ph, s0)
                    for part in range(2):
                        b = up_block(ph, s0, part)
                        wait_block(pe, b, s)
                        wh, wl = weights(b, KC)
                        for c in range(2):
                            u = ph["u"] + 2 * s0 + c
                            if part == 0:
                                pe.wait_ge(u_free, u - 3 + 2 * s)
                            o = UB[u % 4][:, part * T:(part + 1) * T]
                            cs = slice(c * n, c * n + P)
                            for k in range(KC):
                                if s0 == 0 and part == 0 and c == 0:
                                    pe.wait_ge(act_hi[a], 8 * ph["fill"] + k + 1)
                                    pe.wait_ge(act_lo[a], 8 * ph["fill"] + k + 1)
                                ins = product(o, wh[:, k, cs], wl[:, k, cs], a_hi[a][:, k, :], a_lo[a][:, k, :],
                                              k == 0 and part == 0, k == KC - 1)
                            if part == 1 and c == 0:
                                ins.then_inc(half_done, 1)
                        ins.then_inc(blocks_done, 1)
                        if s0 == 0 and part == 0:
                            square_total(ph["stat"])

                def down(s0, s):
                    n = cols(ph, s0)
                    b = down_block(ph, s0)
                    wait_block(pe, b, s)
                    wh, wl = weights(b, 2)
                    for k in range(2):
                        f = ph["f"] + 2 * s0 + k
                        at = 2 * (s0 % 2) + k
                        pe.wait_ge(hl_ready, f + 1 + 2 * s)
                        for m in range(KC):
                            first = first_down and s0 == 0 and k == 0 and m % 2 == 0
                            ins = product(DB[m // 2][:, (m % 2) * T:(m % 2 + 1) * T], wh[0:n, k, m * P:(m + 1) * P],
                                          wl[0:n, k, m * P:(m + 1) * P], hh[0:n, at, :], hl[0:n, at, :], first,
                                          s0 == NSTEP - 1 and k == 1)
                    ins.then_inc(blocks_done, 1)

                first_down = True
                up(0, 0)
                up(1, 0)
                down(0, 0)
                first_down = False
                with pe.Fori(0, NLOOP) as i:
                    for d in range(2):
                        up(d + 2, 2 * i)
                        down(d + 1, 2 * i)
                for st in range(2 * NLOOP + 1, NSTEP - 1):
                    up(st + 1, 0)
                    down(st, 0)
                down(NSTEP - 1, 0)

            def score_operands(ph, m, kk=0):
                if ph.get("cross"):
                    return qT[:, 2 * m + kk, :], kT[:, 2 * m + kk, :]
                ps = slice((m % 2) * HD, (m % 2 + 1) * HD)
                return qT[ps, m // 2, :], kT[ps, m // 4 if ph.get("sink") else m // 2, :]

            def softmax(ph):
                G = ph["heads"] // 2
                cross, diff = ph.get("cross"), ph.get("diff") is not None
                a = ph["act"]

                def scores(g):
                    if g == 0:
                        pe.wait_ge(u_free, ph["u"])
                    if g >= 2:
                        pe.wait_ge(biased, ph["sg"] + g - 1)
                    for s in range(2):
                        o = DB[2 * (g % 2) + s]
                        if cross:
                            for qb in range(QB):
                                for kk in range(2):
                                    q, k = score_operands(ph, 2 * g + s, kk)
                                    ins = pe.matmul(o[:, qb * T:(qb + 1) * T], q[:, qb * P:(qb + 1) * P], k,
                                                    start=kk == 0, stop=kk == 1, skip_group_check=True)
                        else:
                            q, k = score_operands(ph, 2 * g + s)
                            pe.matmul(o[:, 0:P], q[:, 0:P], k[:, 0:P], start=True, stop=True, skip_group_check=True)
                            ins = pe.matmul(o[:, P:3 * P], q[:, P:T], k[:, 0:T], start=True, stop=True,
                                            skip_group_check=True)
                    ins.then_inc(scores_ready, 1)

                def turn(g):
                    pe.wait_ge(diag_ready, ph["sg"] + g + 1)
                    if g >= 1:
                        pe.wait_ge(pt_ready, ph["sg"] + g)
                    parts = [(0, 0), (2, 1), (1, 0), (3, 1)] if cross else [(0, 0), (1, 1), (2, 1)]
                    for n, (c, qb) in enumerate(parts):
                        for s in range(2):
                            o = UB[0 if diff else s][:, n * P:(n + 1) * P]
                            ins = pe.matmul(o, prob[:, g % 2, s, c * P:(c + 1) * P], diag[:, g % 2, 2 * qb + s, :],
                                            start=not (diff and s), stop=not diff or s == 1, skip_group_check=True)
                    ins.then_inc(pt_done, 1)

                def values(g):
                    pe.wait_ge(pt_ready, ph["sg"] + g + 1)
                    if diff:
                        if g >= 2:
                            pe.wait_ge(y_ready, ph["y"] + g - 1)
                    elif cross:
                        if g >= 1:
                            pe.wait_ge(act_lo[a], 8 * ph["fill"] + 4 * g)
                    elif g >= 2:
                        pe.wait_ge(act_lo[a], 8 * ph["fill"] + g - 1)
                    for s in range(1 if diff else 2):
                        m = 2 * g + s
                        pT = probT[:, g % 2, s, :]
                        if cross:
                            for e in range(2):
                                o = UB[2 + s][:, e * T:(e + 1) * T]
                                for kb in range(2):
                                    c0 = m * T + e * P
                                    ins = pe.matmul(o, v[:, kb, c0:c0 + P], pT[:, kb * T:(kb + 1) * T], start=kb == 0,
                                                    stop=kb == 1, skip_group_check=True)
                        else:
                            w = P if diff else HD
                            c0 = g * P if diff else (m // 4 if ph.get("sink") else m) * HD
                            o = UB[2 + g % 2][s * HD:s * HD + w, 0:T]
                            pe.matmul(o, v[:, 0, c0:c0 + w], pT[:, 0:T], start=True, stop=False, skip_group_check=True)
                            ins = pe.matmul(o[:, P:T], v[:, 1, c0:c0 + w], pT[:, T:T + P], start=False, stop=True,
                                            skip_group_check=True)
                    ins.then_inc(pv_done, 1)

                for g in range(G + 2):
                    if g < G:
                        scores(g)
                    if 1 <= g <= G:
                        turn(g - 1)
                    if g >= 2:
                        values(g - 2)
                if diff:
                    for i in range(4):
                        pe.wait_ge(sub_sq, 4 * ph["diff"] + i + 1)
                        pe.matmul(DB[i], ones[:, :], sq[:, 2 * i:2 * i + 2, :].rearrange("p a b -> p (a b)"),
                                  start=True, stop=True, skip_group_check=True).then_inc(sub_ss, 1)
                if ph.get("moba"):
                    pe.wait_ge(win_ok, 4)
                    pe.wait_ge(s_misc, 48)
                    pe.wait_ge(biased, ph["sg"] + G)
                    for g in range(4):
                        src = (win_a, win_b)[g % 2][:, g, :]
                        ins = pe.matmul(DB[g // 2][:, (g % 2) * T:(g % 2 + 1) * T], poolw[:, g, :], src, start=g % 2 == 0,
                                        stop=True, skip_group_check=True)
                    ins.then_inc(poolmix_done, 1)

            def stick(ph):
                a = ph["act"]
                for half in range(2):
                    k0 = ph["kg"] + 4 * half

                    def zT(g):
                        if g == 0 and half == 0:
                            pe.wait_ge(u_free, ph["u"])
                        if g >= 2:
                            pe.wait_ge(t_exp, k0 + g - 1)
                        elif half:
                            pe.wait_ge(z_less, k0)
                        for s in range(2):
                            m = 8 * half + 2 * g + s
                            q, k = score_operands(ph, m)
                            o = DB[2 * (g % 2) + s]
                            pe.matmul(o[:, 0:T], k[:, 0:P], q, start=True, stop=True, skip_group_check=True)
                            ins = pe.matmul(o[:, T:3 * P], k[:, P:T], q[:, P:T], start=True, stop=True,
                                            skip_group_check=True)
                        ins.then_inc(z_done, 1)

                    def suffix(g):
                        pe.wait_ge(sp_ready, k0 + g + 1)
                        if g < 2:
                            pe.wait_ge(t_exp, k0 + 4)
                        else:
                            pe.wait_ge(z_less, k0 + g - 1)
                        for s in range(2):
                            t = tbuf[:, 2 * g + s, :]
                            o = DB[2 * (g % 2) + s]
                            pe.matmul(o[:, 0:T], upper[:, :], t[:, 0:T], start=True, stop=False, skip_group_check=True)
                            pe.matmul(o[:, P:T], ones[:, :], t[:, T:3 * P], start=False, stop=True, skip_group_check=True)
                            ins = pe.matmul(o[:, T:3 * P], upper[:, :], t[:, T:3 * P], start=False, stop=True,
                                            skip_group_check=True)
                        ins.then_inc(cs_done, 1)

                    def values(g):
                        pe.wait_ge(a_ready, k0 + g + 1)
                        if half:
                            pe.wait_ge(act_lo[a], 8 * ph["fill"] + g + 1)
                        for s in range(2):
                            m = 8 * half + 2 * g + s
                            z = zbuf[:, 2 * g + s, :]
                            o = UB[g][s * HD:(s + 1) * HD, 0:T]
                            pe.matmul(o, v[:, 0, m * HD:(m + 1) * HD], z[:, 0:T], start=True, stop=False,
                                      skip_group_check=True)
                            ins = pe.matmul(o[:, P:T], v[:, 1, m * HD:(m + 1) * HD], z[:, T:3 * P], start=False, stop=True,
                                            skip_group_check=True)
                        ins.then_inc(spv_done, 1)

                    for g in range(4):
                        zT(g)
                    for g in range(4):
                        suffix(g)
                    for g in range(4):
                        values(g)

            pe.wait_ge(s_const, 3)
            pe.wait_ge(s_xin, 16)
            for c in range(KC):
                for q in range(QB):
                    ins = pe.transpose(DB[c // 2][:, (c % 2) * T + q * P:(c % 2) * T + (q + 1) * P],
                                       x_rows[:, q, c * P:(c + 1) * P], ident[:, :])
                if c % 2:
                    ins.then_inc(s_setup_pe, 1)
            pe.wait_ge(s_gin, 16 * 14)
            for c in range(KC):
                ins = pe.transpose(UB[0][:, c * NG:(c + 1) * NG], gain_rows[:, c * P:(c + 1) * P], ident[0:NG, 0:NG])
            ins.then_inc(s_setup_pe, 1)
            pe.wait_ge(s_tab_in, 32)
            pe.matmul(UB[1][0:16, 0:TW], kT[0:N_BUCKETS, 0, 0:16],
                      kT[0:N_BUCKETS, 2:4, :].rearrange("p a b -> p (a b)")[:, 0:TW], start=True, stop=True,
                      skip_group_check=True).then_inc(s_setup_pe, 1)
            pe.wait_ge(s_cin, 32)
            last = (F1 - (NSTEP - 1) * 2 * P) // 2
            for j in range(NCH):
                at = j * P if j < NCH - 1 else (NCH - 2) * P + last
                ins = pe.transpose(UB[2 + j // NSTEP][:, (j % NSTEP) * 32:(j % NSTEP) * 32 + 32],
                                   conv_rows[:, at:at + P], ident[0:32, 0:32])
            ins.then_inc(s_setup_pe, 1)
            pe.wait_ge(s_conv, 1)
            for ph in phases:
                if ph["kind"] == "lin":
                    linear(ph)
                elif ph["kind"] == "ffn":
                    ffn(ph)
                elif ph["kind"] == "soft":
                    softmax(ph)
                elif ph["kind"] == "stick":
                    stick(ph)
                elif ph["kind"] == "post":
                    square_total(ph["stat"])
                elif ph["kind"] == "prep" and ph["src"] == "mem":
                    pe.wait_ge(s_mem_in, 16)
                    pe.wait_ge(x_ready, ph["x"])
                    for c in range(KC):
                        for q in range(QB):
                            ins = pe.transpose(DB[c // 2][:, (c % 2) * T + q * P:(c % 2) * T + (q + 1) * P],
                                               x_rows[:, q, c * P:(c + 1) * P], ident[:, :])
                        if c % 2:
                            ins.then_inc(s_memT, 1)
            pe.wait_ge(x_ready, total["x"])
            for c in range(KC):
                for q in range(QB):
                    at = q * D + c * P
                    ins = pe.transpose(DB[at // 512][:, at % 512:at % 512 + P], x[:, c, q * P:(q + 1) * P], ident[:, :])
            ins.then_inc(s_outT, 1)

        @block.vector
        def _(dve):
            links = [0]

            def link(ins):
                links[0] += 1
                ins.then_inc(dve_link, 1)
                dve.wait_ge(dve_link, links[0])

            def split(a, s=0):
                if a % RING != 2 and a < NBLOCKS:
                    dve.wait_ge(hi_ready, a + 1 + RING * s)
                    dve.tensor_tensor(w_lo[:, a % RING, :], raw[:, a % RING, :], w_hi[:, a % RING, :].bitcast(F32),
                                      ALU.subtract).then_inc(lo_dve, 1)

            def invert(si, r):
                dve.wait_ge(sd_ready, si + 1)
                dve.reciprocal(r_all[:, r, :], sd[:, :]).then_inc(r_ready, 1)
                dve.wait_ge(r_ready, si + 1)

            def pairs(ap):
                return ap.rearrange("p (c t) -> p c t", c=2)

            def linear(ph):
                turned = False
                for i, (typ, _, _, j) in enumerate(ph["blocks"]):
                    b, u = ph["n"] + i, i if typ in ("proj", "y") else ph["u"] + i
                    if i == 0:
                        split(b + 2)
                    if i < len(ph["blocks"]) - 1:
                        split(b + 3)
                    if i == 0 and ph["stat"] is not None:
                        invert(ph["stat"], ph["r"])
                    if typ == "v" and not turned:
                        turned = True
                        if ph["n"] == 0:
                            dve.wait_ge(s_tab_out, 16)
                        dve.wait_ge(rT_done, rT_count[ph["n"]])
                        dve.tensor_copy(rT[:, :], DB[3][:, T:T + QB]).then_inc(rT_ready, 1)
                        dve.wait_ge(rT_ready, rT_count[ph["n"]])
                    dve.wait_ge(blocks_done, b + 1)
                    o = UB[u % 4]
                    r = r_all[:, ph["r"], :]
                    if typ in ("q", "k", "pool"):
                        dst = {"q": qT, "k": kT, "pool": pin}[typ][:, 2 * j:2 * j + 2, :]
                        dve.tensor_tensor(dst, pairs(o), both(r), ALU.mult).then_inc(u_free, 1)
                    elif typ == "kdup":
                        for g in range(4):
                            for h in range(2):
                                ins = dve.tensor_tensor(kT[h * HD:(h + 1) * HD, g, :],
                                                        o[(g % 2) * HD:(g % 2 + 1) * HD, (g // 2) * T:(g // 2 + 1) * T],
                                                        r[h * HD:(h + 1) * HD, :], ALU.mult)
                        ins.then_inc(u_free, 1)
                    elif typ == "v":
                        for q in range(QB):
                            ins = dve.tensor_scalar(v[:, q, j * BW:(j + 1) * BW], o[:, q * T:(q + 1) * T], rT[:, q:q + 1],
                                                    None, ALU.mult)
                        ins.then_inc(u_free, 1)
                    elif typ == "proj":
                        xs = x[:, 2 * j:2 * j + 2, :]
                        dve.tensor_tensor(xs, pairs(o), xs, ALU.add).then_inc(x_ready, 1)
                    elif typ == "y":
                        dve.tensor_copy(y[:, 2 * j:2 * j + 2, :], pairs(o)).then_inc(y_ready, 1)

            def prep(ph):
                a = ph["act"]
                src = x if ph["src"] == "x" else y
                if ph["src"] == "mem":
                    for i in range(4):
                        dve.wait_ge(s_memT, i + 1)
                        dve.tensor_copy(y[:, 2 * i:2 * i + 2, :], pairs(DB[i])).then_inc(s_mem_ok, 1)
                for c in range(KC):
                    dve.wait_ge(act_hi[a], 8 * ph["fill"] + c + 1)
                    dve.scalar_tensor_tensor(out=a_lo[a][:, c, :], in0=src[:, c, :],
                                             scalar=gains[:, c, ph["gain"]:ph["gain"] + 1],
                                             in1=a_hi[a][:, c, :].bitcast(F32), op0=ALU.mult, op1=ALU.subtract)\
                        .then_inc(act_lo[a], 1)

            def post(ph):
                invert(ph["stat"], 0)
                r = r_all[:, 0, :]
                for c in range(KC):
                    g = gains[:, c, ph["gain"]:ph["gain"] + 1]
                    if ph["src"] == "x":
                        ins = dve.scalar_tensor_tensor(out=x[:, c, :], in0=x[:, c, :], scalar=g, in1=r, op0=ALU.mult,
                                                       op1=ALU.mult)
                    else:
                        link(dve.scalar_tensor_tensor(out=y[:, c, :], in0=y[:, c, :], scalar=g, in1=r, op0=ALU.mult,
                                                      op1=ALU.mult))
                        ins = dve.tensor_tensor(x[:, c, :], x[:, c, :], y[:, c, :], ALU.add)
                    if c % 2:
                        ins.then_inc(x_ready, 1)

            def ffn(ph):
                def up(s0, s):
                    b = up_block(ph, s0, 0)
                    if s0 == 0:
                        split(b + 2)
                    split(b + 3, s)
                    if s0 == 0:
                        invert(ph["stat"], 0)
                    split(b + 4, s)
                    n = cols(ph, s0)
                    for c in range(2):
                        f, u = ph["f"] + 2 * s0 + c, ph["u"] + 2 * s0 + c
                        if c == 0:
                            dve.wait_ge(half_done, ph["hd"] + s0 + 1 + s)
                        else:
                            dve.wait_ge(blocks_done, b + 2 + 3 * s)
                        if f >= 2:
                            dve.wait_ge(hid_ready, f - 1 + 2 * s)
                        dve.tensor_tensor(us[0:n, c, :, :], pairs(UB[u % 4])[0:n], both(r_all[0:n, 0, :]), ALU.mult)\
                            .then_inc(u_free, 1)
                    if ph["conv"] is not None:
                        for c in range(2):
                            f = ph["f"] + 2 * s0 + c
                            at = (2 * s0 + c) * 32
                            for tap, done in ((1, conv_t1), (0, conv_t0)):
                                sh = 2 - tap
                                for h in range(2):
                                    dve.wait_ge(conv_acc if tap else conv_t1, 2 * f + h + 1 + 4 * s)
                                    rw = (ph["conv"] * 3 + tap) * 2 + h
                                    dve.scalar_tensor_tensor(
                                        out=acc[0:n, c, h, sh:T], in0=us[0:n, c, h, 0:T - sh],
                                        scalar=cw[0:n, bass.ds(at + rw + 64 * s, 1)], in1=acc[0:n, c, h, sh:T],
                                        op0=ALU.mult, op1=ALU.add).then_inc(done, 1)
                    for c in range(2):
                        f = ph["f"] + 2 * s0 + c
                        if ph["conv"] is not None:
                            dve.wait_ge(conv_t0, 2 * f + 2 + 4 * s)
                        dve.wait_ge(sil_ready, f + 1 + 2 * s)
                        if f >= 2:
                            dve.wait_ge(hl_ready, f - 1 + 2 * s)
                        val = acc[0:n, c, 1, :] if ph["conv"] is not None else us[0:n, c, 1, :]
                        dve.tensor_tensor(hid[0:n, c, :], sil[0:n, c, :], val, ALU.mult).then_inc(hid_ready, 1)

                def down(s0, s):
                    if s0 < NSTEP - 1:
                        split(down_block(ph, s0) + 3, s)

                ffn_steps(dve, up, down)
                dve.wait_ge(blocks_done, ph["n"] + 3 * NSTEP)
                for i in range(4):
                    if ph["dst"] == "x":
                        xs = x[:, 2 * i:2 * i + 2, :]
                        dve.tensor_tensor(xs, pairs(DB[i]), xs, ALU.add).then_inc(x_ready, 1)
                    else:
                        dve.tensor_copy(y[:, 2 * i:2 * i + 2, :], pairs(DB[i])).then_inc(y_ready, 1)

            def softmax(ph):
                G = ph["heads"] // 2
                a = ph["act"]
                cross, moba = ph.get("cross"), ph.get("moba")
                W = 2 * T if cross else 3 * P
                A = T if cross else P

                def maxima(g):
                    sg = ph["sg"] + g
                    dve.wait_ge(scores_ready, sg + 1)
                    if g >= 2:
                        dve.wait_ge(pt_done, sg - 1)
                    S = PS[:, 2 * (g % 2):2 * (g % 2) + 2, 0:W]
                    p = prob[:, g % 2, :, 0:W]
                    if cross:
                        dve.tensor_scalar(p, S, ph["scale"], None, ALU.mult).then_inc(biased, 1)
                    else:
                        tab = bias[:, 2 * g:2 * g + 2, :]
                        dve.scalar_tensor_tensor(out=p[:, :, 0:P], in0=S[:, :, 0:P], scalar=ph["scale"],
                                                 in1=tab[:, :, P:T], op0=ALU.mult, op1=ALU.add)
                        dve.scalar_tensor_tensor(out=p[:, :, P:W], in0=S[:, :, P:W], scalar=ph["scale"],
                                                 in1=tab, op0=ALU.mult, op1=ALU.add).then_inc(biased, 1)
                    dve.wait_ge(biased, sg + 1)
                    small = sm_small[:, g % 2]
                    dve.tensor_reduce(small[:, 0, 0:2], p[:, :, 0:A], AX_X, ALU.max)
                    link(dve.tensor_reduce(small[:, 0, 2:4], p[:, :, A:W], AX_X, ALU.max))
                    if ph.get("sink"):
                        sk = both(sink[:, 2 * g:2 * g + 2])
                        mx = small[:, 0, :].rearrange("p (a b) -> p a b", a=2)
                        link(dve.tensor_tensor(mx, mx, sk, ALU.max))
                        dve.tensor_tensor(small[:, 4, :].rearrange("p (a b) -> p a b", a=2), sk, mx, ALU.subtract)
                    dve.tensor_scalar(small[:, 1, :], small[:, 0, :], -1.0, None, ALU.mult).then_inc(negmax, 1)

                def sums(g):
                    sg = ph["sg"] + g
                    dve.wait_ge(exp_ready, sg + 1)
                    if g >= 2:
                        dve.wait_ge(diag_ready, sg - 1)
                    small = sm_small[:, g % 2]
                    if ph.get("sink"):
                        link(dve.tensor_tensor(small[:, 2, :], small[:, 2, :], small[:, 4, :], ALU.add))
                    if ph.get("diff") is not None:
                        link(dve.reciprocal(small[:, 3, :], small[:, 2, :]))
                        dve.tensor_tensor(small[:, 3, :], small[:, 3, :], lam_fac[:, ph["diff"], :], ALU.mult)\
                            .then_inc(rs_ready, 1)
                    else:
                        dve.reciprocal(small[:, 3, :], small[:, 2, :]).then_inc(rs_ready, 1)

                def out_lo(g):
                    if cross:
                        for i in range(4):
                            c = 4 * g + i
                            dve.wait_ge(act_hi[a], 8 * ph["fill"] + c - c % 2 + 2)
                            dve.tensor_tensor(a_lo[a][:, c, :], UB[2 + i // 2][:, (i % 2) * T:(i % 2 + 1) * T],
                                              a_hi[a][:, c, :].bitcast(F32), ALU.subtract).then_inc(act_lo[a], 1)
                    elif ph.get("diff") is None:
                        dve.wait_ge(act_hi[a], 8 * ph["fill"] + g + 1)
                        dve.tensor_tensor(a_lo[a][:, g, :], UB[2 + g % 2][:, 0:T], a_hi[a][:, g, :].bitcast(F32),
                                          ALU.subtract).then_inc(act_lo[a], 1)

                if moba:
                    windows()
                if not cross:
                    dve.wait_ge(s_bias_ok, ok_count[ph["sg"]])
                for g in range(G + 2):
                    if g < G:
                        maxima(g)
                    if 1 <= g <= G:
                        sums(g - 1)
                    if g >= 2:
                        out_lo(g - 2)
                if ph.get("diff") is not None:
                    j = ph["diff"]
                    for i in range(4):
                        c = slice(2 * i, 2 * i + 2)
                        dve.wait_ge(sub_sd, 4 * j + i + 1)
                        link(dve.reciprocal(kT[:, c, :], kT[:, c, :]))
                        dve.scalar_tensor_tensor(out=y[:, c, :], in0=y[:, c, :],
                                                 scalar=gains[:, 0, G_SUBLN + j:G_SUBLN + j + 1], in1=kT[:, c, :],
                                                 op0=ALU.mult, op1=ALU.mult).then_inc(sub_t, 1)
                    for i in range(4):
                        c = slice(2 * i, 2 * i + 2)
                        dve.wait_ge(act_hi[a], 8 * ph["fill"] + 2 * i + 2)
                        dve.scalar_tensor_tensor(out=a_lo[a][:, c, :], in0=y[:, c, :],
                                                 scalar=1.0 - lambda_init(ph["layer"]),
                                                 in1=a_hi[a][:, c, :].bitcast(F32), op0=ALU.mult, op1=ALU.subtract)\
                            .then_inc(act_lo[a], 2)
                if moba:
                    for g in range(4):
                        dve.wait_ge(act_hi[a], 8 * ph["fill"] + 4 + 2 * (g // 2) + 2)
                        dve.scalar_tensor_tensor(out=a_lo[a][:, 4 + g, :], in0=DB[g // 2][:, (g % 2) * T:(g % 2 + 1) * T],
                                                 scalar=gains[:, g, G_POOL:G_POOL + 1],
                                                 in1=a_hi[a][:, 4 + g, :].bitcast(F32), op0=ALU.mult, op1=ALU.subtract)\
                            .then_inc(act_lo[a], 1)

            def windows():
                dve.wait_ge(s_bias_ok, ok_count["cnt"])
                link(dve.reciprocal(inv_cnt, inv_cnt))
                src = pin
                for i in range(4):
                    dst, sh = (win_a, win_b)[i % 2], 1 << i
                    g = slice(i, 4)
                    dve.tensor_copy(dst[:, g, 0:sh], src[:, g, 0:sh])
                    link(dve.tensor_tensor(dst[:, g, sh:T], src[:, g, sh:T], src[:, g, 0:T - sh], ALU.add))
                    src = dst
                for g in range(4):
                    w = (win_a, win_b)[g % 2][:, g, :]
                    link(dve.tensor_tensor(w, w, inv_cnt[:, g, :], ALU.mult))
                    dve.tensor_tensor(w, w, pin[:, g, :], ALU.subtract).then_inc(win_ok, 1)

            def stick(ph):
                a = ph["act"]
                for half in range(2):
                    k0 = ph["kg"] + 4 * half
                    for g in range(4):
                        dve.wait_ge(z_done, k0 + g + 1)
                        if half:
                            dve.wait_ge(spv_done, k0)
                        dve.tensor_scalar(zbuf[:, 2 * g:2 * g + 2, :], PS[:, 2 * (g % 2):2 * (g % 2) + 2, 0:3 * P],
                                          ph["scale"], None, ALU.mult).then_inc(z_copied, 1)
                    for g in range(4):
                        z, t = zbuf[:, 2 * g:2 * g + 2, :], tbuf[:, 2 * g:2 * g + 2, :]
                        dve.wait_ge(t_ln, k0 + g + 1)
                        dve.wait_ge(z_copied, k0 + g + 1)
                        dve.scalar_tensor_tensor(out=t, in0=z, scalar=0.0, in1=t, op0=ALU.max, op1=ALU.add)\
                            .then_inc(sp_sum, 1)
                    for g in range(4):
                        z = zbuf[:, 2 * g:2 * g + 2, :]
                        dve.wait_ge(cs_done, k0 + g + 1)
                        dve.tensor_tensor(z, z, PS[:, 2 * (g % 2):2 * (g % 2) + 2, 0:3 * P], ALU.subtract)\
                            .then_inc(z_less, 1)
                    for g in range(4):
                        c = 4 * half + g
                        dve.wait_ge(act_hi[a], 8 * ph["fill"] + c + 1)
                        dve.tensor_tensor(a_lo[a][:, c, :], UB[g][:, 0:T], a_hi[a][:, c, :].bitcast(F32), ALU.subtract)\
                            .then_inc(act_lo[a], 1)

            dve.memset(eps_t[:, 0:1], EPS)
            dve.memset(eps_t[:, 1:2], EPS * MACARON ** -2)
            for i in range(4):
                dve.wait_ge(s_setup_pe, i + 1)
                dve.tensor_copy(x[:, 2 * i:2 * i + 2, :], pairs(DB[i])).then_inc(x_ready, 1)
            dve.wait_ge(s_setup_pe, 5)
            dve.tensor_copy(gains[:, :, :].rearrange("p c g -> p (c g)"), UB[0][:, 0:KC * NG]).then_inc(s_gain, 1)
            dve.wait_ge(s_setup_pe, 6)
            dve.tensor_copy(table_sb, UB[1][0:16, 0:TW]).then_inc(s_tab, 1)
            dve.wait_ge(s_setup_pe, 7)
            dve.tensor_copy(cw[:, :].rearrange("p (a b) -> p a b", a=2), PS[:, 6:8, 0:NSTEP * 32]).then_inc(s_conv, 1)
            dve.wait_ge(s_misc, 48)
            prod = lam[:, :, 0:4:2, :]
            link(dve.tensor_tensor(prod, lam[:, :, 0:4:2, :], lam[:, :, 1:4:2, :], ALU.mult))
            dve.tensor_reduce(lam_s[:, :].rearrange("p (a b) -> p a b", a=2), prod, AX_X, ALU.add).then_inc(s_lam, 1)
            split(0), split(1)
            dve.wait_ge(s_lam, 2)
            dve.wait_ge(s_const, 5)
            for j, l in enumerate((0, 3)):
                e = lam_s[:, 2 * j:2 * j + 2]
                link(dve.tensor_tensor(lam_fac[:, j, 1:2], e[:, 1:2], e[:, 0:1], ALU.subtract))
                for c in (3, 1):
                    link(dve.tensor_scalar(lam_fac[:, j, c:c + 1], lam_fac[:, j, 1:2], -lambda_init(l), None, ALU.add))
            dve.wait_ge(s_gain, 1)

            for ph in phases:
                {"prep": prep, "post": post, "lin": linear, "ffn": ffn, "soft": softmax, "stick": stick}[ph["kind"]](ph)
            for i in range(4):
                dve.wait_ge(s_outT, 1)
                dve.tensor_copy(x_rows.rearrange("p b d -> p (b d)")[:, i * 512:(i + 1) * 512], DB[i]).then_inc(s_outc, 1)


_INS = ["x", "rel_bias", "attn_norm", "ffn_norm", "w_o", "da_w_qkv", "da_lambda", "da_subln", "sb_w_qkv", "sw_w_qkv",
        "sw_sinks", "ffn_w_up", "ffn_conv_w", "ffn_conv_b", "ffn_w_down", "final_norm", "mem_2", "ffn1_pre_g_2",
        "ffn1_w_gate_2", "ffn1_w_up_2", "ffn1_w_down_2", "ffn1_post_g_2", "mix_pre_g_2", "w_in_2", "pool_w_2",
        "pool_scale_2", "w_out_2", "mix_post_g_2", "xa_pre_g_2", "mem_g_2", "xa_wq_2", "xa_wkv_2", "xa_wo_2",
        "xa_post_g_2", "ffn2_pre_g_2", "ffn2_w_gate_2", "ffn2_w_up_2", "ffn2_w_down_2", "ffn2_post_g_2"]


def bucket_of_distance():
    dist = np.maximum(T - 1 - np.arange(TW), 0)
    half = N_BUCKETS // 2
    large = half + (np.log(np.maximum(dist, 1).astype(np.float32) / half) / math.log(MAX_DIST / half)
                    * (N_BUCKETS - half)).astype(np.int32)
    bucket = np.where(dist < half, dist, np.minimum(large, N_BUCKETS - 1))
    return (np.arange(N_BUCKETS)[:, None] == bucket[None, :]).astype(np.float32)


def kernel(**inputs):
    from concourse import bacc
    from concourse.bass_utils import run_bass_kernel_spmd

    nc = bacc.Bacc("TRN2", target_bir_lowering=False, num_devices=1)
    arrays, io = {}, {}
    for name in _INS + ["bucket_of_distance"]:
        a = bucket_of_distance() if name == "bucket_of_distance" else np.ascontiguousarray(inputs[name])
        arrays[f"in_{name}"] = a
        io[name] = nc.dram_tensor(f"in_{name}", a.shape, mybir.dt.from_np(a.dtype), kind="ExternalInput").ap()
    out = nc.dram_tensor("out_0", (1, T, D), F32, kind="ExternalOutput").ap()
    model_kernel(nc, io, out)
    r = run_bass_kernel_spmd(nc, [arrays], core_ids=[0])
    return r.results[0]["out_0"]
```

```python
import math
from contextlib import ExitStack

import numpy as np

import concourse.bass as bass
from concourse import mybir

P = 128
T = 256
D = 1024
KC = D // P
QB = T // P
BW = 256
BE = KC * BW
RING = 3
DEPTH = 4
F1, F2 = 2752, 2816
NSTEP = 11
NLOOP = 4
NCH = 2 * NSTEP
HD = 64
N_BUCKETS, MAX_DIST = 32, 128
NEG = -1e30
EPS = 1e-6
TW = 384
MACARON = 0.5

F32, F32R = mybir.dt.float32, mybir.dt.float32r
ALU, ACT = mybir.AluOpType, mybir.ActivationFunctionType
AX_X = mybir.AxisListType.X

G_ATTN, G_FFN, G_FINAL = 0, 4, 8
(G_FFN1_PRE, G_FFN1_POST, G_MIX_PRE, G_MIX_POST, G_XA_PRE, G_MEM, G_XA_POST, G_FFN2_PRE,
 G_FFN2_POST) = range(9, 18)
G_POOL, G_SUBLN, NG = 18, 19, 21


def lambda_init(layer):
    return 0.8 - 0.6 * math.exp(-0.3 * layer)


def dve_splits(n):
    return 2 * (n // RING) + min(n % RING, 1) + 1


def plan():
    c = dict(n=0, u=0, f=0, stat=0, tree=0, x=4, y=0, hd=0, sg=0, fill=[0, 0], kg=0)
    out = []

    def prep(src, gain, a, r):
        out.append(dict(kind="prep", src=src, gain=gain, act=a, fill=c["fill"][a], stat=c["stat"], tree=c["tree"],
                        x=c["x"], r=r))
        c["fill"][a] += 1
        c["tree"] += 1
        c["stat"] += 1
        return c["stat"] - 1

    def lin(a, blocks, stat=None, r=0, r_of=None):
        out.append(dict(kind="lin", r_of=stat if r_of is None else r_of, act=a, fill=c["fill"][a] - 1, n=c["n"], u=c["u"], blocks=blocks, stat=stat, r=r,
                        x=c["x"], y=c["y"]))
        c["n"] += len(blocks)
        if blocks[0][0] == "proj":
            c["x"] += 4
        elif blocks[0][0] == "y":
            c["y"] += 4
        else:
            c["u"] += len(blocks)

    def attend(kind, a, heads, **kw):
        out.append(dict(kind=kind, act=a, fill=c["fill"][a], sg=c["sg"], kg=c["kg"], u=c["u"], heads=heads, y=c["y"],
                        stat=c["stat"], **kw))
        c["fill"][a] += 1
        if kind == "soft":
            c["sg"] += heads // 2
        if kw.get("diff") is not None:
            c["y"] += 8
        if kind == "stick":
            c["kg"] += heads // 2

    def ffn(F, a, wup, wdown, conv, dst, stat):
        out.append(dict(kind="ffn", F=F, act=a, fill=c["fill"][a] - 1, n=c["n"], u=c["u"], f=c["f"], hd=c["hd"],
                        up=wup, down=wdown, conv=conv, dst=dst, stat=stat, x=c["x"], y=c["y"]))
        c["n"] += 3 * NSTEP
        c["u"] += NCH
        c["f"] += NCH
        c["hd"] += NSTEP
        c[dst] += 4

    def scale_x(src, gain, weight):
        bank = 4 if out[-1]["kind"] == "ffn" else 3
        out.append(dict(kind="post", bank=bank, src=src, gain=gain, weight=weight, stat=c["stat"], x=c["x"], y=c["y"]))
        c["stat"] += 1
        c["x"] += 4

    def qkv(w, nq, nk, nv, k="k"):
        return ([("q", w, i * BW, i) for i in range(nq)] + [(k, w, (nq + i) * BW, i) for i in range(nk)]
                + [("v", w, (nq + nk + i) * BW, i) for i in range(nv)])

    for l in range(DEPTH):
        s = prep("x", G_ATTN + l, 0, 0)
        if l % 3 == 0:
            lin(0, qkv(("da_w_qkv", l // 3), 4, 4, 4), s)
            attend("soft", 1, 16, diff=l // 3, layer=l, scale=HD ** -0.5)
        elif l % 3 == 1:
            lin(0, qkv(("sb_w_qkv", 0), 4, 4, 4), s)
            attend("stick", 1, 16, scale=HD ** -0.5)
        else:
            lin(0, qkv(("sw_w_qkv", 0), 4, 1, 1, "kdup"), s)
            attend("soft", 1, 16, sink=True, scale=HD ** -0.5)
        lin(1, [("proj", ("w_o", l), i * BW, i) for i in range(4)])
        s = prep("x", G_FFN + l, 0, 0)
        ffn(F1, 0, [("ffn_w_up", l, 0), ("ffn_w_up", l, F1)], ("ffn_w_down", l), l, "x", s)
    scale_x("x", G_FINAL, None)

    s = prep("x", G_FFN1_PRE, 0, 0)
    ffn(F2, 0, [("ffn1_w_gate_2", 0, 0), ("ffn1_w_up_2", 0, 0)], ("ffn1_w_down_2", 0), None, "y", s)
    scale_x("y", G_FFN1_POST, MACARON)
    s = prep("x", G_MIX_PRE, 0, 0)
    lin(0, qkv(("w_in_2", 0), 2, 2, 2) + [("pool", ("w_in_2", 0), (6 + i) * BW, i) for i in range(2)], s)
    attend("soft", 1, 8, moba=True, scale=HD ** -0.5)
    lin(1, [("y", ("w_out_2", 0), i * BW, i) for i in range(4)])
    s = prep("mem", G_MEM, 0, 1)
    kv = qkv(("xa_wkv_2", 0), 0, 4, 4)
    lin(0, kv[:2], s, 1)
    scale_x("y", G_MIX_POST, 1.0)
    t = prep("x", G_XA_PRE, 1, 0)
    lin(0, kv[2:], None, 1, s)
    s = t
    lin(1, [("q", ("xa_wq_2", 0), i * BW, i) for i in range(4)], s)
    attend("soft", 0, 4, cross=True, scale=256 ** -0.5)
    lin(0, [("y", ("xa_wo_2", 0), i * BW, i) for i in range(4)])
    scale_x("y", G_XA_POST, 1.0)
    s = prep("x", G_FFN2_PRE, 0, 0)
    ffn(F2, 0, [("ffn2_w_gate_2", 0, 0), ("ffn2_w_up_2", 0, 0)], ("ffn2_w_down_2", 0), None, "y", s)
    scale_x("y", G_FFN2_POST, MACARON)
    for before, ph in zip(out, out[1:]):
        if ph["kind"] == "prep" and ph["src"] == "x":
            ph["fused"] = True
            before["then"] = ph
    return out, c


def model_kernel(nc, io, out):
    phases, total = plan()
    NBLOCKS = total["n"]
    rT_count = {n: i + 1 for i, n in enumerate(ph["n"] for ph in phases
                                               if ph["kind"] == "lin" and any(b[0] == "v" for b in ph["blocks"]))}
    ok_count = {sg: i + 1 for i, sg in enumerate(ph["sg"] for ph in phases if ph["kind"] == "soft" and not ph.get("cross"))}
    ok_count["cnt"] = 5
    tree_of = {ph["stat"]: ph["tree"] for ph in phases if ph["kind"] == "prep"}
    with ExitStack() as ctx:
        def sb(name, shape, dt=F32):
            return ctx.enter_context(nc.sbuf_tensor("sb_" + name, shape, dt))

        def sem(name):
            return ctx.enter_context(nc.semaphore(name))

        raw = sb("raw", [P, RING, BE])
        w_hi = sb("w_hi", [P, RING, BE], F32R)
        w_lo = sb("w_lo", [P, RING, BE], F32R)
        x = sb("x", [P, KC, T])
        a_hi = [sb(f"a_hi{i}", [P, KC, T], F32R) for i in range(2)]
        a_lo = [sb(f"a_lo{i}", [P, KC, T], F32R) for i in range(2)]
        qT = sb("qT", [P, KC, T])
        kT = sb("kT", [P, KC, T])
        v = sb("v", [P, QB, D])
        y = sb("y", [P, KC, T])
        work = sb("work", [P, 6144])
        bias = sb("bias", [P, 16, T])
        cw = sb("cw", [P, NCH * 32])
        gains = sb("gains", [P, KC, NG])
        ident = sb("ident", [P, P])
        ones = sb("ones", [P, P])
        upper = sb("upper", [P, P])
        r_all = sb("r_all", [P, 2, T])
        sd = sb("sd", [P, T])
        rT = sb("rT", [P, QB])
        poolw = sb("poolw", [P, 4, P])
        lam = sb("lam", [P, 2, 4, HD])
        lam_s = sb("lam_s", [P, 4])
        lam_fac = sb("lam_fac", [P, 2, 4])
        sink = sb("sink", [P, 16])
        sm_small = sb("sm_small", [P, 2, 5, 4])
        hh = sb("hh", [P, 4, T], F32R)
        hl = sb("hl", [P, 4, T], F32R)
        eps_t = sb("eps_t", [P, 2])

        us = work[:, 0:1024].rearrange("p (c h t) -> p c h t", c=2, h=2)
        acc = work[:, 1024:2048].rearrange("p (c h t) -> p c h t", c=2, h=2)
        sil = work[:, 2048:2560].rearrange("p (c t) -> p c t", c=2)
        hid = work[:, 2560:3072].rearrange("p (c t) -> p c t", c=2)
        prob = work[:, 0:3072].rearrange("p (b s k) -> p b s k", b=3, s=2)
        probT = work[:, 3072:5120].rearrange("p (b s k) -> p b s k", b=2, s=2)
        diag = work[:, 5120:6144].rearrange("p (b i q) -> p b i q", b=2, i=4)
        win_b = bias[:, 12:16, :]
        memT = bias[:, 0:8, :]
        zbuf = work[:, 0:3072].rearrange("p (h k) -> p h k", h=8)
        tbuf = work[:, 3072:6144].rearrange("p (h k) -> p h k", h=8)
        conv_rows = work[0:32, 0:2816]
        gain_rows = work[0:NG, 2816:3840]
        x_rows = work[:, 4096:6144].rearrange("p (b d) -> p b d", b=QB)
        sq = qT
        pin = y[:, 0:4, :]
        win_a = y[:, 4:8, :]
        inv_cnt = bias[:, 8:12, :]
        table_sb = v[0:16, 0, 0:TW]

        PS = ctx.enter_context(nc.psum_tensor("ps", [P, 8, 512], F32))
        DB = [PS[:, i, :] for i in range(4)]
        UB = [PS[:, 4 + i, :] for i in range(4)]

        bias_dram = nc.dram_tensor("bias_dram", [16, P * TW], F32)

        s_const = sem("s_const")
        s_xin = sem("s_xin")
        s_gin = sem("s_gin")
        s_cin = sem("s_cin")
        s_rows = sem("s_rows")
        s_misc = sem("s_misc")
        s_tab_in = sem("s_tab_in")
        s_mem_in = sem("s_mem_in")
        s_setup_pe = sem("s_setup_pe")
        s_gain = sem("s_gain")
        s_conv = sem("s_conv")
        s_tab = sem("s_tab")
        s_tab_out = sem("s_tab_out")
        s_bias_in = sem("s_bias_in")
        s_bias_ok = sem("s_bias_ok")
        s_lam = sem("s_lam")
        s_memT = sem("s_memT")
        s_mem_ok = sem("s_mem_ok")
        raw_ready = [sem(f"raw_ready{i}") for i in range(RING)]
        hi_ready = sem("hi_ready")
        lo_dve = sem("lo_dve")
        lo_pool = sem("lo_pool")
        blocks_done = sem("blocks_done")
        half_done = sem("half_done")
        u_free = sem("u_free")
        x_ready = sem("x_ready")
        y_ready = sem("y_ready")
        act_hi = [sem(f"act_hi{i}") for i in range(2)]
        act_lo = [sem(f"act_lo{i}") for i in range(2)]
        sq_ready = sem("sq_ready")
        sq_tree = sem("sq_tree")
        sq_sum = sem("sq_sum")
        ss_done = sem("ss_done")
        sd_ready = sem("sd_ready")
        r_ready = sem("r_ready")
        rT_done = sem("rT_done")
        rT_ready = sem("rT_ready")
        post_t = sem("post_t")
        conv_acc = sem("conv_acc")
        conv_t1 = sem("conv_t1")
        conv_t0 = sem("conv_t0")
        sil_ready = sem("sil_ready")
        hid_ready = sem("hid_ready")
        hh_ready = sem("hh_ready")
        hl_ready = sem("hl_ready")
        scores_ready = sem("scores_ready")
        biased = sem("biased")
        negmax = sem("negmax")
        exp_ready = sem("exp_ready")
        sink_exp = sem("sink_exp")
        rs_ready = sem("rs_ready")
        diag_ready = sem("diag_ready")
        pt_done = sem("pt_done")
        pt_ready = sem("pt_ready")
        pv_done = sem("pv_done")
        sub_sq = sem("sub_sq")
        sub_ss = sem("sub_ss")
        sub_sd = sem("sub_sd")
        sub_t = sem("sub_t")
        win_ok = sem("win_ok")
        poolmix_done = sem("poolmix_done")
        z_done = sem("z_done")
        z_copied = sem("z_copied")
        t_exp = sem("t_exp")
        t_ln = sem("t_ln")
        sp_sum = sem("sp_sum")
        sp_ready = sem("sp_ready")
        cs_done = sem("cs_done")
        z_less = sem("z_less")
        a_exp = sem("a_exp")
        a_ready = sem("a_ready")
        spv_done = sem("spv_done")
        dve_link = sem("dve_link")
        act_link = sem("act_link")
        pool_link = sem("pool_link")
        s_outT = sem("s_outT")
        s_outc = sem("s_outc")
        s_out = sem("s_out")

        block = ctx.enter_context(nc.Block())

        def both(ap, n=2):
            return ap.unsqueeze(1).to_broadcast([ap.shape[0], n, ap.shape[1]])

        def wait_block(eng, a, s=0):
            if a % RING == 2:
                eng.wait_ge(lo_pool, a // RING + 1 + s)
            else:
                eng.wait_ge(lo_dve, dve_splits(a) + 2 * s)

        def up_block(ph, s0, part):
            return ph["n"] + part if s0 == 0 else ph["n"] + 3 * s0 - 1 + part

        def down_block(ph, s0):
            return ph["n"] + (3 * NSTEP - 1 if s0 == NSTEP - 1 else 3 * s0 + 4)

        def cols(ph, s0):
            return (ph["F"] - (NSTEP - 1) * 2 * P) // 2 if s0 == NSTEP - 1 else P

        def ffn_steps(eng, up, down):
            up(0, 0)
            with eng.Fori(0, NLOOP) as i:
                for d in range(2):
                    up(d + 1, 2 * i)
                    down(d, 2 * i)
            for s in range(2 * NLOOP, NSTEP - 1):
                up(s + 1, 0)
                down(s, 0)
            down(NSTEP - 1, 0)

        @block.sync
        def _(sp):
            def load(a, s, dst, src):
                if a >= RING:
                    wait_block(sp, a - RING, s)
                sp.dma_start(dst, src).then_inc(raw_ready[a % RING], 16)

            def slot(a, k):
                return raw[:, a % RING, :].rearrange("p (k n) -> p k n", k=k)

            sp.dma_start(x_rows, io["x"][0].rearrange("(b p) d -> p b d", p=P)).then_inc(s_xin, 16)
            for ph in phases:
                if ph["kind"] == "lin":
                    for i, (_, (w, l), c0, _) in enumerate(ph["blocks"]):
                        src = io[w][l][:, c0:c0 + BW].rearrange("(k p) n -> p k n", p=P)
                        load(ph["n"] + i, 0, slot(ph["n"] + i, KC), src)
                elif ph["kind"] == "ffn":
                    def up(s0, s, ph=ph):
                        n = cols(ph, s0)
                        for part in range(2):
                            w, l, c0 = ph["up"][part]
                            b = up_block(ph, s0, part)
                            src = io[w][l][:, bass.ds(c0 + 2 * P * s0 + 2 * P * s, 2 * n)]
                            load(b, s, slot(b, KC)[:, :, 0:2 * n], src.rearrange("(k p) n -> p k n", p=P))

                    def down(s0, s, ph=ph):
                        n = cols(ph, s0)
                        w, l = ph["down"]
                        b = down_block(ph, s0)
                        src = io[w][l][bass.ds(2 * P * s0 + 2 * P * s, 2 * n), :]
                        load(b, s, slot(b, 2)[0:n, :, :], src.rearrange("(k p) n -> p k n", p=n))

                    ffn_steps(sp, up, down)
                elif ph.get("moba"):
                    moba_lo = 8 * (ph["fill"] + 1)
                elif ph.get("src") == "mem":
                    sp.wait_ge(act_lo[1], moba_lo)
                    sp.dma_start(x_rows, io["mem_2"][0].rearrange("(b p) d -> p b d", p=P)).then_inc(s_mem_in, 16)
            sp.wait_ge(s_outc, 4)
            sp.dma_start(out[0].rearrange("(b p) d -> p b d", p=P), x_rows).then_inc(s_out, 16)
            sp.wait_ge(s_out, 16)

        def make_alibi(pool, link):
            dist = y[:, 0, :]
            idx = y[:, 1, :].bitcast(mybir.dt.int32)
            link(pool.iota(idx, pattern=[[-1, T]], base=P, channel_multiplier=1))
            link(pool.tensor_copy(dist, idx))
            for h in range(8):
                ins = pool.tensor_scalar(bias[:, h, :], dist, -2.0 ** -(h + 1), None, ALU.mult)
            link(ins)
            pool.affine_select(out=bias[:, 0:8, P:T], in_=bias[:, 0:8, P:T], compare_op=ALU.is_ge, fill=NEG, base=0,
                               pattern=[[0, 8], [-1, P]], channel_multiplier=1).then_inc(s_bias_ok, 1)
            link(pool.iota(idx, pattern=[[1, T]], base=1, channel_multiplier=0))
            link(pool.tensor_copy(dist, idx))
            for g in range(4):
                ins = pool.tensor_scalar(inv_cnt[:, g, :], dist, float(2 << g), None, ALU.min)
            ins.then_inc(s_bias_ok, 1)

        @block.gpsimd
        def _(pool):
            links = [0]

            def link(ins):
                links[0] += 1
                ins.then_inc(pool_link, 1)
                pool.wait_ge(pool_link, links[0])

            def split(a, s=0):
                if a % RING == 2 and a < NBLOCKS:
                    pool.wait_ge(hi_ready, a + 1 + RING * s)
                    pool.tensor_tensor(w_lo[:, 2, :], raw[:, 2, :], w_hi[:, 2, :].bitcast(F32), ALU.subtract)\
                        .then_inc(lo_pool, 1)

            def causal(ap, heads, op, fill):
                return pool.affine_select(out=ap, in_=ap, compare_op=op, fill=fill, base=0,
                                          pattern=[[0, heads], [-1, P]], channel_multiplier=1)

            def anticausal(ap, heads):
                return pool.affine_select(out=ap, in_=ap, compare_op=ALU.is_gt, fill=0.0, base=0,
                                          pattern=[[0, heads], [1, P]], channel_multiplier=-1)

            link(pool.memset(ident[:, :], 0.0))
            pool.affine_select(out=ident[:, :], in_=ident[:, :], compare_op=ALU.not_equal, fill=1.0, base=0,
                               pattern=[[-1, P]], channel_multiplier=1).then_inc(s_const, 1)
            pool.memset(ones[:, :], 1.0).then_inc(s_const, 1)
            link(pool.memset(upper[:, :], 1.0))
            pool.affine_select(out=upper[:, :], in_=upper[:, :], compare_op=ALU.is_ge, fill=0.0, base=0,
                               pattern=[[-1, P]], channel_multiplier=1).then_inc(s_const, 1)
            pool.memset(lam_fac[:, :, :], 1.0).then_inc(s_const, 1)

            def mask_bias():
                causal(bias[:, :, P:T], 16, ALU.is_ge, NEG).then_inc(s_bias_ok, 1)

            def square_sum(ph):
                si, k = ph["stat"], ph["tree"]
                for i in range(4):
                    pool.wait_ge(sq_ready, 4 * si + i + 1)
                    if i >= 2:
                        pool.wait_ge(sq_tree, 3 * k + i - 1)
                    if i:
                        pool.tensor_tensor(sq[:, 0:2, :], sq[:, 0:2, :], sq[:, 2 * i:2 * i + 2, :], ALU.add)\
                            .then_inc(sq_tree, 1)
                pool.wait_ge(sq_tree, 3 * k + 3)
                pool.tensor_tensor(sq[:, 0, :], sq[:, 0, :], sq[:, 1, :], ALU.add).then_inc(sq_sum, 1)

            def load_bias():
                src = bass.AP(bias_dram, 127, [[TW - 1, P], [P * TW, 16], [1, T]])
                pool.dma_start(bias[:, :, :], src).then_inc(s_bias_in, 16)

            for ph in phases:
                kind = ph["kind"]
                if kind == "prep":
                    square_sum(ph)
                elif kind == "lin":
                    for i in range(len(ph["blocks"])):
                        b = ph["n"] + i
                        if i == 0:
                            split(b + 2)
                        if i < len(ph["blocks"]) - 1:
                            split(b + 3)
                        if b == 3:
                            pool.wait_ge(s_tab, 1)
                            pool.dma_start(bias_dram[:, :].rearrange("h (q z) -> h q z", q=P),
                                           table_sb.unsqueeze(1).to_broadcast([16, P, TW])).then_inc(s_tab_out, 16)
                        if b == 6:
                            pool.wait_ge(s_tab_out, 16)
                            load_bias()
                    if ph["n"] == 0:
                        pool.wait_ge(s_bias_in, 16)
                        mask_bias()
                elif kind == "soft":
                    for g in range(ph["heads"] // 2):
                        pool.wait_ge(rs_ready, ph["sg"] + g + 1)
                        if g >= 2:
                            pool.wait_ge(pt_done, ph["sg"] + g - 1)
                        for i in range(4):
                            ins = pool.tensor_scalar(diag[:, g % 2, i, :], ident[:, :], sm_small[:, g % 2, 3, i:i + 1],
                                                     None, ALU.mult)
                        ins.then_inc(diag_ready, 1)
                elif kind == "stick":
                    for half in range(2):
                        for g in range(4):
                            pool.wait_ge(sp_sum, ph["kg"] + 4 * half + g + 1)
                            anticausal(tbuf[:, 2 * g:2 * g + 2, 0:P], 2)
                            anticausal(tbuf[:, 2 * g:2 * g + 2, 2 * P:3 * P], 2).then_inc(sp_ready, 1)
                        for g in range(4):
                            pool.wait_ge(a_exp, ph["kg"] + 4 * half + g + 1)
                            anticausal(zbuf[:, 2 * g:2 * g + 2, 0:P], 2)
                            anticausal(zbuf[:, 2 * g:2 * g + 2, 2 * P:3 * P], 2).then_inc(a_ready, 1)
                elif kind == "ffn":
                    def hidden(s0, s, ph=ph):
                        n = cols(ph, s0)
                        for c in range(2):
                            f = ph["f"] + 2 * s0 + c
                            at = 2 * (s0 % 2) + c
                            pool.wait_ge(hh_ready, f + 1 + 2 * s)
                            pool.tensor_tensor(hl[0:n, at, :], hid[0:n, c, :], hh[0:n, at, :].bitcast(F32),
                                               ALU.subtract).then_inc(hl_ready, 1)

                    def up(s0, s, ph=ph):
                        b = up_block(ph, s0, 0)
                        if s0 == 0:
                            split(b + 2)
                        split(b + 3, s)
                        split(b + 4, s)
                        hidden(s0, s)

                    def down(s0, s, ph=ph):
                        if s0 < NSTEP - 1:
                            split(down_block(ph, s0) + 3, s)

                    ffn_steps(pool, up, down)
                    if ph["conv"] == 1:
                        pool.affine_select(out=bias[:, :, 0:P], in_=bias[:, :, 0:P], compare_op=ALU.is_gt, fill=NEG,
                                           base=0, pattern=[[0, 16], [1, P]], channel_multiplier=-1)\
                            .then_inc(s_bias_ok, 1)
                    if ph["conv"] == 2:
                        load_bias()
                        pool.wait_ge(s_bias_in, 32)
                        mask_bias()
                    if ph["conv"] == 3:
                        make_alibi(pool, link)

        def softmax_act(act, ph):
            G = ph["heads"] // 2
            a = ph["act"]
            W = T * 2 if ph.get("cross") else 3 * P
            A = T if ph.get("cross") else P

            if ph["sg"] == 0:
                act.wait_ge(s_lam, 1)
                act.activation(lam_s[:, :], lam_s[:, :], ACT.Exp).then_inc(s_lam, 1)

            def exps(g):
                sg = ph["sg"] + g
                act.wait_ge(negmax, sg + 1)
                small = sm_small[:, g % 2]
                for i in range(4):
                    s, lo, hi = i % 2, (0, A)[i // 2], (A, W)[i // 2]
                    p = prob[:, g % 3, s, lo:hi]
                    ins = act.activation(p, p, ACT.Exp, bias=small[:, 1, i:i + 1], accum_out=small[:, 2, i:i + 1])
                if ph.get("sink"):
                    ins = act.activation(small[:, 4, :], small[:, 4, :], ACT.Exp)
                ins.then_inc(exp_ready, 1)

            def copy_pt(g):
                sg = ph["sg"] + g
                act.wait_ge(pt_done, sg + 1)
                if g >= 2:
                    act.wait_ge(pv_done, sg - 1)
                if ph.get("diff") is not None:
                    act.activation(probT[:, g % 2, 0, 0:W], UB[0][:, 0:W], ACT.Copy).then_inc(pt_ready, 1)
                else:
                    act.activation(probT[:, g % 2, :, 0:W], PS[:, 4:6, 0:W], ACT.Copy).then_inc(pt_ready, 1)

            def out_hi(g):
                sg = ph["sg"] + g
                act.wait_ge(pv_done, sg + 1)
                if ph.get("diff") is not None:
                    act.activation(y[:, g, :], UB[2 + g % 2][:, 0:T], ACT.Copy).then_inc(y_ready, 1)
                elif ph.get("cross"):
                    for i in range(4):
                        act.activation(a_hi[a][:, 4 * g + i, :], UB[2 + i // 2][:, (i % 2) * T:(i % 2 + 1) * T],
                                       ACT.Copy).then_inc(act_hi[a], 1)
                else:
                    act.activation(a_hi[a][:, g, :], UB[2 + g % 2][:, 0:T], ACT.Copy).then_inc(act_hi[a], 1)

            for g in range(G + 3):
                if g < G:
                    exps(g)
                if 2 <= g < G + 2:
                    copy_pt(g - 2)
                if g >= 3:
                    out_hi(g - 3)
            if ph.get("diff") is not None:
                j = ph["diff"]
                act.wait_ge(y_ready, ph["y"] + 8)
                for i in range(4):
                    act.activation(sq[:, 2 * i:2 * i + 2, :], y[:, 2 * i:2 * i + 2, :], ACT.Square).then_inc(sub_sq, 1)
                for i in range(4):
                    act.wait_ge(sub_ss, 4 * j + i + 1)
                    act.activation(kT[:, 2 * i:2 * i + 2, :], DB[i].rearrange("p (a b) -> p a b", a=2), ACT.Sqrt,
                                   scale=1.0 / P, bias=eps_t[:, 0:1]).then_inc(sub_sd, 1)
                for i in range(4):
                    act.wait_ge(sub_t, 4 * j + i + 1)
                    act.activation(a_hi[a][:, 2 * i:2 * i + 2, :], y[:, 2 * i:2 * i + 2, :], ACT.Copy,
                                   scale=1.0 - lambda_init(ph["layer"])).then_inc(act_hi[a], 2)
            if ph.get("moba"):
                act.wait_ge(poolmix_done, 1)
                for g in range(4):
                    act.activation(a_hi[a][:, 4 + g, :], DB[g // 2][:, (g % 2) * T:(g % 2 + 1) * T], ACT.Copy,
                                   scale=gains[:, g, G_POOL:G_POOL + 1]).then_inc(act_hi[a], 1)

        def stick_act(act, ph):
            a = ph["act"]
            for half in range(2):
                k0 = ph["kg"] + 4 * half
                for g in range(4):
                    act.wait_ge(z_done, k0 + g + 1)
                    act.wait_ge(z_copied, k0 + g + 1)
                    S = PS[:, 2 * (g % 2):2 * (g % 2) + 2, 0:3 * P]
                    t = tbuf[:, 2 * g:2 * g + 2, :]
                    if half == 1:
                        act.wait_ge(cs_done, k0)
                    act.activation(t, S, ACT.Abs, scale=ph["scale"]).then_inc(act_link, 1)
                    act.wait_ge(act_link, k0 - ph["kg"] + g + 1)
                    act.activation(t, t, ACT.Exp, scale=-1.0).then_inc(t_exp, 1)
                for g in range(4):
                    t = tbuf[:, 2 * g:2 * g + 2, :]
                    act.wait_ge(t_exp, k0 + g + 1)
                    act.activation(t, t, ACT.Ln, bias=1.0).then_inc(t_ln, 1)
                for g in range(4):
                    z = zbuf[:, 2 * g:2 * g + 2, :]
                    act.wait_ge(z_less, k0 + g + 1)
                    act.activation(z, z, ACT.Exp).then_inc(a_exp, 1)
                for g in range(4):
                    act.wait_ge(spv_done, k0 + g + 1)
                    act.activation(a_hi[a][:, 4 * half + g, :], UB[g][:, 0:T], ACT.Copy).then_inc(act_hi[a], 1)

        @block.scalar
        def _(act):
            act.wait_ge(s_rows, 2)
            for i, (name, n) in enumerate((("attn_norm", 4), ("ffn_norm", 4))):
                act.dma_start(gain_rows[4 * i:4 * i + n, :], io[name]).then_inc(s_gin, 16)
            act.dma_start(gain_rows[8:9, :], io["final_norm"].unsqueeze(0)).then_inc(s_gin, 16)
            for i, name in enumerate(("ffn1_pre_g_2", "ffn1_post_g_2", "mix_pre_g_2", "mix_post_g_2", "xa_pre_g_2",
                                      "mem_g_2", "xa_post_g_2", "ffn2_pre_g_2", "ffn2_post_g_2")):
                act.dma_start(gain_rows[9 + i:10 + i, :], io[name]).then_inc(s_gin, 16)
            act.dma_start(gain_rows[18:19, 0:512], io["pool_scale_2"]).then_inc(s_gin, 16)
            act.dma_start(gain_rows[19:21, 0:P], io["da_subln"]).then_inc(s_gin, 16)
            act.dma_start(conv_rows[0:24, 0:F1], io["ffn_conv_w"].rearrange("l w (h f) -> (l w h) f", h=2))\
                .then_inc(s_cin, 16)
            act.dma_start(conv_rows[24:32, 0:F1], io["ffn_conv_b"].rearrange("l (h f) -> (l h) f", h=2))\
                .then_inc(s_cin, 16)
            act.dma_start(kT[0:N_BUCKETS, 0, 0:16], io["rel_bias"]).then_inc(s_tab_in, 16)
            act.dma_start(kT[0:N_BUCKETS, 2:4, :].rearrange("p a b -> p (a b)")[:, 0:TW], io["bucket_of_distance"])\
                .then_inc(s_tab_in, 16)
            act.dma_start(lam[:, :, :, :].rearrange("p a b c -> p (a b c)"),
                          io["da_lambda"].rearrange("a b c -> (a b c)").unsqueeze(0).to_broadcast([P, 2 * 4 * HD]))\
                .then_inc(s_misc, 16)
            act.dma_start(sink[:, :], io["sw_sinks"].to_broadcast([P, 16])).then_inc(s_misc, 16)
            act.dma_start(poolw[:, :, :], io["pool_w_2"][0].rearrange("g c d -> c g d")).then_inc(s_misc, 16)

            def split(a, s=0):
                if a >= NBLOCKS:
                    return
                act.wait_ge(raw_ready[a % RING], 16 * (a // RING + 1) + 16 * s)
                if a >= RING:
                    act.wait_ge(blocks_done, a - RING + 1 + RING * s)
                act.activation(w_hi[:, a % RING, :], raw[:, a % RING, :], ACT.Copy).then_inc(hi_ready, 1)

            def root(si, bank=3, mul=1.0):
                act.wait_ge(ss_done, si + 1)
                if si >= 1:
                    act.wait_ge(r_ready, si)
                act.activation(sd[:, :], PS[:, bank, 0:T], ACT.Sqrt, scale=mul / D, bias=eps_ap(mul))\
                    .then_inc(sd_ready, 1)

            def hi_pair(ph, src, i):
                for c in (2 * i, 2 * i + 1):
                    act.activation(a_hi[ph["act"]][:, c, :], src[:, c, :], ACT.Copy,
                                   scale=gains[:, c, ph["gain"]:ph["gain"] + 1]).then_inc(act_hi[ph["act"]], 1)
                square_pair(src, i)

            def square_pair(src, i):
                act.activation(sq[:, 2 * i:2 * i + 2, :], src[:, 2 * i:2 * i + 2, :], ACT.Square).then_inc(sq_ready, 1)

            def prep_pair(ph, i):
                act.wait_ge(x_ready, ph["x"] - 4 + i + 1)
                hi_pair(ph, x, i)

            def eps_ap(mul):
                return eps_t[:, (0 if mul == 1.0 else 1):(1 if mul == 1.0 else 2)]

            split(0)
            act.wait_ge(s_gain, 1)
            for i in range(4):
                prep_pair(phases[0], i)
            split(1)
            for ph in phases[1:]:
                kind = ph["kind"]
                if kind == "prep" and ph["src"] == "mem":
                    for i in range(4):
                        act.wait_ge(s_mem_ok, i + 1)
                        hi_pair(ph, memT, i)
                elif kind == "post":
                    for i in range(4):
                        if ph["src"] == "y":
                            act.wait_ge(y_ready, ph["y"] - 4 + i + 1)
                            square_pair(y, i)
                        else:
                            act.wait_ge(x_ready, ph["x"] - 4 + i + 1)
                            square_pair(x, i)
                    root(ph["stat"], ph["bank"], (ph["weight"] or 1.0) ** -2)
                    for i in range(4):
                        prep_pair(ph["then"], i) if "then" in ph else None
                elif kind == "lin":
                    for i in range(len(ph["blocks"])):
                        b = ph["n"] + i
                        if i == 0:
                            split(b + 2)
                        if i < len(ph["blocks"]) - 1:
                            split(b + 3)
                        if i == 1 and ph["stat"] is not None:
                            root(ph["stat"])
                        if "then" in ph:
                            prep_pair(ph["then"], i)
                elif kind == "soft":
                    softmax_act(act, ph)
                elif kind == "stick":
                    stick_act(act, ph)
                elif kind == "ffn":
                    def up(s0, s, ph=ph):
                        b = up_block(ph, s0, 0)
                        if s0 == 0:
                            split(b + 2)
                        split(b + 3, s)
                        split(b + 4, s)
                        if s0 == 0:
                            root(ph["stat"])
                        n = cols(ph, s0)
                        if ph["conv"] is not None:
                            for c in range(2):
                                u = ph["u"] + 2 * s0 + c
                                f = ph["f"] + 2 * s0 + c
                                act.wait_ge(u_free, u + 1 + 2 * s)
                                if f >= 2:
                                    act.wait_ge(hid_ready, f - 1 + 2 * s)
                                for h in range(2):
                                    at = (2 * s0 + c) * 32
                                    rw, rb = (ph["conv"] * 3 + 2) * 2 + h, 24 + ph["conv"] * 2 + h
                                    act.activation(acc[0:n, c, h, :], us[0:n, c, h, :], ACT.Identity,
                                                   scale=cw[0:n, bass.ds(at + rw + 64 * s, 1)],
                                                   bias=cw[0:n, bass.ds(at + rb + 64 * s, 1)]).then_inc(conv_acc, 1)
                        for c in range(2):
                            f = ph["f"] + 2 * s0 + c
                            if ph["conv"] is not None:
                                act.wait_ge(conv_t0, 2 * f + 1 + 4 * s)
                                src = acc[0:n, c, 0, :]
                            else:
                                act.wait_ge(u_free, ph["u"] + 2 * s0 + c + 1 + 2 * s)
                                act.wait_ge(hid_ready, f - 1 + 2 * s)
                                src = us[0:n, c, 0, :]
                            act.activation(sil[0:n, c, :], src, ACT.Silu).then_inc(sil_ready, 1)
                        for c in range(2):
                            if c == 0 and s0 >= 1:
                                act.wait_ge(blocks_done, ph["n"] + 3 * s0 - 1 + 3 * s)
                            act.wait_ge(hid_ready, ph["f"] + 2 * s0 + c + 1 + 2 * s)
                            act.activation(hh[0:n, 2 * (s0 % 2) + c, :], hid[0:n, c, :], ACT.Copy).then_inc(hh_ready, 1)

                    def down(s0, s, ph=ph):
                        if s0 < NSTEP - 1:
                            split(down_block(ph, s0) + 3, s)

                    ffn_steps(act, up, down)
                    if "then" in ph:
                        for i in range(4):
                            prep_pair(ph["then"], i)

        @block.tensor
        def _(pe):
            def product(o, hi1, lo1, hi2, lo2, start, stop):
                pe.matmul(o, hi1, hi2, start=start, stop=False, skip_group_check=True)
                pe.matmul(o, hi1, lo2, start=False, stop=False, skip_group_check=True)
                return pe.matmul(o, lo1, hi2, start=False, stop=stop, skip_group_check=True)

            def weights(a, k):
                s = a % RING
                return (w_hi[:, s, :].rearrange("p (k n) -> p k n", k=k), w_lo[:, s, :].rearrange("p (k n) -> p k n", k=k))

            def square_total(si):
                pe.wait_ge(sq_sum, tree_of[si] + 1)
                if si >= 1:
                    pe.wait_ge(sd_ready, si)
                pe.matmul(DB[3][:, 0:T], ones[:, :], sq[:, 0, :], start=True, stop=True, skip_group_check=True)\
                    .then_inc(ss_done, 1)

            def square_total_by_chunk(ph):
                pe.wait_ge(sd_ready, ph["stat"])
                for c in range(KC):
                    pe.wait_ge(sq_ready, 4 * ph["stat"] + c // 2 + 1)
                    ins = pe.matmul(PS[:, ph["bank"], 0:T], ones[:, :], sq[:, c, :], start=c == 0, stop=c == KC - 1,
                                    skip_group_check=True)
                ins.then_inc(ss_done, 1)

            def linear(ph):
                a = ph["act"]
                ah, al = a_hi[a], a_lo[a]
                turned = False
                for i, (typ, _, _, _) in enumerate(ph["blocks"]):
                    counted = typ not in ("proj", "y")
                    b, u = ph["n"] + i, ph["u"] + i
                    wait_block(pe, b)
                    if counted and u >= 4:
                        pe.wait_ge(u_free, u - 3)
                    elif i == 0:
                        pe.wait_ge(act_lo[a], 8 * (ph["fill"] + 1))
                    if typ == "v" and not turned:
                        turned = True
                        pe.wait_ge(r_ready, ph["r_of"] + 1)
                        for q in range(QB):
                            ins = pe.matmul(DB[3][:, T + q:T + q + 1], r_all[0:1, ph["r"], q * P:(q + 1) * P],
                                            ones[0:1, 0:1], start=True, stop=True, skip_group_check=True)
                        ins.then_inc(rT_done, 1)
                    wh, wl = weights(b, KC)
                    o = UB[u % 4]
                    for j in range(2):
                        for k in range(KC):
                            if i == 0 and j == 0:
                                pe.wait_ge(act_hi[a], 8 * ph["fill"] + k + 1)
                                pe.wait_ge(act_lo[a], 8 * ph["fill"] + k + 1)
                            oj = o[:, j * T:(j + 1) * T]
                            if typ == "v":
                                ts = slice(j * P, (j + 1) * P)
                                ins = product(oj, ah[:, k, ts], al[:, k, ts], wh[:, k, :], wl[:, k, :], k == 0, k == KC - 1)
                            else:
                                cs = slice(j * P, (j + 1) * P)
                                ins = product(oj, wh[:, k, cs], wl[:, k, cs], ah[:, k, :], al[:, k, :], k == 0, k == KC - 1)
                    ins.then_inc(blocks_done, 1)
                    if i == 1 and ph["stat"] is not None:
                        square_total(ph["stat"])
                    if b == 1:
                        setup_rest()

            def ffn(ph):
                a = ph["act"]

                def up(s0, s):
                    n = cols(ph, s0)
                    for part in range(2):
                        b = up_block(ph, s0, part)
                        wait_block(pe, b, s)
                        wh, wl = weights(b, KC)
                        for c in range(2):
                            u = ph["u"] + 2 * s0 + c
                            if part == 0:
                                pe.wait_ge(u_free, u - 3 + 2 * s)
                            o = UB[u % 4][:, part * T:(part + 1) * T]
                            cs = slice(c * n, c * n + P)
                            for k in range(KC):
                                if s0 == 0 and part == 0 and c == 0:
                                    pe.wait_ge(act_hi[a], 8 * ph["fill"] + k + 1)
                                    pe.wait_ge(act_lo[a], 8 * ph["fill"] + k + 1)
                                ins = product(o, wh[:, k, cs], wl[:, k, cs], a_hi[a][:, k, :], a_lo[a][:, k, :],
                                              k == 0 and part == 0, k == KC - 1)
                            if part == 1 and c == 0:
                                ins.then_inc(half_done, 1)
                        ins.then_inc(blocks_done, 1)
                        if s0 == 0 and part == 1:
                            square_total(ph["stat"])

                def down(s0, s):
                    n = cols(ph, s0)
                    b = down_block(ph, s0)
                    wait_block(pe, b, s)
                    wh, wl = weights(b, 2)
                    for k in range(2):
                        f = ph["f"] + 2 * s0 + k
                        at = 2 * (s0 % 2) + k
                        pe.wait_ge(hl_ready, f + 1 + 2 * s)
                        for m in range(KC):
                            first = first_down and s0 == 0 and k == 0 and m % 2 == 0
                            ins = product(DB[m // 2][:, (m % 2) * T:(m % 2 + 1) * T], wh[0:n, k, m * P:(m + 1) * P],
                                          wl[0:n, k, m * P:(m + 1) * P], hh[0:n, at, :], hl[0:n, at, :], first,
                                          s0 == NSTEP - 1 and k == 1)
                    ins.then_inc(blocks_done, 1)

                first_down = True
                up(0, 0)
                up(1, 0)
                down(0, 0)
                first_down = False
                with pe.Fori(0, NLOOP) as i:
                    for d in range(2):
                        up(d + 2, 2 * i)
                        down(d + 1, 2 * i)
                for st in range(2 * NLOOP + 1, NSTEP - 1):
                    up(st + 1, 0)
                    down(st, 0)
                down(NSTEP - 1, 0)

            def score_operands(ph, m, kk=0):
                if ph.get("cross"):
                    return qT[:, 2 * m + kk, :], kT[:, 2 * m + kk, :]
                ps = slice((m % 2) * HD, (m % 2 + 1) * HD)
                return qT[ps, m // 2, :], kT[ps, m // 4 if ph.get("sink") else m // 2, :]

            def softmax(ph):
                G = ph["heads"] // 2
                cross, diff = ph.get("cross"), ph.get("diff") is not None
                a = ph["act"]

                def scores(g):
                    if g == 0:
                        pe.wait_ge(u_free, ph["u"])
                    if g >= 2:
                        pe.wait_ge(biased, ph["sg"] + g - 1)
                    if cross:
                        for s in range(2):
                            o = DB[2 * (g % 2) + s]
                            for qb in range(QB):
                                for kk in range(2):
                                    q, k = score_operands(ph, 2 * g + s, kk)
                                    ins = pe.matmul(o[:, qb * T:(qb + 1) * T], q[:, qb * P:(qb + 1) * P], k,
                                                    start=kk == 0, stop=kk == 1, skip_group_check=True)
                    else:
                        for qb in range(QB):
                            for s in range(2):
                                q, k = score_operands(ph, 2 * g + s)
                                ins = pe.matmul(DB[2 * (g % 2) + s][:, qb * P:(1 + 2 * qb) * P], q[:, qb * P:(qb + 1) * P],
                                                k[:, 0:(qb + 1) * P], start=True, stop=True, skip_group_check=True)
                    ins.then_inc(scores_ready, 1)

                def turn(g):
                    pe.wait_ge(diag_ready, ph["sg"] + g + 1)
                    if g >= 1:
                        pe.wait_ge(pt_ready, ph["sg"] + g)
                    parts = [(0, 0), (2, 1), (1, 0), (3, 1)] if cross else [(0, 0), (1, 1), (2, 1)]
                    for n, (c, qb) in enumerate(parts):
                        for s in range(2):
                            o = UB[0 if diff else s][:, n * P:(n + 1) * P]
                            ins = pe.matmul(o, prob[:, g % 3, s, c * P:(c + 1) * P], diag[:, g % 2, 2 * qb + s, :],
                                            start=not (diff and s), stop=not diff or s == 1, skip_group_check=True)
                    ins.then_inc(pt_done, 1)

                def values(g):
                    pe.wait_ge(pt_ready, ph["sg"] + g + 1)
                    if diff:
                        if g >= 2:
                            pe.wait_ge(y_ready, ph["y"] + g - 1)
                    elif cross:
                        if g >= 1:
                            pe.wait_ge(act_lo[a], 8 * ph["fill"] + 4 * g)
                    elif g >= 2:
                        pe.wait_ge(act_lo[a], 8 * ph["fill"] + g - 1)
                    for s in range(1 if diff else 2):
                        m = 2 * g + s
                        pT = probT[:, g % 2, s, :]
                        if cross:
                            for e in range(2):
                                o = UB[2 + s][:, e * T:(e + 1) * T]
                                for kb in range(2):
                                    c0 = m * T + e * P
                                    ins = pe.matmul(o, v[:, kb, c0:c0 + P], pT[:, kb * T:(kb + 1) * T], start=kb == 0,
                                                    stop=kb == 1, skip_group_check=True)
                        else:
                            w = P if diff else HD
                            c0 = g * P if diff else (m // 4 if ph.get("sink") else m) * HD
                            o = UB[2 + g % 2][s * HD:s * HD + w, 0:T]
                            pe.matmul(o, v[:, 0, c0:c0 + w], pT[:, 0:T], start=True, stop=False, skip_group_check=True)
                            ins = pe.matmul(o[:, P:T], v[:, 1, c0:c0 + w], pT[:, T:T + P], start=False, stop=True,
                                            skip_group_check=True)
                    ins.then_inc(pv_done, 1)

                for g in range(G + 3):
                    if g < G:
                        scores(g)
                    if 2 <= g < G + 2:
                        turn(g - 2)
                    if g >= 3:
                        values(g - 3)
                if diff:
                    for i in range(4):
                        pe.wait_ge(sub_sq, 4 * ph["diff"] + i + 1)
                        pe.matmul(DB[i], ones[:, :], sq[:, 2 * i:2 * i + 2, :].rearrange("p a b -> p (a b)"),
                                  start=True, stop=True, skip_group_check=True).then_inc(sub_ss, 1)
                if ph.get("moba"):
                    pe.wait_ge(win_ok, 4)
                    pe.wait_ge(s_misc, 48)
                    pe.wait_ge(biased, ph["sg"] + G)
                    for g in range(4):
                        src = (win_a, win_b)[g % 2][:, g, :]
                        ins = pe.matmul(DB[g // 2][:, (g % 2) * T:(g % 2 + 1) * T], poolw[:, g, :], src, start=g % 2 == 0,
                                        stop=True, skip_group_check=True)
                    ins.then_inc(poolmix_done, 1)

            def stick(ph):
                a = ph["act"]
                for half in range(2):
                    k0 = ph["kg"] + 4 * half

                    def zT(g):
                        if g == 0 and half == 0:
                            pe.wait_ge(u_free, ph["u"])
                        if g >= 2:
                            pe.wait_ge(t_exp, k0 + g - 1)
                        elif half:
                            pe.wait_ge(z_less, k0)
                        for s in range(2):
                            m = 8 * half + 2 * g + s
                            q, k = score_operands(ph, m)
                            o = DB[2 * (g % 2) + s]
                            pe.matmul(o[:, 0:T], k[:, 0:P], q, start=True, stop=True, skip_group_check=True)
                            ins = pe.matmul(o[:, T:3 * P], k[:, P:T], q[:, P:T], start=True, stop=True,
                                            skip_group_check=True)
                        ins.then_inc(z_done, 1)

                    def suffix(g):
                        pe.wait_ge(sp_ready, k0 + g + 1)
                        if g < 2:
                            pe.wait_ge(t_exp, k0 + 4)
                        else:
                            pe.wait_ge(z_less, k0 + g - 1)
                        for s in range(2):
                            t = tbuf[:, 2 * g + s, :]
                            o = DB[2 * (g % 2) + s]
                            pe.matmul(o[:, 0:T], upper[:, :], t[:, 0:T], start=True, stop=False, skip_group_check=True)
                            pe.matmul(o[:, P:T], ones[:, :], t[:, T:3 * P], start=False, stop=True, skip_group_check=True)
                            ins = pe.matmul(o[:, T:3 * P], upper[:, :], t[:, T:3 * P], start=False, stop=True,
                                            skip_group_check=True)
                        ins.then_inc(cs_done, 1)

                    def values(g):
                        pe.wait_ge(a_ready, k0 + g + 1)
                        if half:
                            pe.wait_ge(act_lo[a], 8 * ph["fill"] + g + 1)
                        for s in range(2):
                            m = 8 * half + 2 * g + s
                            z = zbuf[:, 2 * g + s, :]
                            o = UB[g][s * HD:(s + 1) * HD, 0:T]
                            pe.matmul(o, v[:, 0, m * HD:(m + 1) * HD], z[:, 0:T], start=True, stop=False,
                                      skip_group_check=True)
                            ins = pe.matmul(o[:, P:T], v[:, 1, m * HD:(m + 1) * HD], z[:, T:3 * P], start=False, stop=True,
                                            skip_group_check=True)
                        ins.then_inc(spv_done, 1)

                    for g in range(4):
                        zT(g)
                    for g in range(4):
                        suffix(g)
                    for g in range(4):
                        values(g)

            pe.wait_ge(s_const, 2)
            pe.wait_ge(s_xin, 16)
            for c in range(KC):
                for q in range(QB):
                    ins = pe.transpose(DB[c // 2][:, (c % 2) * T + q * P:(c % 2) * T + (q + 1) * P],
                                       x_rows[:, q, c * P:(c + 1) * P], ident[:, :])
                if c % 2:
                    ins.then_inc(s_setup_pe, 1)
            pe.wait_ge(s_gin, 16 * 14)
            for c in range(KC):
                ins = pe.transpose(UB[0][:, c * NG:(c + 1) * NG], gain_rows[:, c * P:(c + 1) * P], ident[0:NG, 0:NG])
            ins.then_inc(s_setup_pe, 1)

            def setup_rest():
                pe.wait_ge(s_tab_in, 32)
                pe.wait_ge(x_ready, 4)
                pe.matmul(DB[0][0:16, 0:TW], kT[0:N_BUCKETS, 0, 0:16],
                          kT[0:N_BUCKETS, 2:4, :].rearrange("p a b -> p (a b)")[:, 0:TW], start=True, stop=True,
                          skip_group_check=True).then_inc(s_setup_pe, 1)
                pe.wait_ge(s_cin, 32)
                last = (F1 - (NSTEP - 1) * 2 * P) // 2
                for j in range(NCH):
                    at = j * P if j < NCH - 1 else (NCH - 2) * P + last
                    ins = pe.transpose(DB[1 + j // NSTEP][:, (j % NSTEP) * 32:(j % NSTEP) * 32 + 32],
                                       conv_rows[:, at:at + P], ident[0:32, 0:32])
                ins.then_inc(s_setup_pe, 1)

            pe.wait_ge(s_gain, 1)
            for ph in phases:
                if ph["kind"] == "lin":
                    linear(ph)
                elif ph["kind"] == "ffn":
                    ffn(ph)
                elif ph["kind"] == "soft":
                    softmax(ph)
                elif ph["kind"] == "stick":
                    stick(ph)
                elif ph["kind"] == "post":
                    square_total_by_chunk(ph)
                elif ph["kind"] == "prep" and ph["src"] == "mem":
                    pe.wait_ge(s_mem_in, 16)
                    for c in range(KC):
                        for q in range(QB):
                            ins = pe.transpose(DB[c // 2][:, (c % 2) * T + q * P:(c % 2) * T + (q + 1) * P],
                                               x_rows[:, q, c * P:(c + 1) * P], ident[:, :])
                        if c % 2:
                            ins.then_inc(s_memT, 1)
            pe.wait_ge(x_ready, total["x"])
            for c in range(KC):
                for q in range(QB):
                    at = q * D + c * P
                    ins = pe.transpose(DB[at // 512][:, at % 512:at % 512 + P], x[:, c, q * P:(q + 1) * P], ident[:, :])
            ins.then_inc(s_outT, 1)

        @block.vector
        def _(dve):
            links = [0]

            def link(ins):
                links[0] += 1
                ins.then_inc(dve_link, 1)
                dve.wait_ge(dve_link, links[0])

            def split(a, s=0):
                if a % RING != 2 and a < NBLOCKS:
                    dve.wait_ge(hi_ready, a + 1 + RING * s)
                    dve.tensor_tensor(w_lo[:, a % RING, :], raw[:, a % RING, :], w_hi[:, a % RING, :].bitcast(F32),
                                      ALU.subtract).then_inc(lo_dve, 1)

            def invert(si, r):
                dve.wait_ge(sd_ready, si + 1)
                dve.reciprocal(r_all[:, r, :], sd[:, :]).then_inc(r_ready, 1)
                dve.wait_ge(r_ready, si + 1)

            def pairs(ap):
                return ap.rearrange("p (c t) -> p c t", c=2)

            def linear(ph):
                def take(i):
                    typ, _, _, j = ph["blocks"][i]
                    b, u = ph["n"] + i, ph["u"] + i
                    if typ == "v" and ("v" not in (t[0] for t in ph["blocks"][:i])):
                        if ph["n"] == 0:
                            dve.wait_ge(s_tab_out, 16)
                        dve.wait_ge(rT_done, rT_count[ph["n"]])
                        dve.tensor_copy(rT[:, :], DB[3][:, T:T + QB]).then_inc(rT_ready, 1)
                        dve.wait_ge(rT_ready, rT_count[ph["n"]])
                    dve.wait_ge(blocks_done, b + 1)
                    o = UB[u % 4]
                    r = r_all[:, ph["r"], :]
                    if typ in ("q", "k", "pool"):
                        dst = {"q": qT, "k": kT, "pool": pin}[typ][:, 2 * j:2 * j + 2, :]
                        dve.tensor_tensor(dst, pairs(o), both(r), ALU.mult).then_inc(u_free, 1)
                    elif typ == "kdup":
                        for g in range(4):
                            for h in range(2):
                                ins = dve.tensor_tensor(kT[h * HD:(h + 1) * HD, g, :],
                                                        o[(g % 2) * HD:(g % 2 + 1) * HD, (g // 2) * T:(g // 2 + 1) * T],
                                                        r[h * HD:(h + 1) * HD, :], ALU.mult)
                        ins.then_inc(u_free, 1)
                    elif typ == "v":
                        for q in range(QB):
                            ins = dve.tensor_scalar(v[:, q, j * BW:(j + 1) * BW], o[:, q * T:(q + 1) * T], rT[:, q:q + 1],
                                                    None, ALU.mult)
                        ins.then_inc(u_free, 1)
                    elif typ == "proj":
                        xs = x[:, 2 * j:2 * j + 2, :]
                        dve.tensor_tensor(xs, pairs(o), xs, ALU.add).then_inc(x_ready, 1)
                    elif typ == "y":
                        dve.tensor_copy(y[:, 2 * j:2 * j + 2, :], pairs(o)).then_inc(y_ready, 1)

                for i in range(len(ph["blocks"])):
                    b = ph["n"] + i
                    if i == 0:
                        split(b + 2)
                    if i < len(ph["blocks"]) - 1:
                        split(b + 3)
                    if ph["stat"] is None:
                        take(i)
                    elif i:
                        if i == 1:
                            invert(ph["stat"], ph["r"])
                            take(0)
                        take(i)
                    if b == 1:
                        setup_rest()
                    if "then" in ph:
                        lo_pair(ph["then"], x, i)

            def lo_pair(ph, src, i):
                a = ph["act"]
                for c in (2 * i, 2 * i + 1):
                    dve.wait_ge(act_hi[a], 8 * ph["fill"] + c + 1)
                    dve.scalar_tensor_tensor(out=a_lo[a][:, c, :], in0=src[:, c, :],
                                             scalar=gains[:, c, ph["gain"]:ph["gain"] + 1],
                                             in1=a_hi[a][:, c, :].bitcast(F32), op0=ALU.mult, op1=ALU.subtract)\
                        .then_inc(act_lo[a], 1)

            def prep(ph):
                if ph["src"] == "mem":
                    for i in range(4):
                        dve.wait_ge(s_memT, i + 1)
                        dve.tensor_copy(memT[:, 2 * i:2 * i + 2, :], pairs(DB[i])).then_inc(s_mem_ok, 1)
                    for i in range(4):
                        lo_pair(ph, memT, i)

            def chunk_pairs(ph, finish):
                for i in range(4):
                    finish(i)
                    if i and "then" in ph:
                        lo_pair(ph["then"], x, i - 1)
                if "then" in ph:
                    lo_pair(ph["then"], x, 3)

            def post(ph):
                invert(ph["stat"], 0)
                r = r_all[:, 0, :]

                def finish(i):
                    for c in (2 * i, 2 * i + 1):
                        g = gains[:, c, ph["gain"]:ph["gain"] + 1]
                        dst = x if ph["src"] == "x" else y
                        ins = dve.scalar_tensor_tensor(out=dst[:, c, :], in0=dst[:, c, :], scalar=g, in1=r, op0=ALU.mult,
                                                       op1=ALU.mult)
                    if ph["src"] == "y":
                        link(ins)
                        c = slice(2 * i, 2 * i + 2)
                        ins = dve.tensor_tensor(x[:, c, :], x[:, c, :], y[:, c, :], ALU.add)
                    ins.then_inc(x_ready, 1)

                chunk_pairs(ph, finish)

            def ffn(ph):
                def up(s0, s):
                    b = up_block(ph, s0, 0)
                    if s0 == 0:
                        split(b + 2)
                    split(b + 3, s)
                    split(b + 4, s)
                    if s0 == 0:
                        invert(ph["stat"], 0)
                    n = cols(ph, s0)
                    for c in range(2):
                        f, u = ph["f"] + 2 * s0 + c, ph["u"] + 2 * s0 + c
                        if c == 0:
                            dve.wait_ge(half_done, ph["hd"] + s0 + 1 + s)
                        else:
                            dve.wait_ge(blocks_done, b + 2 + 3 * s)
                        if f >= 2:
                            dve.wait_ge(hid_ready, f - 1 + 2 * s)
                        dve.tensor_tensor(us[0:n, c, :, :], pairs(UB[u % 4])[0:n], both(r_all[0:n, 0, :]), ALU.mult)\
                            .then_inc(u_free, 1)
                    if ph["conv"] is not None:
                        for c in range(2):
                            f = ph["f"] + 2 * s0 + c
                            at = (2 * s0 + c) * 32
                            for tap, done in ((1, conv_t1), (0, conv_t0)):
                                sh = 2 - tap
                                for h in range(2):
                                    dve.wait_ge(conv_acc if tap else conv_t1, 2 * f + h + 1 + 4 * s)
                                    rw = (ph["conv"] * 3 + tap) * 2 + h
                                    dve.scalar_tensor_tensor(
                                        out=acc[0:n, c, h, sh:T], in0=us[0:n, c, h, 0:T - sh],
                                        scalar=cw[0:n, bass.ds(at + rw + 64 * s, 1)], in1=acc[0:n, c, h, sh:T],
                                        op0=ALU.mult, op1=ALU.add).then_inc(done, 1)
                    for c in range(2):
                        f = ph["f"] + 2 * s0 + c
                        if ph["conv"] is not None:
                            dve.wait_ge(conv_t0, 2 * f + 2 + 4 * s)
                        dve.wait_ge(sil_ready, f + 1 + 2 * s)
                        if f >= 2:
                            dve.wait_ge(hl_ready, f - 1 + 2 * s)
                        val = acc[0:n, c, 1, :] if ph["conv"] is not None else us[0:n, c, 1, :]
                        dve.tensor_tensor(hid[0:n, c, :], sil[0:n, c, :], val, ALU.mult).then_inc(hid_ready, 1)

                def down(s0, s):
                    if s0 < NSTEP - 1:
                        split(down_block(ph, s0) + 3, s)

                ffn_steps(dve, up, down)
                dve.wait_ge(blocks_done, ph["n"] + 3 * NSTEP)

                def finish(i):
                    if ph["dst"] == "x":
                        xs = x[:, 2 * i:2 * i + 2, :]
                        dve.tensor_tensor(xs, pairs(DB[i]), xs, ALU.add).then_inc(x_ready, 1)
                    else:
                        dve.tensor_copy(y[:, 2 * i:2 * i + 2, :], pairs(DB[i])).then_inc(y_ready, 1)

                chunk_pairs(ph, finish)

            def softmax(ph):
                G = ph["heads"] // 2
                a = ph["act"]
                cross, moba = ph.get("cross"), ph.get("moba")
                W = 2 * T if cross else 3 * P
                A = T if cross else P

                def maxima(g):
                    sg = ph["sg"] + g
                    dve.wait_ge(scores_ready, sg + 1)
                    if g >= 3:
                        dve.wait_ge(pt_done, sg - 2)
                    S = PS[:, 2 * (g % 2):2 * (g % 2) + 2, 0:W]
                    p = prob[:, g % 3, :, 0:W]
                    if cross:
                        dve.tensor_scalar(p, S, ph["scale"], None, ALU.mult).then_inc(biased, 1)
                    else:
                        tab = bias[:, 2 * g:2 * g + 2, :]
                        dve.scalar_tensor_tensor(out=p[:, :, 0:P], in0=S[:, :, 0:P], scalar=ph["scale"],
                                                 in1=tab[:, :, P:T], op0=ALU.mult, op1=ALU.add)
                        dve.scalar_tensor_tensor(out=p[:, :, P:W], in0=S[:, :, P:W], scalar=ph["scale"],
                                                 in1=tab, op0=ALU.mult, op1=ALU.add).then_inc(biased, 1)
                    dve.wait_ge(biased, sg + 1)
                    small = sm_small[:, g % 2]
                    dve.tensor_reduce(small[:, 0, 0:2], p[:, :, 0:A], AX_X, ALU.max)
                    link(dve.tensor_reduce(small[:, 0, 2:4], p[:, :, A:W], AX_X, ALU.max))
                    if ph.get("sink"):
                        sk = both(sink[:, 2 * g:2 * g + 2])
                        mx = small[:, 0, :].rearrange("p (a b) -> p a b", a=2)
                        link(dve.tensor_tensor(mx, mx, sk, ALU.max))
                        dve.tensor_tensor(small[:, 4, :].rearrange("p (a b) -> p a b", a=2), sk, mx, ALU.subtract)
                    dve.tensor_scalar(small[:, 1, :], small[:, 0, :], -1.0, None, ALU.mult).then_inc(negmax, 1)

                def sums(g):
                    sg = ph["sg"] + g
                    dve.wait_ge(exp_ready, sg + 1)
                    if g >= 2:
                        dve.wait_ge(diag_ready, sg - 1)
                    small = sm_small[:, g % 2]
                    if ph.get("sink"):
                        link(dve.tensor_tensor(small[:, 2, :], small[:, 2, :], small[:, 4, :], ALU.add))
                    if ph.get("diff") is not None:
                        link(dve.reciprocal(small[:, 3, :], small[:, 2, :]))
                        dve.tensor_tensor(small[:, 3, :], small[:, 3, :], lam_fac[:, ph["diff"], :], ALU.mult)\
                            .then_inc(rs_ready, 1)
                    else:
                        dve.reciprocal(small[:, 3, :], small[:, 2, :]).then_inc(rs_ready, 1)

                def out_lo(g):
                    if cross:
                        for i in range(4):
                            c = 4 * g + i
                            dve.wait_ge(act_hi[a], 8 * ph["fill"] + c - c % 2 + 2)
                            dve.tensor_tensor(a_lo[a][:, c, :], UB[2 + i // 2][:, (i % 2) * T:(i % 2 + 1) * T],
                                              a_hi[a][:, c, :].bitcast(F32), ALU.subtract).then_inc(act_lo[a], 1)
                    elif ph.get("diff") is None:
                        dve.wait_ge(act_hi[a], 8 * ph["fill"] + g + 1)
                        dve.tensor_tensor(a_lo[a][:, g, :], UB[2 + g % 2][:, 0:T], a_hi[a][:, g, :].bitcast(F32),
                                          ALU.subtract).then_inc(act_lo[a], 1)

                if ph["sg"] == 0:
                    lambdas()
                if moba:
                    windows()
                if not cross:
                    dve.wait_ge(s_bias_ok, ok_count[ph["sg"]])
                for g in range(G + 3):
                    if g < G:
                        maxima(g)
                    if 1 <= g <= G:
                        sums(g - 1)
                    if g >= 3:
                        out_lo(g - 3)
                if ph.get("diff") is not None:
                    j = ph["diff"]
                    for i in range(4):
                        c = slice(2 * i, 2 * i + 2)
                        dve.wait_ge(sub_sd, 4 * j + i + 1)
                        link(dve.reciprocal(kT[:, c, :], kT[:, c, :]))
                        dve.scalar_tensor_tensor(out=y[:, c, :], in0=y[:, c, :],
                                                 scalar=gains[:, 0, G_SUBLN + j:G_SUBLN + j + 1], in1=kT[:, c, :],
                                                 op0=ALU.mult, op1=ALU.mult).then_inc(sub_t, 1)
                    for i in range(4):
                        c = slice(2 * i, 2 * i + 2)
                        dve.wait_ge(act_hi[a], 8 * ph["fill"] + 2 * i + 2)
                        dve.scalar_tensor_tensor(out=a_lo[a][:, c, :], in0=y[:, c, :],
                                                 scalar=1.0 - lambda_init(ph["layer"]),
                                                 in1=a_hi[a][:, c, :].bitcast(F32), op0=ALU.mult, op1=ALU.subtract)\
                            .then_inc(act_lo[a], 2)
                if moba:
                    for g in range(4):
                        dve.wait_ge(act_hi[a], 8 * ph["fill"] + 4 + 2 * (g // 2) + 2)
                        dve.scalar_tensor_tensor(out=a_lo[a][:, 4 + g, :], in0=DB[g // 2][:, (g % 2) * T:(g % 2 + 1) * T],
                                                 scalar=gains[:, g, G_POOL:G_POOL + 1],
                                                 in1=a_hi[a][:, 4 + g, :].bitcast(F32), op0=ALU.mult, op1=ALU.subtract)\
                            .then_inc(act_lo[a], 1)

            def windows():
                dve.wait_ge(s_bias_ok, ok_count["cnt"])
                link(dve.reciprocal(inv_cnt, inv_cnt))
                src = pin
                for i in range(4):
                    dst, sh = (win_a, win_b)[i % 2], 1 << i
                    g = slice(i, 4)
                    dve.tensor_copy(dst[:, g, 0:sh], src[:, g, 0:sh])
                    link(dve.tensor_tensor(dst[:, g, sh:T], src[:, g, sh:T], src[:, g, 0:T - sh], ALU.add))
                    src = dst
                for g in range(4):
                    w = (win_a, win_b)[g % 2][:, g, :]
                    link(dve.tensor_tensor(w, w, inv_cnt[:, g, :], ALU.mult))
                    dve.tensor_tensor(w, w, pin[:, g, :], ALU.subtract).then_inc(win_ok, 1)

            def stick(ph):
                a = ph["act"]
                for half in range(2):
                    k0 = ph["kg"] + 4 * half
                    for g in range(4):
                        dve.wait_ge(z_done, k0 + g + 1)
                        if half:
                            dve.wait_ge(spv_done, k0)
                        dve.tensor_scalar(zbuf[:, 2 * g:2 * g + 2, :], PS[:, 2 * (g % 2):2 * (g % 2) + 2, 0:3 * P],
                                          ph["scale"], None, ALU.mult).then_inc(z_copied, 1)
                    for g in range(4):
                        z, t = zbuf[:, 2 * g:2 * g + 2, :], tbuf[:, 2 * g:2 * g + 2, :]
                        dve.wait_ge(t_ln, k0 + g + 1)
                        dve.wait_ge(z_copied, k0 + g + 1)
                        dve.scalar_tensor_tensor(out=t, in0=z, scalar=0.0, in1=t, op0=ALU.max, op1=ALU.add)\
                            .then_inc(sp_sum, 1)
                    for g in range(4):
                        z = zbuf[:, 2 * g:2 * g + 2, :]
                        dve.wait_ge(cs_done, k0 + g + 1)
                        dve.tensor_tensor(z, z, PS[:, 2 * (g % 2):2 * (g % 2) + 2, 0:3 * P], ALU.subtract)\
                            .then_inc(z_less, 1)
                    for g in range(4):
                        c = 4 * half + g
                        dve.wait_ge(act_hi[a], 8 * ph["fill"] + c + 1)
                        dve.tensor_tensor(a_lo[a][:, c, :], UB[g][:, 0:T], a_hi[a][:, c, :].bitcast(F32), ALU.subtract)\
                            .then_inc(act_lo[a], 1)

            def setup_rest():
                dve.wait_ge(s_setup_pe, 6)
                dve.tensor_copy(table_sb, DB[0][0:16, 0:TW]).then_inc(s_tab, 1)
                dve.wait_ge(s_setup_pe, 7)
                dve.tensor_copy(cw[:, :].rearrange("p (a b) -> p a b", a=2), PS[:, 1:3, 0:NSTEP * 32]).then_inc(s_conv, 1)
                dve.wait_ge(s_misc, 48)
                prod = lam[:, :, 0:4:2, :]
                link(dve.tensor_tensor(prod, lam[:, :, 0:4:2, :], lam[:, :, 1:4:2, :], ALU.mult))
                dve.tensor_reduce(lam_s[:, :].rearrange("p (a b) -> p a b", a=2), prod, AX_X, ALU.add).then_inc(s_lam, 1)

            def lambdas():
                dve.wait_ge(s_lam, 2)
                dve.wait_ge(s_const, 4)
                for j, l in enumerate((0, 3)):
                    e = lam_s[:, 2 * j:2 * j + 2]
                    link(dve.tensor_tensor(lam_fac[:, j, 1:2], e[:, 1:2], e[:, 0:1], ALU.subtract))
                    for c in (3, 1):
                        link(dve.tensor_scalar(lam_fac[:, j, c:c + 1], lam_fac[:, j, 1:2], -lambda_init(l), None, ALU.add))

            dve.memset(gain_rows, 0.0).then_inc(s_rows, 1)
            dve.memset(conv_rows[:, F1:], 0.0).then_inc(s_rows, 1)
            dve.memset(eps_t[:, 0:1], EPS)
            dve.memset(eps_t[:, 1:2], EPS * MACARON ** -2)
            for i in range(4):
                dve.wait_ge(s_setup_pe, i + 1)
                dve.tensor_copy(x[:, 2 * i:2 * i + 2, :], pairs(DB[i])).then_inc(x_ready, 1)
            dve.wait_ge(s_setup_pe, 5)
            dve.tensor_copy(gains[:, :, :].rearrange("p c g -> p (c g)"), UB[0][:, 0:KC * NG]).then_inc(s_gain, 1)
            dve.wait_ge(s_gain, 1)
            split(0)
            for i in range(4):
                lo_pair(phases[0], x, i)
            split(1)

            for ph in phases:
                {"prep": prep, "post": post, "lin": linear, "ffn": ffn, "soft": softmax, "stick": stick}[ph["kind"]](ph)
            for i in range(4):
                dve.wait_ge(s_outT, 1)
                dve.tensor_copy(x_rows.rearrange("p b d -> p (b d)")[:, i * 512:(i + 1) * 512], DB[i]).then_inc(s_outc, 1)


_INS = ["x", "rel_bias", "attn_norm", "ffn_norm", "w_o", "da_w_qkv", "da_lambda", "da_subln", "sb_w_qkv", "sw_w_qkv",
        "sw_sinks", "ffn_w_up", "ffn_conv_w", "ffn_conv_b", "ffn_w_down", "final_norm", "mem_2", "ffn1_pre_g_2",
        "ffn1_w_gate_2", "ffn1_w_up_2", "ffn1_w_down_2", "ffn1_post_g_2", "mix_pre_g_2", "w_in_2", "pool_w_2",
        "pool_scale_2", "w_out_2", "mix_post_g_2", "xa_pre_g_2", "mem_g_2", "xa_wq_2", "xa_wkv_2", "xa_wo_2",
        "xa_post_g_2", "ffn2_pre_g_2", "ffn2_w_gate_2", "ffn2_w_up_2", "ffn2_w_down_2", "ffn2_post_g_2"]


def bucket_of_distance():
    dist = np.maximum(T - 1 - np.arange(TW), 0)
    half = N_BUCKETS // 2
    large = half + (np.log(np.maximum(dist, 1).astype(np.float32) / half) / math.log(MAX_DIST / half)
                    * (N_BUCKETS - half)).astype(np.int32)
    bucket = np.where(dist < half, dist, np.minimum(large, N_BUCKETS - 1))
    return (np.arange(N_BUCKETS)[:, None] == bucket[None, :]).astype(np.float32)


def kernel(**inputs):
    from concourse import bacc
    from concourse.bass_utils import run_bass_kernel_spmd

    nc = bacc.Bacc("TRN2", target_bir_lowering=False, num_devices=1)
    arrays, io = {}, {}
    for name in _INS + ["bucket_of_distance"]:
        a = bucket_of_distance() if name == "bucket_of_distance" else np.ascontiguousarray(inputs[name])
        arrays[f"in_{name}"] = a
        io[name] = nc.dram_tensor(f"in_{name}", a.shape, mybir.dt.from_np(a.dtype), kind="ExternalInput").ap()
    out = nc.dram_tensor("out_0", (1, T, D), F32, kind="ExternalOutput").ap()
    model_kernel(nc, io, out)
    r = run_bass_kernel_spmd(nc, [arrays], core_ids=[0])
    return r.results[0]["out_0"]
```

```python
import math
from contextlib import ExitStack

import numpy as np

import concourse.bass as bass
from concourse import mybir

P = 128
T = 256
D = 1024
KC = D // P
QB = T // P
BW = 256
BE = KC * BW
RING = 3
DEPTH = 4
F1, F2 = 2752, 2816
NSTEP = 11
NLOOP, LSTEPS = 2, 4
NCH = 2 * NSTEP
HD = 64
N_BUCKETS, MAX_DIST = 32, 128
NEG = -1e30
EPS = 1e-6
TW = 384
MACARON = 0.5

F32, F32R = mybir.dt.float32, mybir.dt.float32r
ALU, ACT = mybir.AluOpType, mybir.ActivationFunctionType
AX_X = mybir.AxisListType.X

G_ATTN, G_FFN, G_FINAL = 0, 4, 8
(G_FFN1_PRE, G_FFN1_POST, G_MIX_PRE, G_MIX_POST, G_XA_PRE, G_MEM, G_XA_POST, G_FFN2_PRE,
 G_FFN2_POST) = range(9, 18)
G_POOL, G_SUBLN, NG = 18, 19, 21


def lambda_init(layer):
    return 0.8 - 0.6 * math.exp(-0.3 * layer)


def dve_splits(n):
    return 2 * (n // RING) + min(n % RING, 1) + 1


def plan():
    c = dict(n=0, u=0, f=0, stat=0, tree=0, roots=0, added=0, x=4, y=0, hd=0, sg=0, fill=[0, 0], kg=0)
    out = []

    def prep(src, gain, a, r):
        out.append(dict(kind="prep", src=src, gain=gain, act=a, fill=c["fill"][a], stat=c["stat"], tree=c["tree"],
                        x=c["x"], r=r))
        c["fill"][a] += 1
        c["tree"] += 1
        c["stat"] += 1
        return c["stat"] - 1

    def lin(a, blocks, stat=None, r=0, r_of=None):
        c["roots"] += stat is not None
        out.append(dict(kind="lin", r_of=stat if r_of is None else r_of, act=a, fill=c["fill"][a] - 1, n=c["n"],
                        u=c["u"], blocks=blocks, stat=stat, r=r,
                        roots=c["roots"], x=c["x"], y=c["y"]))
        c["n"] += len(blocks)
        if blocks[0][0] == "proj":
            c["x"] += 4
        elif blocks[0][0] == "y":
            c["y"] += 4
        else:
            c["u"] += len(blocks)

    def attend(kind, a, heads, **kw):
        out.append(dict(kind=kind, act=a, fill=c["fill"][a], sg=c["sg"], kg=c["kg"], u=c["u"], heads=heads, y=c["y"],
                        stat=c["stat"], **kw))
        c["fill"][a] += 1
        if kind == "soft":
            c["sg"] += heads // 2
        if kw.get("diff") is not None:
            c["y"] += 8
        if kind == "stick":
            c["kg"] += heads // 2

    def ffn(F, a, wup, wdown, conv, dst, stat):
        out.append(dict(kind="ffn", index=c["hd"] // NSTEP, F=F, act=a, fill=c["fill"][a] - 1, n=c["n"], u=c["u"], f=c["f"], hd=c["hd"],
                        up=wup, down=wdown, conv=conv, dst=dst, stat=stat, x=c["x"], y=c["y"]))
        c["roots"] += 1
        c["n"] += 3 * NSTEP
        c["u"] += NCH
        c["f"] += NCH
        c["hd"] += NSTEP
        c[dst] += 4

    def scale_x(src, gain, weight):
        bank = 4 if out[-1]["kind"] == "ffn" else 3
        out.append(dict(kind="post", bank=bank, src=src, gain=gain, weight=weight, stat=c["stat"], x=c["x"], y=c["y"],
                        added=c["added"]))
        c["added"] += 4 if src == "y" else 0
        c["stat"] += 1
        c["roots"] += 1
        c["x"] += 4

    def qkv(w, nq, nk, nv, k="k"):
        return ([("q", w, i * BW, i) for i in range(nq)] + [(k, w, (nq + i) * BW, i) for i in range(nk)]
                + [("v", w, (nq + nk + i) * BW, i) for i in range(nv)])

    for l in range(DEPTH):
        s = prep("x", G_ATTN + l, 0, 0)
        if l % 3 == 0:
            lin(0, qkv(("da_w_qkv", l // 3), 4, 4, 4), s)
            attend("soft", 1, 16, diff=l // 3, layer=l, scale=HD ** -0.5)
        elif l % 3 == 1:
            lin(0, qkv(("sb_w_qkv", 0), 4, 4, 4), s)
            attend("stick", 1, 16, scale=HD ** -0.5)
        else:
            lin(0, qkv(("sw_w_qkv", 0), 4, 1, 1, "kdup"), s)
            attend("soft", 1, 16, sink=True, scale=HD ** -0.5)
        lin(1, [("proj", ("w_o", l), i * BW, i) for i in range(4)])
        s = prep("x", G_FFN + l, 0, 0)
        ffn(F1, 0, [("ffn_w_up", l, 0), ("ffn_w_up", l, F1)], ("ffn_w_down", l), l, "x", s)
    scale_x("x", G_FINAL, None)

    s = prep("x", G_FFN1_PRE, 0, 0)
    ffn(F2, 0, [("ffn1_w_gate_2", 0, 0), ("ffn1_w_up_2", 0, 0)], ("ffn1_w_down_2", 0), None, "y", s)
    scale_x("y", G_FFN1_POST, MACARON)
    s = prep("x", G_MIX_PRE, 0, 0)
    lin(0, [("pool", ("w_in_2", 0), (6 + i) * BW, i) for i in range(2)] + qkv(("w_in_2", 0), 2, 2, 2), s)
    attend("soft", 1, 8, moba=True, scale=HD ** -0.5)
    lin(1, [("y", ("w_out_2", 0), i * BW, i) for i in range(4)])
    s = prep("mem", G_MEM, 0, 1)
    kv = qkv(("xa_wkv_2", 0), 0, 4, 4)
    lin(0, kv[:3], s, 1)
    scale_x("y", G_MIX_POST, 1.0)
    t = prep("x", G_XA_PRE, 1, 0)
    lin(0, kv[3:], None, 1, s)
    s = t
    lin(1, [("q", ("xa_wq_2", 0), i * BW, i) for i in range(4)], s)
    attend("soft", 0, 4, cross=True, scale=256 ** -0.5)
    lin(0, [("y", ("xa_wo_2", 0), i * BW, i) for i in range(4)])
    scale_x("y", G_XA_POST, 1.0)
    s = prep("x", G_FFN2_PRE, 0, 0)
    ffn(F2, 0, [("ffn2_w_gate_2", 0, 0), ("ffn2_w_up_2", 0, 0)], ("ffn2_w_down_2", 0), None, "y", s)
    scale_x("y", G_FFN2_POST, MACARON)
    for before, ph in zip(out, out[1:]):
        if ph["kind"] == "prep" and ph["src"] == "x":
            ph["fused"] = True
            before["then"] = ph
    for i, ph in enumerate(out):
        if ph["kind"] == "post" and ph["gain"] == G_MIX_POST:
            user = next(later for later in out[i:] if later["kind"] == "lin")
            ph["ahead"] = user["n"] + 2
            user["ahead"] = True
    return out, c


def model_kernel(nc, io, out):
    phases, total = plan()
    NBLOCKS = total["n"]
    rT_count = {n: i + 1 for i, n in enumerate(ph["n"] for ph in phases
                                               if ph["kind"] == "lin" and any(b[0] == "v" for b in ph["blocks"]))}
    ok_count = {sg: i + 1 for i, sg in enumerate(ph["sg"] for ph in phases if ph["kind"] == "soft" and not ph.get("cross"))}
    ok_count["cnt"] = 5
    tree_of = {ph["stat"]: ph["tree"] for ph in phases if ph["kind"] == "prep"}
    with ExitStack() as ctx:
        def sb(name, shape, dt=F32):
            return ctx.enter_context(nc.sbuf_tensor("sb_" + name, shape, dt))

        def sem(name):
            return ctx.enter_context(nc.semaphore(name))

        raw = sb("raw", [P, RING, BE])
        w_hi = sb("w_hi", [P, RING, BE], F32R)
        w_lo = sb("w_lo", [P, RING, BE], F32R)
        x = sb("x", [P, KC, T])
        a_hi = [sb(f"a_hi{i}", [P, KC, T], F32R) for i in range(2)]
        a_lo = [sb(f"a_lo{i}", [P, KC, T], F32R) for i in range(2)]
        qT = sb("qT", [P, KC, T])
        kT = sb("kT", [P, KC, T])
        v = sb("v", [P, QB, D])
        y = sb("y", [P, KC, T])
        work = sb("work", [P, 6144])
        bias = sb("bias", [P, 16, T])
        cw = sb("cw", [P, NCH * 32])
        gains = sb("gains", [P, KC, NG])
        ident = sb("ident", [P, P])
        ones = sb("ones", [P, P])
        upper = sb("upper", [P, P])
        r_all = sb("r_all", [P, 2, T])
        warm_out = sb("warm_out", [P, 1])
        one_col = sb("one_col", [P, 15])
        sd = sb("sd", [P, T])
        rT = sb("rT", [P, QB])
        poolw = sb("poolw", [P, 4, P])
        lam = sb("lam", [P, 2, 4, HD])
        lam_s = sb("lam_s", [P, 4])
        lam_fac = sb("lam_fac", [P, 2, 4])
        sink = sb("sink", [P, 16])
        sm_small = sb("sm_small", [P, 2, 5, 4])
        hh = sb("hh", [P, 4, T], F32R)
        hl = sb("hl", [P, 4, T], F32R)
        eps_t = sb("eps_t", [P, 2])

        us = work[:, 0:1024].rearrange("p (c h t) -> p c h t", c=2, h=2)
        acc = work[:, 1024:2048].rearrange("p (c h t) -> p c h t", c=2, h=2)
        sil = work[:, 2048:2560].rearrange("p (c t) -> p c t", c=2)
        hid = work[:, 2560:3072].rearrange("p (c t) -> p c t", c=2)
        prob = work[:, 0:3072].rearrange("p (b s k) -> p b s k", b=4, s=2)
        prob_x = work[:, 0:2048].rearrange("p (b s k) -> p b s k", b=2, s=2)
        probT = work[:, 3072:5120].rearrange("p (b s k) -> p b s k", b=2, s=2)
        diag = work[:, 5120:6144].rearrange("p (b i q) -> p b i q", b=2, i=4)
        win_b = bias[:, 12:16, :]
        memT = bias[:, 0:8, :]
        zbuf = work[:, 0:3072].rearrange("p (h k) -> p h k", h=8)
        tbuf = work[:, 3072:6144].rearrange("p (h k) -> p h k", h=8)
        conv_rows = work[0:32, 0:2816]
        gain_rows = work[0:NG, 2816:3840]
        first_rows = kT[0:DEPTH, 4:8, :].rearrange("p c t -> p (c t)")
        x_rows = work[:, 4096:6144].rearrange("p (b d) -> p b d", b=QB)
        sq = qT
        head_rms = kT[0:8, 0, :]
        pin = y[:, 0:4, :]
        win_a = y[:, 4:8, :]
        inv_cnt = bias[:, 8:12, :]
        table_sb = v[0:16, 0, 0:TW]

        PS = ctx.enter_context(nc.psum_tensor("ps", [P, 8, 512], F32))
        DB = [PS[:, i, :] for i in range(4)]
        UB = [PS[:, 4 + i, :] for i in range(4)]

        bias_dram = nc.dram_tensor("bias_dram", [16, P * TW], F32)

        s_const = sem("s_const")
        s_xin = sem("s_xin")
        s_gin = sem("s_gin")
        s_first = sem("s_first")
        s_cin = sem("s_cin")
        s_rows = sem("s_rows")
        s_misc = sem("s_misc")
        s_tab_in = sem("s_tab_in")
        s_mem_in = sem("s_mem_in")
        s_setup_pe = sem("s_setup_pe")
        s_gain = sem("s_gain")
        s_conv = sem("s_conv")
        s_tab = sem("s_tab")
        s_tab_out = sem("s_tab_out")
        s_bias_in = sem("s_bias_in")
        s_bias_ok = sem("s_bias_ok")
        s_lam = sem("s_lam")
        s_memT = sem("s_memT")
        s_mem_ok = sem("s_mem_ok")
        raw_ready = [sem(f"raw_ready{i}") for i in range(RING)]
        hi_ready = sem("hi_ready")
        lo_dve = sem("lo_dve")
        lo_pool = sem("lo_pool")
        blocks_done = sem("blocks_done")
        half_done = sem("half_done")
        bank_done = sem("bank_done")
        u_free = sem("u_free")
        x_ready = sem("x_ready")
        y_ready = sem("y_ready")
        y_scaled = sem("y_scaled")
        act_hi = [sem(f"act_hi{i}") for i in range(2)]
        act_lo = [sem(f"act_lo{i}") for i in range(2)]
        sq_ready = sem("sq_ready")
        sq_tree = sem("sq_tree")
        sq_sum = sem("sq_sum")
        ss_done = sem("ss_done")
        sd_ready = sem("sd_ready")
        r_ready = sem("r_ready")
        rT_done = sem("rT_done")
        rT_ready = sem("rT_ready")
        post_t = sem("post_t")
        conv_acc = sem("conv_acc")
        conv_t1 = sem("conv_t1")
        conv_t0 = sem("conv_t0")
        sil_ready = sem("sil_ready")
        hid_ready = sem("hid_ready")
        hh_ready = sem("hh_ready")
        hl_ready = sem("hl_ready")
        scores_ready = sem("scores_ready")
        biased = sem("biased")
        negmax = sem("negmax")
        exp_ready = sem("exp_ready")
        sink_exp = sem("sink_exp")
        rs_ready = sem("rs_ready")
        diag_ready = sem("diag_ready")
        pt_done = sem("pt_done")
        pt_ready = sem("pt_ready")
        pv_done = sem("pv_done")
        sub_sq = sem("sub_sq")
        sub_ss = sem("sub_ss")
        sub_sd = sem("sub_sd")
        warm_done = sem("warm_done")
        sub_r = sem("sub_r")
        sub_b = sem("sub_b")
        sub_t = sem("sub_t")
        win_ok = sem("win_ok")
        poolmix_done = sem("poolmix_done")
        z_done = sem("z_done")
        z_copied = sem("z_copied")
        t_exp = sem("t_exp")
        t_ln = sem("t_ln")
        sp_sum = sem("sp_sum")
        sp_ready = sem("sp_ready")
        cs_done = sem("cs_done")
        z_less = sem("z_less")
        a_exp = sem("a_exp")
        a_ready = sem("a_ready")
        spv_done = sem("spv_done")
        dve_link = sem("dve_link")
        act_link = sem("act_link")
        pool_link = sem("pool_link")
        s_outT = sem("s_outT")
        s_outc = sem("s_outc")
        s_out = sem("s_out")

        block = ctx.enter_context(nc.Block())

        def both(ap, n=2):
            return ap.unsqueeze(1).to_broadcast([ap.shape[0], n, ap.shape[1]])

        def wait_block(eng, a, s=0):
            if a % RING == 2:
                eng.wait_ge(lo_pool, a // RING + 1 + s)
            else:
                eng.wait_ge(lo_dve, dve_splits(a) + 2 * s)

        def up_block(ph, s0, part):
            return ph["n"] + part if s0 == 0 else ph["n"] + 3 * s0 - 1 + part

        def down_block(ph, s0):
            return ph["n"] + (3 * NSTEP - 1 if s0 == NSTEP - 1 else 3 * s0 + 4)

        def turn_lag(ph):
            return 2 if ph.get("cross") else 3

        def prob_of(ph, g):
            if ph.get("cross"):
                return prob_x[:, g % 2]
            return prob[:, g % 4]

        def cols(ph, s0):
            return (ph["F"] - (NSTEP - 1) * 2 * P) // 2 if s0 == NSTEP - 1 else P

        def ffn_steps(eng, up, down):
            up(0, 0)
            with eng.Fori(0, NLOOP) as i:
                for d in range(LSTEPS):
                    up(d + 1, LSTEPS * i)
                    down(d, LSTEPS * i)
            for s in range(LSTEPS * NLOOP, NSTEP - 1):
                up(s + 1, 0)
                down(s, 0)
            down(NSTEP - 1, 0)

        @block.sync
        def _(sp):
            def load(a, s, dst, src):
                if a >= RING:
                    wait_block(sp, a - RING, s)
                sp.dma_start(dst, src).then_inc(raw_ready[a % RING], 16)

            def slot(a, k):
                return raw[:, a % RING, :].rearrange("p (k n) -> p k n", k=k)

            def small_loads():
                sp.wait_ge(s_rows, 2)
                sp.dma_start(gain_rows[4:8, :], io["ffn_norm"]).then_inc(s_gin, 16)
                sp.dma_start(gain_rows[8:9, :], io["final_norm"].unsqueeze(0)).then_inc(s_gin, 16)
                for i, name in enumerate(("ffn1_pre_g_2", "ffn1_post_g_2", "mix_pre_g_2", "mix_post_g_2", "xa_pre_g_2",
                                          "mem_g_2", "xa_post_g_2", "ffn2_pre_g_2", "ffn2_post_g_2")):
                    sp.dma_start(gain_rows[9 + i:10 + i, :], io[name]).then_inc(s_gin, 16)
                sp.dma_start(gain_rows[18:19, 0:512], io["pool_scale_2"]).then_inc(s_gin, 16)
                sp.dma_start(gain_rows[19:21, 0:P], io["da_subln"]).then_inc(s_gin, 16)
                sp.dma_start(conv_rows[0:24, 0:F1], io["ffn_conv_w"].rearrange("l w (h f) -> (l w h) f", h=2))\
                    .then_inc(s_cin, 16)
                sp.dma_start(conv_rows[24:32, 0:F1], io["ffn_conv_b"].rearrange("l (h f) -> (l h) f", h=2))\
                    .then_inc(s_cin, 16)
                sp.dma_start(kT[0:N_BUCKETS, 0, 0:16], io["rel_bias"]).then_inc(s_tab_in, 16)
                sp.dma_start(kT[0:N_BUCKETS, 2:4, :].rearrange("p a b -> p (a b)")[:, 0:TW], io["bucket_of_distance"])\
                    .then_inc(s_tab_in, 16)
                sp.dma_start(lam[:, :, :, :].rearrange("p a b c -> p (a b c)"),
                              io["da_lambda"].rearrange("a b c -> (a b c)").unsqueeze(0).to_broadcast([P, 2 * 4 * HD]))\
                    .then_inc(s_misc, 16)
                sp.dma_start(sink[:, :], io["sw_sinks"].to_broadcast([P, 16])).then_inc(s_misc, 16)
                sp.dma_start(poolw[:, :, :], io["pool_w_2"][0].rearrange("g c d -> c g d")).then_inc(s_misc, 16)

            sp.dma_start(x_rows, io["x"][0].rearrange("(b p) d -> p b d", p=P)).then_inc(s_xin, 16)
            for ph in phases:
                if ph["kind"] == "lin":
                    for i, (_, (w, l), c0, _) in enumerate(ph["blocks"]):
                        if ph["n"] + i == RING:
                            small_loads()
                        src = io[w][l][:, c0:c0 + BW].rearrange("(k p) n -> p k n", p=P)
                        load(ph["n"] + i, 0, slot(ph["n"] + i, KC), src)
                elif ph["kind"] == "ffn":
                    def up(s0, s, ph=ph):
                        n = cols(ph, s0)
                        for part in range(2):
                            w, l, c0 = ph["up"][part]
                            b = up_block(ph, s0, part)
                            src = io[w][l][:, bass.ds(c0 + 2 * P * s0 + 2 * P * s, 2 * n)]
                            load(b, s, slot(b, KC)[:, :, 0:2 * n], src.rearrange("(k p) n -> p k n", p=P))

                    def down(s0, s, ph=ph):
                        n = cols(ph, s0)
                        w, l = ph["down"]
                        b = down_block(ph, s0)
                        src = io[w][l][bass.ds(2 * P * s0 + 2 * P * s, 2 * n), :]
                        load(b, s, slot(b, 2)[0:n, :, :], src.rearrange("(k p) n -> p k n", p=n))

                    ffn_steps(sp, up, down)
                elif ph.get("moba"):
                    moba_lo = 8 * (ph["fill"] + 1)
                elif ph.get("src") == "mem":
                    sp.wait_ge(act_lo[1], moba_lo)
                    sp.dma_start(x_rows, io["mem_2"][0].rearrange("(b p) d -> p b d", p=P)).then_inc(s_mem_in, 16)
            sp.wait_ge(s_outc, 4)
            sp.dma_start(out[0].rearrange("(b p) d -> p b d", p=P), x_rows).then_inc(s_out, 16)
            sp.wait_ge(s_out, 16)

        def make_alibi(pool, link):
            dist = y[:, 0, :]
            idx = y[:, 1, :].bitcast(mybir.dt.int32)
            link(pool.iota(idx, pattern=[[-1, T]], base=P, channel_multiplier=1))
            link(pool.tensor_copy(dist, idx))
            for h in range(8):
                ins = pool.tensor_scalar(bias[:, h, :], dist, -2.0 ** -(h + 1), None, ALU.mult)
            link(ins)
            pool.affine_select(out=bias[:, 0:8, P:T], in_=bias[:, 0:8, P:T], compare_op=ALU.is_ge, fill=NEG, base=0,
                               pattern=[[0, 8], [-1, P]], channel_multiplier=1).then_inc(s_bias_ok, 1)
            link(pool.iota(idx, pattern=[[1, T]], base=1, channel_multiplier=0))
            link(pool.tensor_copy(dist, idx))
            for g in range(4):
                ins = pool.tensor_scalar(inv_cnt[:, g, :], dist, float(2 << g), None, ALU.min)
            ins.then_inc(s_bias_ok, 1)

        @block.gpsimd
        def _(pool):
            links = [0]

            def link(ins):
                links[0] += 1
                ins.then_inc(pool_link, 1)
                pool.wait_ge(pool_link, links[0])

            def split(a, s=0):
                if a % RING == 2 and a < NBLOCKS:
                    pool.wait_ge(hi_ready, a + 1 + RING * s)
                    pool.tensor_tensor(w_lo[:, 2, :], raw[:, 2, :], w_hi[:, 2, :].bitcast(F32), ALU.subtract)\
                        .then_inc(lo_pool, 1)

            def causal(ap, heads, op, fill):
                return pool.affine_select(out=ap, in_=ap, compare_op=op, fill=fill, base=0,
                                          pattern=[[0, heads], [-1, P]], channel_multiplier=1)

            def anticausal(ap, heads):
                return pool.affine_select(out=ap, in_=ap, compare_op=ALU.is_gt, fill=0.0, base=0,
                                          pattern=[[0, heads], [1, P]], channel_multiplier=-1)

            link(pool.memset(ident[:, :], 0.0))
            pool.affine_select(out=ident[:, :], in_=ident[:, :], compare_op=ALU.not_equal, fill=1.0, base=0,
                               pattern=[[-1, P]], channel_multiplier=1).then_inc(s_const, 1)
            pool.memset(ones[:, :], 1.0).then_inc(s_const, 1)
            link(pool.memset(upper[:, :], 1.0))
            pool.affine_select(out=upper[:, :], in_=upper[:, :], compare_op=ALU.is_ge, fill=0.0, base=0,
                               pattern=[[-1, P]], channel_multiplier=1).then_inc(s_const, 1)
            link(pool.memset(one_col[:, :], 0.0))
            pool.memset(one_col[:, 7:8], 1.0)
            pool.memset(lam_fac[:, :, :], 1.0).then_inc(s_const, 1)

            def mask_bias():
                causal(bias[:, :, P:T], 16, ALU.is_ge, NEG).then_inc(s_bias_ok, 1)

            def square_sum(ph):
                si, k = ph["stat"], ph["tree"]
                for i in range(4):
                    pool.wait_ge(sq_ready, 4 * si + i + 1)
                    if i >= 2:
                        pool.wait_ge(sq_tree, 3 * k + i - 1)
                    if i:
                        pool.tensor_tensor(sq[:, 0:2, :], sq[:, 0:2, :], sq[:, 2 * i:2 * i + 2, :], ALU.add)\
                            .then_inc(sq_tree, 1)
                pool.wait_ge(sq_tree, 3 * k + 3)
                pool.tensor_tensor(sq[:, 0, :], sq[:, 0, :], sq[:, 1, :], ALU.add).then_inc(sq_sum, 1)

            def load_bias():
                src = bass.AP(bias_dram, 127, [[TW - 1, P], [P * TW, 16], [1, T]])
                pool.dma_start(bias[:, :, :], src).then_inc(s_bias_in, 16)

            for ph in phases:
                kind = ph["kind"]
                if kind == "post":
                    if "ahead" in ph:
                        split(ph["ahead"])
                    if ph["src"] == "y":
                        for i in range(4):
                            c = slice(2 * i, 2 * i + 2)
                            pool.wait_ge(y_scaled, ph["added"] + i + 1)
                            pool.tensor_tensor(x[:, c, :], x[:, c, :], y[:, c, :], ALU.add).then_inc(x_ready, 1)
                elif kind == "prep":
                    square_sum(ph)
                elif kind == "lin":
                    for i in range(len(ph["blocks"])):
                        b = ph["n"] + i
                        if i == 0 and "ahead" not in ph:
                            split(b + 2)
                        if i < len(ph["blocks"]) - 1:
                            split(b + 3)
                        if b == 3:
                            pool.wait_ge(s_tab, 1)
                            pool.dma_start(bias_dram[:, :].rearrange("h (q z) -> h q z", q=P),
                                           table_sb.unsqueeze(1).to_broadcast([16, P, TW])).then_inc(s_tab_out, 16)
                        if b == 6:
                            pool.wait_ge(s_tab_out, 16)
                            load_bias()
                    if ph["n"] == 0:
                        pool.wait_ge(s_bias_in, 16)
                        mask_bias()
                elif kind == "soft":
                    for g in range(ph["heads"] // 2):
                        pool.wait_ge(rs_ready, ph["sg"] + g + 1)
                        if g >= 2:
                            pool.wait_ge(pt_done, ph["sg"] + g - 1)
                        for i in range(4):
                            ins = pool.tensor_scalar(diag[:, g % 2, i, :], ident[:, :], sm_small[:, g % 2, 3, i:i + 1],
                                                     None, ALU.mult)
                        ins.then_inc(diag_ready, 1)
                elif kind == "stick":
                    for half in range(2):
                        for g in range(4):
                            pool.wait_ge(sp_sum, ph["kg"] + 4 * half + g + 1)
                            anticausal(tbuf[:, 2 * g:2 * g + 2, 0:P], 2)
                            anticausal(tbuf[:, 2 * g:2 * g + 2, 2 * P:3 * P], 2).then_inc(sp_ready, 1)
                        for g in range(4):
                            pool.wait_ge(a_exp, ph["kg"] + 4 * half + g + 1)
                            anticausal(zbuf[:, 2 * g:2 * g + 2, 0:P], 2)
                            anticausal(zbuf[:, 2 * g:2 * g + 2, 2 * P:3 * P], 2).then_inc(a_ready, 1)
                elif kind == "ffn":
                    def hidden(s0, s, ph=ph):
                        n = cols(ph, s0)
                        for c in range(2):
                            f = ph["f"] + 2 * s0 + c
                            at = 2 * (s0 % 2) + c
                            pool.wait_ge(hh_ready, f + 1 + 2 * s)
                            pool.tensor_tensor(hl[0:n, at, :], hid[0:n, c, :], hh[0:n, at, :].bitcast(F32),
                                               ALU.subtract).then_inc(hl_ready, 1)

                    def up(s0, s, ph=ph):
                        b = up_block(ph, s0, 0)
                        if s0 == 0 and "ahead" not in ph:
                            split(b + 2)
                        split(b + 3, s)
                        split(b + 4, s)
                        hidden(s0, s)

                    def down(s0, s, ph=ph):
                        if s0 < NSTEP - 1:
                            split(down_block(ph, s0) + 3, s)

                    ffn_steps(pool, up, down)
                    if ph["conv"] == 1:
                        pool.affine_select(out=bias[:, :, 0:P], in_=bias[:, :, 0:P], compare_op=ALU.is_gt, fill=NEG,
                                           base=0, pattern=[[0, 16], [1, P]], channel_multiplier=-1)\
                            .then_inc(s_bias_ok, 1)
                    if ph["conv"] == 2:
                        load_bias()
                        pool.wait_ge(s_bias_in, 32)
                        mask_bias()
                    if ph["conv"] == 3:
                        make_alibi(pool, link)

        warmed = [0]

        def warm(act, func):
            if warmed[0]:
                act.wait_ge(warm_done, warmed[0])
            warmed[0] += 1
            act.activation(warm_out[:, :], ones[:, 0:1], func).then_inc(warm_done, 1)

        def softmax_act(act, ph):
            G = ph["heads"] // 2
            a = ph["act"]
            W = T * 2 if ph.get("cross") else 3 * P
            A = T if ph.get("cross") else P

            warm(act, ACT.Exp)
            if ph["sg"] == 0:
                act.wait_ge(s_gain, 2)
                act.wait_ge(s_conv, 1)
                act.wait_ge(s_lam, 1)
                act.activation(lam_s[:, :], lam_s[:, :], ACT.Exp).then_inc(s_lam, 1)

            def exps(g):
                sg = ph["sg"] + g
                act.wait_ge(negmax, sg + 1)
                small = sm_small[:, g % 2]
                for i in range(4):
                    s, lo, hi = i % 2, (0, A)[i // 2], (A, W)[i // 2]
                    p = prob_of(ph, g)[:, s, lo:hi]
                    ins = act.activation(p, p, ACT.Exp, bias=small[:, 1, i:i + 1], accum_out=small[:, 2, i:i + 1])
                if ph.get("sink"):
                    ins = act.activation(small[:, 4, :], small[:, 4, :], ACT.Exp)
                ins.then_inc(exp_ready, 1)

            def copy_pt(g):
                sg = ph["sg"] + g
                act.wait_ge(pt_done, sg + 1)
                if g >= 2:
                    act.wait_ge(pv_done, sg - 1)
                if ph.get("diff") is not None:
                    act.activation(probT[:, g % 2, 0, 0:W], UB[0][:, 0:W], ACT.Copy).then_inc(pt_ready, 1)
                else:
                    act.activation(probT[:, g % 2, :, 0:W], PS[:, 4:6, 0:W], ACT.Copy).then_inc(pt_ready, 1)

            def out_hi(g):
                sg = ph["sg"] + g
                act.wait_ge(pv_done, sg + 1)
                if ph.get("diff") is not None:
                    act.activation(y[:, g, :], UB[2 + g % 2][:, 0:T], ACT.Copy).then_inc(y_ready, 1)
                    act.activation(sq[:, g, :], UB[2 + g % 2][:, 0:T], ACT.Square).then_inc(sub_sq, 1)
                elif ph.get("cross"):
                    for i in range(4):
                        act.activation(a_hi[a][:, 4 * g + i, :], UB[2 + i // 2][:, (i % 2) * T:(i % 2 + 1) * T],
                                       ACT.Copy).then_inc(act_hi[a], 1)
                else:
                    act.activation(a_hi[a][:, g, :], UB[2 + g % 2][:, 0:T], ACT.Copy).then_inc(act_hi[a], 1)

            lag = turn_lag(ph)
            for g in range(G + lag + 1):
                if lag <= g < G + lag:
                    copy_pt(g - lag)
                if g < G:
                    exps(g)
                if g > lag:
                    out_hi(g - lag - 1)
            if ph.get("diff") is not None:
                j = ph["diff"]
                warm(act, ACT.Sqrt)
                act.wait_ge(sub_ss, 8 * j + 8)
                act.activation(head_rms, UB[1][0:8, 0:T], ACT.Sqrt, scale=1.0 / P, bias=eps_t[0:8, 0:1])\
                    .then_inc(sub_sd, 1)
                for i in range(4):
                    act.wait_ge(sub_t, 4 * j + i + 1)
                    act.activation(a_hi[a][:, 2 * i:2 * i + 2, :], y[:, 2 * i:2 * i + 2, :], ACT.Copy,
                                   scale=1.0 - lambda_init(ph["layer"])).then_inc(act_hi[a], 2)
            if ph.get("moba"):
                act.wait_ge(poolmix_done, 1)
                for g in range(4):
                    act.activation(a_hi[a][:, 4 + g, :], DB[g // 2][:, (g % 2) * T:(g % 2 + 1) * T], ACT.Copy,
                                   scale=gains[:, g, G_POOL:G_POOL + 1]).then_inc(act_hi[a], 1)

        def stick_act(act, ph):
            a = ph["act"]
            for half in range(2):
                k0 = ph["kg"] + 4 * half
                if half == 0:
                    warm(act, ACT.Exp)
                for g in range(4):
                    act.wait_ge(z_done, k0 + g + 1)
                    act.wait_ge(z_copied, k0 + g + 1)
                    S = PS[:, 2 * (g % 2):2 * (g % 2) + 2, 0:3 * P]
                    t = tbuf[:, 2 * g:2 * g + 2, :]
                    if half == 1:
                        act.wait_ge(cs_done, k0)
                    act.activation(t, S, ACT.Abs, scale=ph["scale"]).then_inc(act_link, 1)
                    act.wait_ge(act_link, k0 - ph["kg"] + g + 1)
                    act.activation(t, t, ACT.Exp, scale=-1.0).then_inc(t_exp, 1)
                for g in range(4):
                    t = tbuf[:, 2 * g:2 * g + 2, :]
                    act.wait_ge(t_exp, k0 + g + 1)
                    act.activation(t, t, ACT.Ln, bias=1.0).then_inc(t_ln, 1)
                warm(act, ACT.Exp)
                for g in range(4):
                    z = zbuf[:, 2 * g:2 * g + 2, :]
                    act.wait_ge(z_less, k0 + g + 1)
                    act.activation(z, z, ACT.Exp).then_inc(a_exp, 1)
                for g in range(4):
                    act.wait_ge(spv_done, k0 + g + 1)
                    act.activation(a_hi[a][:, 4 * half + g, :], UB[g][:, 0:T], ACT.Copy).then_inc(act_hi[a], 1)

        @block.scalar
        def _(act):
            act.dma_start(first_rows, io["attn_norm"]).then_inc(s_first, 16)

            def split(a, s=0):
                if a >= NBLOCKS:
                    return
                act.wait_ge(raw_ready[a % RING], 16 * (a // RING + 1) + 16 * s)
                if a >= RING:
                    act.wait_ge(blocks_done, a - RING + 1 + RING * s)
                act.activation(w_hi[:, a % RING, :], raw[:, a % RING, :], ACT.Copy).then_inc(hi_ready, 1)

            def root(si, bank=3, mul=1.0):
                act.wait_ge(ss_done, si + 1)
                if si >= 1:
                    act.wait_ge(r_ready, si)
                act.activation(sd[:, :], PS[:, bank, 0:T], ACT.Sqrt, scale=mul / D, bias=eps_ap(mul))\
                    .then_inc(sd_ready, 1)

            def hi_pair(ph, src, i):
                for c in (2 * i, 2 * i + 1):
                    act.activation(a_hi[ph["act"]][:, c, :], src[:, c, :], ACT.Copy,
                                   scale=gains[:, c, ph["gain"]:ph["gain"] + 1]).then_inc(act_hi[ph["act"]], 1)
                square_pair(src, i)

            def square_pair(src, i):
                act.activation(sq[:, 2 * i:2 * i + 2, :], src[:, 2 * i:2 * i + 2, :], ACT.Square).then_inc(sq_ready, 1)

            def prep_pair(ph, i):
                act.wait_ge(x_ready, ph["x"] - 4 + i + 1)
                hi_pair(ph, x, i)

            def eps_ap(mul):
                return eps_t[:, (0 if mul == 1.0 else 1):(1 if mul == 1.0 else 2)]

            split(0)
            act.wait_ge(s_gain, 1)
            for i in range(4):
                prep_pair(phases[0], i)
            split(1)
            for ph in phases[1:]:
                kind = ph["kind"]
                if kind == "prep" and ph["src"] == "mem":
                    for i in range(4):
                        act.wait_ge(s_mem_ok, i + 1)
                        hi_pair(ph, memT, i)
                elif kind == "post":
                    warm(act, ACT.Sqrt)
                    for i in range(4):
                        if ph["src"] == "y":
                            act.wait_ge(y_ready, ph["y"] - 4 + i + 1)
                            square_pair(y, i)
                        else:
                            act.wait_ge(x_ready, ph["x"] - 4 + i + 1)
                            square_pair(x, i)
                    if "ahead" in ph:
                        split(ph["ahead"])
                    root(ph["stat"], ph["bank"], (ph["weight"] or 1.0) ** -2)
                    for i in range(4):
                        prep_pair(ph["then"], i) if "then" in ph else None
                elif kind == "lin":
                    for i in range(len(ph["blocks"])):
                        b = ph["n"] + i
                        if i == 0 and "ahead" not in ph:
                            split(b + 2)
                        if i < len(ph["blocks"]) - 1:
                            split(b + 3)
                        if i == 1 and ph["stat"] is not None:
                            root(ph["stat"])
                        if "then" in ph:
                            prep_pair(ph["then"], i)
                elif kind == "soft":
                    softmax_act(act, ph)
                elif kind == "stick":
                    stick_act(act, ph)
                elif kind == "ffn":
                    def up(s0, s, ph=ph):
                        b = up_block(ph, s0, 0)
                        if s0 == 0 and "ahead" not in ph:
                            split(b + 2)
                        split(b + 3, s)
                        if s0 == 0:
                            root(ph["stat"])
                        n = cols(ph, s0)

                        def newest_tap(c):
                            if ph["conv"] is None:
                                return
                            u = ph["u"] + 2 * s0 + c
                            f = ph["f"] + 2 * s0 + c
                            act.wait_ge(u_free, u + 1 + 2 * s)
                            if f >= 2:
                                act.wait_ge(hid_ready, f - 1 + 2 * s)
                            for h in range(2):
                                at = (2 * s0 + c) * 32
                                rw, rb = (ph["conv"] * 3 + 2) * 2 + h, 24 + ph["conv"] * 2 + h
                                act.activation(acc[0:n, c, h, :], us[0:n, c, h, :], ACT.Identity,
                                               scale=cw[0:n, bass.ds(at + rw + 64 * s, 1)],
                                               bias=cw[0:n, bass.ds(at + rb + 64 * s, 1)]).then_inc(conv_acc, 1)

                        newest_tap(0)
                        split(b + 4, s)
                        newest_tap(1)
                        for c in range(2):
                            f = ph["f"] + 2 * s0 + c
                            if ph["conv"] is not None:
                                act.wait_ge(conv_t0, 2 * f + 1 + 4 * s)
                                src = acc[0:n, c, 0, :]
                            else:
                                act.wait_ge(u_free, ph["u"] + 2 * s0 + c + 1 + 2 * s)
                                act.wait_ge(hid_ready, f - 1 + 2 * s)
                                src = us[0:n, c, 0, :]
                            act.activation(sil[0:n, c, :], src, ACT.Silu).then_inc(sil_ready, 1)
                        for c in range(2):
                            if c == 0 and s0 >= 1:
                                act.wait_ge(blocks_done, ph["n"] + 3 * s0 - 1 + 3 * s)
                            act.wait_ge(hid_ready, ph["f"] + 2 * s0 + c + 1 + 2 * s)
                            act.activation(hh[0:n, 2 * (s0 % 2) + c, :], hid[0:n, c, :], ACT.Copy).then_inc(hh_ready, 1)

                    def down(s0, s, ph=ph):
                        if s0 < NSTEP - 1:
                            split(down_block(ph, s0) + 3, s)

                    ffn_steps(act, up, down)
                    if "then" in ph:
                        for i in range(4):
                            prep_pair(ph["then"], i)

        @block.tensor
        def _(pe):
            def product(o, hi1, lo1, hi2, lo2, start, stop):
                pe.matmul(o, hi1, hi2, start=start, stop=False, skip_group_check=True)
                pe.matmul(o, hi1, lo2, start=False, stop=False, skip_group_check=True)
                return pe.matmul(o, lo1, hi2, start=False, stop=stop, skip_group_check=True)

            def weights(a, k):
                s = a % RING
                return (w_hi[:, s, :].rearrange("p (k n) -> p k n", k=k), w_lo[:, s, :].rearrange("p (k n) -> p k n", k=k))

            def square_total(si):
                pe.wait_ge(sq_sum, tree_of[si] + 1)
                if si >= 1:
                    pe.wait_ge(sd_ready, si)
                pe.matmul(DB[3][:, 0:T], ones[:, :], sq[:, 0, :], start=True, stop=True, skip_group_check=True)\
                    .then_inc(ss_done, 1)

            def square_total_by_chunk(ph):
                pe.wait_ge(sd_ready, ph["stat"])
                for c in range(KC):
                    pe.wait_ge(sq_ready, 4 * ph["stat"] + c // 2 + 1)
                    ins = pe.matmul(PS[:, ph["bank"], 0:T], ones[:, :], sq[:, c, :], start=c == 0, stop=c == KC - 1,
                                    skip_group_check=True)
                ins.then_inc(ss_done, 1)

            def linear(ph):
                a = ph["act"]
                ah, al = a_hi[a], a_lo[a]
                turned = False
                for i, (typ, _, _, _) in enumerate(ph["blocks"]):
                    counted = typ not in ("proj", "y")
                    b, u = ph["n"] + i, ph["u"] + i
                    wait_block(pe, b)
                    if counted and u >= 4:
                        pe.wait_ge(u_free, u - 3)
                    elif i == 0:
                        pe.wait_ge(act_lo[a], 8 * (ph["fill"] + 1))
                    if typ == "v" and not turned:
                        turned = True
                        pe.wait_ge(r_ready, ph["r_of"] + 1)
                        pe.wait_ge(sd_ready, ph["roots"])
                        for q in range(QB):
                            ins = pe.matmul(DB[3][:, T + q:T + q + 1], r_all[0:1, ph["r"], q * P:(q + 1) * P],
                                            ones[0:1, 0:1], start=True, stop=True, skip_group_check=True)
                        ins.then_inc(rT_done, 1)
                    wh, wl = weights(b, KC)
                    o = UB[u % 4]
                    order = ([(j, k) for k in range(KC) for j in range(2)] if i == 0
                             else [(j, k) for j in range(2) for k in range(KC)])
                    for j, k in order:
                        if i == 0 and j == 0:
                            pe.wait_ge(act_hi[a], 8 * ph["fill"] + k + 1)
                            pe.wait_ge(act_lo[a], 8 * ph["fill"] + k + 1)
                        oj, first = o[:, j * T:(j + 1) * T], (j, k) == (0, 0)
                        js = slice(j * P, (j + 1) * P)
                        if typ == "v":
                            ins = product(oj, ah[:, k, js], al[:, k, js], wh[:, k, :], wl[:, k, :], first, k == KC - 1)
                        else:
                            ins = product(oj, wh[:, k, js], wl[:, k, js], ah[:, k, :], al[:, k, :], first, k == KC - 1)
                    ins.then_inc(blocks_done, 1)
                    if i == 1 and ph["stat"] is not None:
                        square_total(ph["stat"])
                    if b == 1:
                        setup_rest()

            def ffn(ph):
                a = ph["act"]

                def up(s0, s):
                    n = cols(ph, s0)
                    for part in range(2):
                        b = up_block(ph, s0, part)
                        wait_block(pe, b, s)
                        wh, wl = weights(b, KC)
                        first_block = s0 == 0 and part == 0
                        order = ([(c, k) for k in range(KC) for c in range(2)] if first_block
                                 else [(c, k) for c in range(2) for k in range(KC)])
                        for c, k in order:
                            u = ph["u"] + 2 * s0 + c
                            if part == 0 and k == 0:
                                pe.wait_ge(u_free, u - 3 + 2 * s)
                            if first_block and (c, k) == (1, 0):
                                pe.wait_ge(x_ready, ph["x"] - 2)
                            if first_block and c == 0:
                                pe.wait_ge(act_hi[a], 8 * ph["fill"] + k + 1)
                                pe.wait_ge(act_lo[a], 8 * ph["fill"] + k + 1)
                            cs = slice(c * n, c * n + P)
                            ins = product(UB[u % 4][:, part * T:(part + 1) * T], wh[:, k, cs], wl[:, k, cs],
                                          a_hi[a][:, k, :], a_lo[a][:, k, :], k == 0 and part == 0, k == KC - 1)
                            if part == 1 and (c, k) == (0, KC - 1):
                                ins.then_inc(half_done, 1)
                        ins.then_inc(blocks_done, 1)
                        if s0 == 0 and part == 1:
                            square_total(ph["stat"])

                def down(s0, s):
                    n = cols(ph, s0)
                    b = down_block(ph, s0)
                    wait_block(pe, b, s)
                    wh, wl = weights(b, 2)
                    last = s0 == NSTEP - 1
                    order = ([(k, m) for i in range(4) for k in range(2) for m in (2 * i, 2 * i + 1)] if last
                             else [(k, m) for k in range(2) for m in range(KC)])
                    for k, m in order:
                        at = 2 * (s0 % 2) + k
                        if m == 0:
                            pe.wait_ge(hl_ready, ph["f"] + 2 * s0 + k + 1 + 2 * s)
                        first = first_down and s0 == 0 and k == 0 and m % 2 == 0
                        ins = product(DB[m // 2][:, (m % 2) * T:(m % 2 + 1) * T], wh[0:n, k, m * P:(m + 1) * P],
                                      wl[0:n, k, m * P:(m + 1) * P], hh[0:n, at, :], hl[0:n, at, :], first,
                                      last and k == 1)
                        if last and k == 1 and m in (1, 3, 5):
                            ins.then_inc(bank_done, 1)
                    ins.then_inc(blocks_done, 1)

                first_down = True
                up(0, 0)
                up(1, 0)
                down(0, 0)
                first_down = False
                with pe.Fori(0, NLOOP) as i:
                    for d in range(LSTEPS):
                        up(d + 2, LSTEPS * i)
                        down(d + 1, LSTEPS * i)
                for st in range(LSTEPS * NLOOP + 1, NSTEP - 1):
                    up(st + 1, 0)
                    down(st, 0)
                down(NSTEP - 1, 0)

            def score_operands(ph, m, kk=0):
                if ph.get("cross"):
                    return qT[:, 2 * m + kk, :], kT[:, 2 * m + kk, :]
                ps = slice((m % 2) * HD, (m % 2 + 1) * HD)
                return qT[ps, m // 2, :], kT[ps, m // 4 if ph.get("sink") else m // 2, :]

            def softmax(ph):
                G = ph["heads"] // 2
                cross, diff = ph.get("cross"), ph.get("diff") is not None
                a = ph["act"]

                def scores(g):
                    if g == 0:
                        pe.wait_ge(u_free, ph["u"])
                    if g >= 2:
                        pe.wait_ge(biased, ph["sg"] + g - 1)
                    if cross:
                        for s in range(2):
                            o = DB[2 * (g % 2) + s]
                            for qb in range(QB):
                                for kk in range(2):
                                    q, k = score_operands(ph, 2 * g + s, kk)
                                    ins = pe.matmul(o[:, qb * T:(qb + 1) * T], q[:, qb * P:(qb + 1) * P], k,
                                                    start=kk == 0, stop=kk == 1, skip_group_check=True)
                    else:
                        for qb in range(QB):
                            for s in range(2):
                                q, k = score_operands(ph, 2 * g + s)
                                ins = pe.matmul(DB[2 * (g % 2) + s][:, qb * P:(1 + 2 * qb) * P], q[:, qb * P:(qb + 1) * P],
                                                k[:, 0:(qb + 1) * P], start=True, stop=True, skip_group_check=True)
                    ins.then_inc(scores_ready, 1)

                def turn(g):
                    pe.wait_ge(diag_ready, ph["sg"] + g + 1)
                    if g >= 1:
                        pe.wait_ge(pt_ready, ph["sg"] + g)
                    parts = [(0, 0), (2, 1), (1, 0), (3, 1)] if cross else [(0, 0), (1, 1), (2, 1)]
                    for n, (c, qb) in enumerate(parts):
                        for s in range(2):
                            o = UB[0 if diff else s][:, n * P:(n + 1) * P]
                            ins = pe.matmul(o, prob_of(ph, g)[:, s, c * P:(c + 1) * P], diag[:, g % 2, 2 * qb + s, :],
                                            start=not (diff and s), stop=not diff or s == 1, skip_group_check=True)
                    ins.then_inc(pt_done, 1)

                def values(g):
                    pe.wait_ge(pt_ready, ph["sg"] + g + 1)
                    if diff:
                        if g >= 2:
                            pe.wait_ge(sub_sq, 8 * ph["diff"] + g - 1)
                    elif cross:
                        if g >= 1:
                            pe.wait_ge(act_lo[a], 8 * ph["fill"] + 4 * g)
                    elif g >= 2:
                        pe.wait_ge(act_lo[a], 8 * ph["fill"] + g - 1)
                    for s in range(1 if diff else 2):
                        m = 2 * g + s
                        pT = probT[:, g % 2, s, :]
                        if cross:
                            for e in range(2):
                                o = UB[2 + s][:, e * T:(e + 1) * T]
                                for kb in range(2):
                                    c0 = m * T + e * P
                                    ins = pe.matmul(o, v[:, kb, c0:c0 + P], pT[:, kb * T:(kb + 1) * T], start=kb == 0,
                                                    stop=kb == 1, skip_group_check=True)
                        else:
                            w = P if diff else HD
                            c0 = g * P if diff else (m // 4 if ph.get("sink") else m) * HD
                            o = UB[2 + g % 2][s * HD:s * HD + w, 0:T]
                            pe.matmul(o, v[:, 0, c0:c0 + w], pT[:, 0:T], start=True, stop=False, skip_group_check=True)
                            ins = pe.matmul(o[:, P:T], v[:, 1, c0:c0 + w], pT[:, T:T + P], start=False, stop=True,
                                            skip_group_check=True)
                    ins.then_inc(pv_done, 1)

                def head_squares(g):
                    pe.wait_ge(sub_sq, 8 * ph["diff"] + g + 1)
                    pe.matmul(UB[1][0:8, 0:T], one_col[:, 7 - g:15 - g], sq[:, g, :], start=g == 0, stop=g == G - 1,
                              skip_group_check=True).then_inc(sub_ss, 1)

                lag = turn_lag(ph)
                for g in range(G + lag + 1):
                    if g < G:
                        scores(g)
                    if lag <= g < G + lag:
                        turn(g - lag)
                    if g > lag:
                        values(g - lag - 1)
                        if diff and g > lag + 1:
                            head_squares(g - lag - 2)
                if diff:
                    head_squares(G - 1)
                    pe.wait_ge(sub_r, ph["diff"] + 1)
                    for g in range(G):
                        pe.matmul(DB[g // 2][:, (g % 2) * T:(g % 2 + 1) * T], ident[0:8, g:g + 1].to_broadcast([8, P]),
                                  head_rms, start=g % 2 == 0, stop=True, skip_group_check=True).then_inc(sub_b, 1)
                if ph.get("moba"):
                    pe.wait_ge(win_ok, 4)
                    pe.wait_ge(s_misc, 48)
                    pe.wait_ge(biased, ph["sg"] + G)
                    for g in range(4):
                        src = (win_a, win_b)[g % 2][:, g, :]
                        ins = pe.matmul(DB[g // 2][:, (g % 2) * T:(g % 2 + 1) * T], poolw[:, g, :], src, start=g % 2 == 0,
                                        stop=True, skip_group_check=True)
                    ins.then_inc(poolmix_done, 1)

            def stick(ph):
                a = ph["act"]
                for half in range(2):
                    k0 = ph["kg"] + 4 * half

                    def zT(g):
                        if g == 0 and half == 0:
                            pe.wait_ge(u_free, ph["u"])
                        if g >= 2:
                            pe.wait_ge(t_exp, k0 + g - 1)
                        elif half:
                            pe.wait_ge(z_less, k0)
                        for s in range(2):
                            m = 8 * half + 2 * g + s
                            q, k = score_operands(ph, m)
                            o = DB[2 * (g % 2) + s]
                            pe.matmul(o[:, 0:T], k[:, 0:P], q, start=True, stop=True, skip_group_check=True)
                            ins = pe.matmul(o[:, T:3 * P], k[:, P:T], q[:, P:T], start=True, stop=True,
                                            skip_group_check=True)
                        ins.then_inc(z_done, 1)

                    def suffix(g):
                        pe.wait_ge(sp_ready, k0 + g + 1)
                        if g < 2:
                            pe.wait_ge(t_exp, k0 + 4)
                        else:
                            pe.wait_ge(z_less, k0 + g - 1)
                        for s in range(2):
                            t = tbuf[:, 2 * g + s, :]
                            o = DB[2 * (g % 2) + s]
                            pe.matmul(o[:, 0:T], upper[:, :], t[:, 0:T], start=True, stop=False, skip_group_check=True)
                            pe.matmul(o[:, P:T], ones[:, :], t[:, T:3 * P], start=False, stop=True, skip_group_check=True)
                            ins = pe.matmul(o[:, T:3 * P], upper[:, :], t[:, T:3 * P], start=False, stop=True,
                                            skip_group_check=True)
                        ins.then_inc(cs_done, 1)

                    def values(g):
                        pe.wait_ge(a_ready, k0 + g + 1)
                        if half:
                            pe.wait_ge(act_lo[a], 8 * ph["fill"] + g + 1)
                        for s in range(2):
                            m = 8 * half + 2 * g + s
                            z = zbuf[:, 2 * g + s, :]
                            o = UB[g][s * HD:(s + 1) * HD, 0:T]
                            pe.matmul(o, v[:, 0, m * HD:(m + 1) * HD], z[:, 0:T], start=True, stop=False,
                                      skip_group_check=True)
                            ins = pe.matmul(o[:, P:T], v[:, 1, m * HD:(m + 1) * HD], z[:, T:3 * P], start=False, stop=True,
                                            skip_group_check=True)
                        ins.then_inc(spv_done, 1)

                    for g in range(4):
                        zT(g)
                    for g in range(4):
                        suffix(g)
                    for g in range(4):
                        values(g)

            pe.wait_ge(s_const, 2)
            pe.wait_ge(s_first, 16)
            for c in range(KC):
                ins = pe.transpose(UB[0][:, c * DEPTH:(c + 1) * DEPTH], first_rows[:, c * P:(c + 1) * P],
                                   ident[0:DEPTH, 0:DEPTH])
            ins.then_inc(s_setup_pe, 1)
            pe.wait_ge(s_xin, 16)
            for c in range(KC):
                for q in range(QB):
                    ins = pe.transpose(DB[c // 2][:, (c % 2) * T + q * P:(c % 2) * T + (q + 1) * P],
                                       x_rows[:, q, c * P:(c + 1) * P], ident[:, :])
                if c % 2:
                    ins.then_inc(s_setup_pe, 1)

            def setup_rest():
                pe.wait_ge(s_tab_in, 32)
                pe.wait_ge(x_ready, 4)
                pe.matmul(DB[0][0:16, 0:TW], kT[0:N_BUCKETS, 0, 0:16],
                          kT[0:N_BUCKETS, 2:4, :].rearrange("p a b -> p (a b)")[:, 0:TW], start=True, stop=True,
                          skip_group_check=True).then_inc(s_setup_pe, 1)
                pe.wait_ge(s_cin, 32)
                last = (F1 - (NSTEP - 1) * 2 * P) // 2
                for j in range(NCH):
                    at = j * P if j < NCH - 1 else (NCH - 2) * P + last
                    ins = pe.transpose(DB[1 + j // NSTEP][:, (j % NSTEP) * 32:(j % NSTEP) * 32 + 32],
                                       conv_rows[:, at:at + P], ident[0:32, 0:32])
                pe.wait_ge(s_gin, 16 * 13)
                for c in range(KC):
                    at = NSTEP * 32 + (c % 4) * NG
                    ins = pe.transpose(DB[1 + c // 4][:, at:at + NG], gain_rows[:, c * P:(c + 1) * P], ident[0:NG, 0:NG])
                ins.then_inc(s_setup_pe, 1)

            pe.wait_ge(s_gain, 1)
            for ph in phases:
                if ph["kind"] == "lin":
                    linear(ph)
                elif ph["kind"] == "ffn":
                    ffn(ph)
                elif ph["kind"] == "soft":
                    softmax(ph)
                elif ph["kind"] == "stick":
                    stick(ph)
                elif ph["kind"] == "post":
                    square_total_by_chunk(ph)
                elif ph["kind"] == "prep" and ph["src"] == "mem":
                    pe.wait_ge(s_mem_in, 16)
                    for c in range(KC):
                        for q in range(QB):
                            ins = pe.transpose(DB[c // 2][:, (c % 2) * T + q * P:(c % 2) * T + (q + 1) * P],
                                               x_rows[:, q, c * P:(c + 1) * P], ident[:, :])
                        if c % 2:
                            ins.then_inc(s_memT, 1)
            pe.wait_ge(x_ready, total["x"])
            for c in range(KC):
                for q in range(QB):
                    at = q * D + c * P
                    ins = pe.transpose(DB[at // 512][:, at % 512:at % 512 + P], x[:, c, q * P:(q + 1) * P], ident[:, :])
            ins.then_inc(s_outT, 1)

        @block.vector
        def _(dve):
            links = [0]

            def link(ins):
                links[0] += 1
                ins.then_inc(dve_link, 1)
                dve.wait_ge(dve_link, links[0])

            def split(a, s=0):
                if a % RING != 2 and a < NBLOCKS:
                    dve.wait_ge(hi_ready, a + 1 + RING * s)
                    dve.tensor_tensor(w_lo[:, a % RING, :], raw[:, a % RING, :], w_hi[:, a % RING, :].bitcast(F32),
                                      ALU.subtract).then_inc(lo_dve, 1)

            def invert(si, r):
                dve.wait_ge(sd_ready, si + 1)
                dve.reciprocal(r_all[:, r, :], sd[:, :]).then_inc(r_ready, 1)
                dve.wait_ge(r_ready, si + 1)

            def pairs(ap):
                return ap.rearrange("p (c t) -> p c t", c=2)

            def linear(ph):
                def take(i):
                    typ, _, _, j = ph["blocks"][i]
                    b, u = ph["n"] + i, ph["u"] + i
                    if typ == "v" and ("v" not in (t[0] for t in ph["blocks"][:i])):
                        if ph["n"] == 0:
                            dve.wait_ge(s_tab_out, 16)
                        dve.wait_ge(rT_done, rT_count[ph["n"]])
                        dve.tensor_copy(rT[:, :], DB[3][:, T:T + QB]).then_inc(rT_ready, 1)
                        dve.wait_ge(rT_ready, rT_count[ph["n"]])
                    dve.wait_ge(blocks_done, b + 1)
                    o = UB[u % 4]
                    r = r_all[:, ph["r"], :]
                    if typ in ("q", "k", "pool"):
                        dst = {"q": qT, "k": kT, "pool": pin}[typ][:, 2 * j:2 * j + 2, :]
                        dve.tensor_tensor(dst, pairs(o), both(r), ALU.mult).then_inc(u_free, 1)
                    elif typ == "kdup":
                        for g in range(4):
                            for h in range(2):
                                ins = dve.tensor_tensor(kT[h * HD:(h + 1) * HD, g, :],
                                                        o[(g % 2) * HD:(g % 2 + 1) * HD, (g // 2) * T:(g // 2 + 1) * T],
                                                        r[h * HD:(h + 1) * HD, :], ALU.mult)
                        ins.then_inc(u_free, 1)
                    elif typ == "v":
                        for q in range(QB):
                            ins = dve.tensor_scalar(v[:, q, j * BW:(j + 1) * BW], o[:, q * T:(q + 1) * T], rT[:, q:q + 1],
                                                    None, ALU.mult)
                        ins.then_inc(u_free, 1)
                    elif typ == "proj":
                        xs = x[:, 2 * j:2 * j + 2, :]
                        dve.tensor_tensor(xs, pairs(o), xs, ALU.add).then_inc(x_ready, 1)
                    elif typ == "y":
                        dve.tensor_copy(y[:, 2 * j:2 * j + 2, :], pairs(o)).then_inc(y_ready, 1)

                for i in range(len(ph["blocks"])):
                    b = ph["n"] + i
                    if i == 0 and "ahead" not in ph:
                        split(b + 2)
                    if i < len(ph["blocks"]) - 1:
                        split(b + 3)
                    if ph["stat"] is None:
                        take(i)
                    elif i:
                        if i == 1:
                            invert(ph["stat"], ph["r"])
                            take(0)
                        take(i)
                    if b == 1:
                        setup_rest()
                    if ph["blocks"][0][0] == "pool" and 2 <= i < 7:
                        window_step(i - 2)
                    if "then" in ph:
                        lo_pair(ph["then"], x, i)

            def lo_pair(ph, src, i):
                a = ph["act"]
                for c in (2 * i, 2 * i + 1):
                    dve.wait_ge(act_hi[a], 8 * ph["fill"] + c + 1)
                    dve.scalar_tensor_tensor(out=a_lo[a][:, c, :], in0=src[:, c, :],
                                             scalar=gains[:, c, ph["gain"]:ph["gain"] + 1],
                                             in1=a_hi[a][:, c, :].bitcast(F32), op0=ALU.mult, op1=ALU.subtract)\
                        .then_inc(act_lo[a], 1)

            def prep(ph):
                if ph["src"] == "mem":
                    for i in range(4):
                        dve.wait_ge(s_memT, i + 1)
                        dve.tensor_copy(memT[:, 2 * i:2 * i + 2, :], pairs(DB[i])).then_inc(s_mem_ok, 1)
                    for i in range(4):
                        lo_pair(ph, memT, i)

            def chunk_pairs(ph, finish):
                for i in range(4):
                    finish(i)
                    if i and "then" in ph:
                        lo_pair(ph["then"], x, i - 1)
                if "then" in ph:
                    lo_pair(ph["then"], x, 3)

            def post(ph):
                if "ahead" in ph:
                    split(ph["ahead"])
                invert(ph["stat"], 0)
                r = r_all[:, 0, :]

                def finish(i):
                    for c in (2 * i, 2 * i + 1):
                        g = gains[:, c, ph["gain"]:ph["gain"] + 1]
                        dst = x if ph["src"] == "x" else y
                        ins = dve.scalar_tensor_tensor(out=dst[:, c, :], in0=dst[:, c, :], scalar=g, in1=r, op0=ALU.mult,
                                                       op1=ALU.mult)
                    ins.then_inc(y_scaled if ph["src"] == "y" else x_ready, 1)

                chunk_pairs(ph, finish)

            def ffn(ph):
                def up(s0, s):
                    b = up_block(ph, s0, 0)
                    if s0 == 0 and "ahead" not in ph:
                        split(b + 2)
                    split(b + 3, s)
                    if s0 == 0:
                        invert(ph["stat"], 0)
                    n = cols(ph, s0)

                    def take(c):
                        f, u = ph["f"] + 2 * s0 + c, ph["u"] + 2 * s0 + c
                        if c == 0:
                            dve.wait_ge(half_done, ph["hd"] + s0 + 1 + s)
                        else:
                            dve.wait_ge(blocks_done, b + 2 + 3 * s)
                        if f >= 2:
                            dve.wait_ge(hid_ready, f - 1 + 2 * s)
                        dve.tensor_tensor(us[0:n, c, :, :], pairs(UB[u % 4])[0:n], both(r_all[0:n, 0, :]), ALU.mult)\
                            .then_inc(u_free, 1)

                    def older_taps(c):
                        if ph["conv"] is None:
                            return
                        f = ph["f"] + 2 * s0 + c
                        at = (2 * s0 + c) * 32
                        for tap, done in ((1, conv_t1), (0, conv_t0)):
                            sh = 2 - tap
                            for h in range(2):
                                dve.wait_ge(conv_acc if tap else conv_t1, 2 * f + h + 1 + 4 * s)
                                rw = (ph["conv"] * 3 + tap) * 2 + h
                                dve.scalar_tensor_tensor(
                                    out=acc[0:n, c, h, sh:T], in0=us[0:n, c, h, 0:T - sh],
                                    scalar=cw[0:n, bass.ds(at + rw + 64 * s, 1)], in1=acc[0:n, c, h, sh:T],
                                    op0=ALU.mult, op1=ALU.add).then_inc(done, 1)

                    take(0)
                    older_taps(0)
                    take(1)
                    split(b + 4, s)
                    older_taps(1)
                    for c in range(2):
                        f = ph["f"] + 2 * s0 + c
                        if ph["conv"] is not None:
                            dve.wait_ge(conv_t0, 2 * f + 2 + 4 * s)
                        dve.wait_ge(sil_ready, f + 1 + 2 * s)
                        if f >= 2:
                            dve.wait_ge(hl_ready, f - 1 + 2 * s)
                        val = acc[0:n, c, 1, :] if ph["conv"] is not None else us[0:n, c, 1, :]
                        dve.tensor_tensor(hid[0:n, c, :], sil[0:n, c, :], val, ALU.mult).then_inc(hid_ready, 1)

                def down(s0, s):
                    if s0 < NSTEP - 1:
                        split(down_block(ph, s0) + 3, s)

                ffn_steps(dve, up, down)

                def finish(i):
                    if i < 3:
                        dve.wait_ge(bank_done, 3 * ph["index"] + i + 1)
                    else:
                        dve.wait_ge(blocks_done, ph["n"] + 3 * NSTEP)
                    if ph["dst"] == "x":
                        xs = x[:, 2 * i:2 * i + 2, :]
                        dve.tensor_tensor(xs, pairs(DB[i]), xs, ALU.add).then_inc(x_ready, 1)
                    else:
                        dve.tensor_copy(y[:, 2 * i:2 * i + 2, :], pairs(DB[i])).then_inc(y_ready, 1)

                chunk_pairs(ph, finish)

            def softmax(ph):
                G = ph["heads"] // 2
                a = ph["act"]
                cross, moba = ph.get("cross"), ph.get("moba")
                W = 2 * T if cross else 3 * P
                A = T if cross else P

                def maxima(g):
                    sg = ph["sg"] + g
                    dve.wait_ge(scores_ready, sg + 1)
                    if g >= 4:
                        dve.wait_ge(pt_done, sg - 3)
                    S = PS[:, 2 * (g % 2):2 * (g % 2) + 2, 0:W]
                    p = prob_of(ph, g)
                    if cross:
                        dve.tensor_scalar(p, S, ph["scale"], None, ALU.mult).then_inc(biased, 1)
                    else:
                        tab = bias[:, 2 * g:2 * g + 2, :]
                        dve.scalar_tensor_tensor(out=p[:, :, 0:P], in0=S[:, :, 0:P], scalar=ph["scale"],
                                                 in1=tab[:, :, P:T], op0=ALU.mult, op1=ALU.add)
                        dve.scalar_tensor_tensor(out=p[:, :, P:W], in0=S[:, :, P:W], scalar=ph["scale"],
                                                 in1=tab, op0=ALU.mult, op1=ALU.add).then_inc(biased, 1)
                    dve.wait_ge(biased, sg + 1)
                    small = sm_small[:, g % 2]
                    dve.tensor_reduce(small[:, 0, 0:2], p[:, :, 0:A], AX_X, ALU.max)
                    link(dve.tensor_reduce(small[:, 0, 2:4], p[:, :, A:W], AX_X, ALU.max))
                    if ph.get("sink"):
                        sk = both(sink[:, 2 * g:2 * g + 2])
                        mx = small[:, 0, :].rearrange("p (a b) -> p a b", a=2)
                        link(dve.tensor_tensor(mx, mx, sk, ALU.max))
                        dve.tensor_tensor(small[:, 4, :].rearrange("p (a b) -> p a b", a=2), sk, mx, ALU.subtract)
                    dve.tensor_scalar(small[:, 1, :], small[:, 0, :], -1.0, None, ALU.mult).then_inc(negmax, 1)

                def sums(g):
                    sg = ph["sg"] + g
                    dve.wait_ge(exp_ready, sg + 1)
                    if g >= 2:
                        dve.wait_ge(diag_ready, sg - 1)
                    small = sm_small[:, g % 2]
                    if ph.get("sink"):
                        link(dve.tensor_tensor(small[:, 2, :], small[:, 2, :], small[:, 4, :], ALU.add))
                    if ph.get("diff") is not None:
                        link(dve.reciprocal(small[:, 3, :], small[:, 2, :]))
                        dve.tensor_tensor(small[:, 3, :], small[:, 3, :], lam_fac[:, ph["diff"], :], ALU.mult)\
                            .then_inc(rs_ready, 1)
                    else:
                        dve.reciprocal(small[:, 3, :], small[:, 2, :]).then_inc(rs_ready, 1)

                def out_lo(g):
                    if cross:
                        for i in range(4):
                            c = 4 * g + i
                            dve.wait_ge(act_hi[a], 8 * ph["fill"] + c - c % 2 + 2)
                            dve.tensor_tensor(a_lo[a][:, c, :], UB[2 + i // 2][:, (i % 2) * T:(i % 2 + 1) * T],
                                              a_hi[a][:, c, :].bitcast(F32), ALU.subtract).then_inc(act_lo[a], 1)
                    elif ph.get("diff") is None:
                        dve.wait_ge(act_hi[a], 8 * ph["fill"] + g + 1)
                        dve.tensor_tensor(a_lo[a][:, g, :], UB[2 + g % 2][:, 0:T], a_hi[a][:, g, :].bitcast(F32),
                                          ALU.subtract).then_inc(act_lo[a], 1)

                if ph["sg"] == 0:
                    lambdas()
                if not cross:
                    dve.wait_ge(s_bias_ok, ok_count[ph["sg"]])
                lag = turn_lag(ph)
                for g in range(G + lag + 1):
                    if g < G:
                        maxima(g)
                    if 1 <= g <= G:
                        sums(g - 1)
                    if g > lag:
                        out_lo(g - lag - 1)
                if ph.get("diff") is not None:
                    j = ph["diff"]
                    dve.wait_ge(sub_sd, j + 1)
                    dve.reciprocal(head_rms, head_rms).then_inc(sub_r, 1)

                    def head_lo(i):
                        c = slice(2 * i, 2 * i + 2)
                        dve.wait_ge(act_hi[a], 8 * ph["fill"] + 2 * i + 2)
                        dve.scalar_tensor_tensor(out=a_lo[a][:, c, :], in0=y[:, c, :],
                                                 scalar=1.0 - lambda_init(ph["layer"]),
                                                 in1=a_hi[a][:, c, :].bitcast(F32), op0=ALU.mult, op1=ALU.subtract)\
                            .then_inc(act_lo[a], 2)

                    for i in range(4):
                        c = slice(2 * i, 2 * i + 2)
                        dve.wait_ge(sub_b, 8 * j + 2 * i + 2)
                        dve.wait_ge(y_ready, ph["y"] + 2 * i + 2)
                        dve.scalar_tensor_tensor(out=y[:, c, :], in0=y[:, c, :],
                                                 scalar=gains[:, 0, G_SUBLN + j:G_SUBLN + j + 1], in1=pairs(DB[i]),
                                                 op0=ALU.mult, op1=ALU.mult).then_inc(sub_t, 1)
                        if i:
                            head_lo(i - 1)
                    head_lo(3)
                if moba:
                    for g in range(4):
                        dve.wait_ge(act_hi[a], 8 * ph["fill"] + 4 + 2 * (g // 2) + 2)
                        dve.scalar_tensor_tensor(out=a_lo[a][:, 4 + g, :], in0=DB[g // 2][:, (g % 2) * T:(g % 2 + 1) * T],
                                                 scalar=gains[:, g, G_POOL:G_POOL + 1],
                                                 in1=a_hi[a][:, 4 + g, :].bitcast(F32), op0=ALU.mult, op1=ALU.subtract)\
                            .then_inc(act_lo[a], 1)

            def window_step(i):
                if i == 0:
                    dve.wait_ge(s_bias_ok, ok_count["cnt"])
                    link(dve.reciprocal(inv_cnt, inv_cnt))
                if i < 4:
                    src, dst, sh = (pin if i == 0 else (win_b, win_a)[i % 2]), (win_a, win_b)[i % 2], 1 << i
                    g = slice(i, 4)
                    dve.tensor_copy(dst[:, g, 0:sh], src[:, g, 0:sh])
                    link(dve.tensor_tensor(dst[:, g, sh:T], src[:, g, sh:T], src[:, g, 0:T - sh], ALU.add))
                    return
                for g in range(4):
                    w = (win_a, win_b)[g % 2][:, g, :]
                    link(dve.tensor_tensor(w, w, inv_cnt[:, g, :], ALU.mult))
                    dve.tensor_tensor(w, w, pin[:, g, :], ALU.subtract).then_inc(win_ok, 1)

            def stick(ph):
                a = ph["act"]
                for half in range(2):
                    k0 = ph["kg"] + 4 * half
                    for g in range(4):
                        dve.wait_ge(z_done, k0 + g + 1)
                        if half:
                            dve.wait_ge(spv_done, k0)
                        dve.tensor_scalar(zbuf[:, 2 * g:2 * g + 2, :], PS[:, 2 * (g % 2):2 * (g % 2) + 2, 0:3 * P],
                                          ph["scale"], None, ALU.mult).then_inc(z_copied, 1)
                    for g in range(4):
                        z, t = zbuf[:, 2 * g:2 * g + 2, :], tbuf[:, 2 * g:2 * g + 2, :]
                        dve.wait_ge(t_ln, k0 + g + 1)
                        dve.wait_ge(z_copied, k0 + g + 1)
                        dve.scalar_tensor_tensor(out=t, in0=z, scalar=0.0, in1=t, op0=ALU.max, op1=ALU.add)\
                            .then_inc(sp_sum, 1)
                    for g in range(4):
                        z = zbuf[:, 2 * g:2 * g + 2, :]
                        dve.wait_ge(cs_done, k0 + g + 1)
                        dve.tensor_tensor(z, z, PS[:, 2 * (g % 2):2 * (g % 2) + 2, 0:3 * P], ALU.subtract)\
                            .then_inc(z_less, 1)
                    for g in range(4):
                        c = 4 * half + g
                        dve.wait_ge(act_hi[a], 8 * ph["fill"] + c + 1)
                        dve.tensor_tensor(a_lo[a][:, c, :], UB[g][:, 0:T], a_hi[a][:, c, :].bitcast(F32), ALU.subtract)\
                            .then_inc(act_lo[a], 1)

            def setup_rest():
                dve.wait_ge(s_setup_pe, 6)
                dve.tensor_copy(table_sb, DB[0][0:16, 0:TW]).then_inc(s_tab, 1)
                dve.wait_ge(s_setup_pe, 7)
                dve.tensor_copy(cw[:, :].rearrange("p (a b) -> p a b", a=2), PS[:, 1:3, 0:NSTEP * 32]).then_inc(s_conv, 1)
                rest = PS[:, 1:3, NSTEP * 32:NSTEP * 32 + 4 * NG].rearrange("p a (c g) -> p a c g", c=4)
                dve.tensor_copy(gains[:, :, DEPTH:NG].rearrange("p (a c) g -> p a c g", a=2),
                                rest[:, :, :, DEPTH:NG]).then_inc(s_gain, 1)
                dve.wait_ge(s_misc, 48)
                prod = lam[:, :, 0:4:2, :]
                link(dve.tensor_tensor(prod, lam[:, :, 0:4:2, :], lam[:, :, 1:4:2, :], ALU.mult))
                dve.tensor_reduce(lam_s[:, :].rearrange("p (a b) -> p a b", a=2), prod, AX_X, ALU.add).then_inc(s_lam, 1)

            def lambdas():
                dve.wait_ge(s_gain, 2)
                dve.wait_ge(s_conv, 1)
                dve.wait_ge(s_lam, 2)
                dve.wait_ge(s_const, 4)
                for j, l in enumerate((0, 3)):
                    e = lam_s[:, 2 * j:2 * j + 2]
                    link(dve.tensor_tensor(lam_fac[:, j, 1:2], e[:, 1:2], e[:, 0:1], ALU.subtract))
                    for c in (3, 1):
                        link(dve.tensor_scalar(lam_fac[:, j, c:c + 1], lam_fac[:, j, 1:2], -lambda_init(l), None, ALU.add))

            dve.memset(gain_rows, 0.0).then_inc(s_rows, 1)
            dve.memset(conv_rows[:, F1:], 0.0).then_inc(s_rows, 1)
            dve.memset(eps_t[:, 0:1], EPS)
            dve.memset(eps_t[:, 1:2], EPS * MACARON ** -2)
            dve.wait_ge(s_setup_pe, 1)
            dve.tensor_copy(gains[:, :, 0:DEPTH], UB[0][:, 0:KC * DEPTH].rearrange("p (c g) -> p c g", c=KC))\
                .then_inc(s_gain, 1)
            for i in range(4):
                dve.wait_ge(s_setup_pe, i + 2)
                dve.tensor_copy(x[:, 2 * i:2 * i + 2, :], pairs(DB[i])).then_inc(x_ready, 1)
            dve.wait_ge(s_gain, 1)
            split(0)
            for i in range(4):
                lo_pair(phases[0], x, i)
            split(1)

            for ph in phases:
                {"prep": prep, "post": post, "lin": linear, "ffn": ffn, "soft": softmax, "stick": stick}[ph["kind"]](ph)
            for i in range(4):
                dve.wait_ge(s_outT, 1)
                dve.tensor_copy(x_rows.rearrange("p b d -> p (b d)")[:, i * 512:(i + 1) * 512], DB[i]).then_inc(s_outc, 1)


_INS = ["x", "rel_bias", "attn_norm", "ffn_norm", "w_o", "da_w_qkv", "da_lambda", "da_subln", "sb_w_qkv", "sw_w_qkv",
        "sw_sinks", "ffn_w_up", "ffn_conv_w", "ffn_conv_b", "ffn_w_down", "final_norm", "mem_2", "ffn1_pre_g_2",
        "ffn1_w_gate_2", "ffn1_w_up_2", "ffn1_w_down_2", "ffn1_post_g_2", "mix_pre_g_2", "w_in_2", "pool_w_2",
        "pool_scale_2", "w_out_2", "mix_post_g_2", "xa_pre_g_2", "mem_g_2", "xa_wq_2", "xa_wkv_2", "xa_wo_2",
        "xa_post_g_2", "ffn2_pre_g_2", "ffn2_w_gate_2", "ffn2_w_up_2", "ffn2_w_down_2", "ffn2_post_g_2"]


def bucket_of_distance():
    dist = np.maximum(T - 1 - np.arange(TW), 0)
    half = N_BUCKETS // 2
    large = half + (np.log(np.maximum(dist, 1).astype(np.float32) / half) / math.log(MAX_DIST / half)
                    * (N_BUCKETS - half)).astype(np.int32)
    bucket = np.where(dist < half, dist, np.minimum(large, N_BUCKETS - 1))
    return (np.arange(N_BUCKETS)[:, None] == bucket[None, :]).astype(np.float32)


def kernel(**inputs):
    from concourse import bacc
    from concourse.bass_utils import run_bass_kernel_spmd

    nc = bacc.Bacc("TRN2", target_bir_lowering=False, num_devices=1)
    arrays, io = {}, {}
    for name in _INS + ["bucket_of_distance"]:
        a = bucket_of_distance() if name == "bucket_of_distance" else np.ascontiguousarray(inputs[name])
        arrays[f"in_{name}"] = a
        io[name] = nc.dram_tensor(f"in_{name}", a.shape, mybir.dt.from_np(a.dtype), kind="ExternalInput").ap()
    out = nc.dram_tensor("out_0", (1, T, D), F32, kind="ExternalOutput").ap()
    model_kernel(nc, io, out)
    r = run_bass_kernel_spmd(nc, [arrays], core_ids=[0])
    return r.results[0]["out_0"]
```
